# Optimizing a Trainium2 kernel written in Bass

```python
import jax, jax.numpy as jnp
from jax import lax
import numpy as np

D_MODEL = 1024
BATCH = 1
SEQ = 1024
DEPTH = 2

CTX_LEN = 256
GRID_W = 64
D_BRANCH = D_MODEL // 2
N_EVEN = (DEPTH + 1) // 2
N_ODD = DEPTH // 2
POOL_WINDOWS = (2, 4, 8, 16)
POOL_GROUP = D_BRANCH // len(POOL_WINDOWS)
SHORT_CONV_W = 3
RWKV_HEAD = 64
RWKV_HEADS = D_BRANCH // RWKV_HEAD
D_DECAY_LORA = 32
D_AAA_LORA = 32
D_GATE_LORA = 96
CONF_CONV_W = 31
EVEN_IN = 6 * D_BRANCH
ODD_IN = 8 * D_BRANCH
NORM_EPS = 1e-6
LNX_EPS = 64e-5
CONF_LN_EPS = 1e-5


def rmsnorm(x, g):
    xf = x.astype(jnp.float32)
    y = xf * lax.rsqrt(jnp.mean(xf * xf, axis=-1, keepdims=True) + NORM_EPS)
    return (y * g.astype(jnp.float32)).astype(x.dtype)

def layernorm(x, g, b, eps):
    xf = x.astype(jnp.float32)
    mu = jnp.mean(xf, axis=-1, keepdims=True)
    var = jnp.mean(jnp.square(xf - mu), axis=-1, keepdims=True)
    y = (xf - mu) * lax.rsqrt(var + eps) * g.astype(jnp.float32) + b.astype(jnp.float32)
    return y.astype(x.dtype)

def adaln(cvec, w, b):
    m = jax.nn.silu(cvec) @ w + b
    return jnp.split(m[..., None, :], 3, axis=-1)

def modulate(x, g, shift, scale):
    return rmsnorm(x, g) * (1.0 + scale) + shift

def to_lines(h, layout):
    if layout == "seq":
        return h
    b, t, ch = h.shape
    rows = t // GRID_W
    g = h.reshape(b, rows, GRID_W, ch)
    if layout == "rows":
        return g.reshape(b * rows, GRID_W, ch)
    return g.transpose(0, 2, 1, 3).reshape(b * GRID_W, rows, ch)

def from_lines(y, layout, b):
    if layout == "seq":
        return y
    ch = y.shape[-1]
    if layout == "rows":
        return y.reshape(b, -1, ch)
    rows = y.shape[1]
    return y.reshape(b, GRID_W, rows, ch).transpose(0, 2, 1, 3).reshape(b, rows * GRID_W, ch)

def dwconv(u, w):
    k = w.shape[0]
    return lax.conv_general_dilated(
        u, w[:, None, :].astype(u.dtype), window_strides=(1,), padding=[(k // 2, k // 2)],
        dimension_numbers=("NWC", "WIO", "NWC"), feature_group_count=u.shape[-1])

def centred_mean(u, window):
    l = u.shape[1]
    cs = jnp.pad(jnp.cumsum(u.astype(jnp.float32), axis=1), ((0, 0), (1, 0), (0, 0)))
    t = jnp.arange(l)
    lo = jnp.clip(t - window // 2, 0, l)
    hi = jnp.clip(t - window // 2 + window, 0, l)
    s = jnp.take(cs, hi, axis=1) - jnp.take(cs, lo, axis=1)
    return (s / (hi - lo).astype(jnp.float32)[None, :, None]).astype(u.dtype)

def even_mix(h, w_in, w_out, pool_w, pool_scale, sconv_w, grid):
    b = h.shape[0]
    line = "rows" if grid else "seq"
    u_a, z_a, v_b, g_b, g_c, z_b = jnp.split(h @ w_in, 6, axis=-1)
    ua = to_lines(u_a, line)
    n, l, _ = ua.shape
    ug = ua.reshape(n, l, len(POOL_WINDOWS), POOL_GROUP)
    pooled = jnp.stack([centred_mean(ug[:, :, i], w) for i, w in enumerate(POOL_WINDOWS)], axis=2) - ug
    y_a = jnp.einsum("nlgc,gcd->nlgd", pooled, pool_w).reshape(n, l, D_BRANCH)
    y_a = from_lines(y_a, line, b) * pool_scale
    y_b = g_b * from_lines(dwconv(to_lines(g_c * v_b, line), sconv_w), line, b)
    y = jnp.concatenate([y_a * jax.nn.silu(z_a), y_b * jax.nn.silu(z_b)], axis=-1)
    return y @ w_out

def token_shift_mix(z, mu):
    zp = jnp.pad(z, ((0, 0), (1, 1), (0, 0)))
    nb = 0.5 * (zp[:, :-2] + zp[:, 2:])
    return z + (nb - z) * mu

def wkv_scan(r, w, k, v, a, bb, s0, reverse):
    def step(s, inp):
        r_t, w_t, k_t, v_t, a_t, b_t = inp
        sa = jnp.einsum("bhvk,bhk->bhv", s, a_t)
        s = s * w_t[:, :, None, :] + sa[..., None] * b_t[:, :, None, :] + v_t[..., None] * k_t[:, :, None, :]
        return s, jnp.einsum("bhvk,bhk->bhv", s, r_t)
    xs = tuple(jnp.moveaxis(z.astype(jnp.float32), 1, 0) for z in (r, w, k, v, a, bb))
    s_fin, o = lax.scan(step, s0, xs, reverse=reverse)
    return s_fin, jnp.moveaxis(o, 0, 1)

def rwkv_branch(u, r, k, v, mu, w0, w1, w2, a0, a1, a2, g1, g2, k_k, k_a, r_k, lnx_g, lnx_b, s0):
    b, l, _ = u.shape
    heads = lambda z: z.reshape(b, l, RWKV_HEADS, RWKV_HEAD)
    r = token_shift_mix(r, mu[0])
    k = token_shift_mix(k, mu[1])
    v = token_shift_mix(v, mu[2])
    uw = token_shift_mix(u, mu[3])
    ua = token_shift_mix(u, mu[4])
    ugt = token_shift_mix(u, mu[5])
    g = jax.nn.sigmoid(ugt @ g1) @ g2
    kk = heads(k * k_k).astype(jnp.float32)
    kk = kk / jnp.maximum(jnp.sqrt(jnp.sum(kk * kk, axis=-1, keepdims=True)), 1e-12)
    r_h = heads(r).astype(jnp.float32)
    v_h = heads(v).astype(jnp.float32)
    outs, finals, k_dirs = [], [], []
    for d in range(2):
        logw = -jax.nn.softplus(-(w0[d] + jnp.tanh(uw @ w1[d]) @ w2[d])) - 0.5
        decay = jnp.exp(-jnp.exp(logw.astype(jnp.float32)))
        a = jax.nn.sigmoid(a0[d] + (ua @ a1[d]) @ a2[d])
        k_d = heads(k * (1.0 + (a - 1.0) * k_a)).astype(jnp.float32)
        a_h = heads(a).astype(jnp.float32)
        init = jnp.zeros((b, RWKV_HEADS, RWKV_HEAD, RWKV_HEAD), jnp.float32) if s0 is None else s0[d]
        s_fin, o = wkv_scan(r_h, heads(decay), k_d, v_h, -kk, kk * a_h, init, reverse=(d == 1))
        outs.append(o)
        finals.append(s_fin)
        k_dirs.append(k_d)
    o = outs[0] + outs[1]
    mu_o = jnp.mean(o, axis=-1, keepdims=True)
    var_o = jnp.mean(jnp.square(o - mu_o), axis=-1, keepdims=True)
    o = ((o - mu_o) * lax.rsqrt(var_o + LNX_EPS)).reshape(b, l, D_BRANCH)
    o = o * lnx_g.astype(jnp.float32) + lnx_b.astype(jnp.float32)
    bonus = jnp.sum(r_h * (k_dirs[0] + k_dirs[1]) * r_k.astype(jnp.float32), axis=-1, keepdims=True) * v_h
    y = (o + bonus.reshape(b, l, D_BRANCH)) * g.astype(jnp.float32)
    return y.astype(u.dtype), (finals[0], finals[1])

def conformer_branch(p1, p2, dw_w, dw_b, ln_g, ln_b, line):
    b = p1.shape[0]
    h = p1 * jax.nn.sigmoid(p2)
    h = from_lines(dwconv(to_lines(h, line), dw_w), line, b) + dw_b
    return jax.nn.silu(layernorm(h, ln_g, ln_b, CONF_LN_EPS))

def odd_merge(y_c, z_c, p1, p2, z_d, w_out, dw_w, dw_b, ln_g, ln_b, grid):
    y_d = conformer_branch(p1, p2, dw_w, dw_b, ln_g, ln_b, "cols" if grid else "seq")
    y = jnp.concatenate([y_c * jax.nn.silu(z_c), y_d * jax.nn.silu(z_d)], axis=-1)
    return y @ w_out

def first_inputs(seed: int = 0) -> dict:
    key = jax.random.key(seed)
    ks = iter(jax.random.split(key, 48))
    nrm = lambda shape, s: jax.random.normal(next(ks), shape, jnp.float32) * s
    uni = lambda shape, lo, hi: jax.random.uniform(next(ks), shape, jnp.float32, lo, hi)
    D, DB, ne, no = D_MODEL, D_BRANCH, N_EVEN, N_ODD
    return {
        "x": nrm((BATCH, SEQ, D), 1.0),
        "c": nrm((BATCH, D), 1.0),
        "ctx": nrm((BATCH, CTX_LEN, D), 1.0),
        "c_ctx": nrm((D,), 1.0),
        "ada_w_e": nrm((ne, D, 3 * D), 0.5 * D ** -0.5),
        "ada_b_e": nrm((ne, 3 * D), 0.01),
        "norm_e": 1.0 + nrm((ne, D), 0.02),
        "in_e": nrm((ne, D, EVEN_IN), D ** -0.5),
        "out_e": nrm((ne, 2 * DB, D), (2 * DB) ** -0.5),
        "pool_w": nrm((ne, len(POOL_WINDOWS), POOL_GROUP, POOL_GROUP), POOL_GROUP ** -0.5),
        "pool_scale": 1.0 + nrm((ne, DB), 0.02),
        "sconv_w": nrm((ne, SHORT_CONV_W, DB), SHORT_CONV_W ** -0.5),
        "ada_w_o": nrm((no, D, 3 * D), 0.5 * D ** -0.5),
        "ada_b_o": nrm((no, 3 * D), 0.01),
        "norm_o": 1.0 + nrm((no, D), 0.02),
        "in_o": nrm((no, D, ODD_IN), D ** -0.5),
        "out_o": nrm((no, 2 * DB, D), (2 * DB) ** -0.5),
        "rwkv_mu": uni((no, 6, DB), 0.0, 1.0),
        "w0": uni((no, 2, DB), -6.5, -1.5),
        "w1": nrm((no, 2, DB, D_DECAY_LORA), DB ** -0.5),
        "w2": nrm((no, 2, D_DECAY_LORA, DB), 0.1 * D_DECAY_LORA ** -0.5),
        "a0": nrm((no, 2, DB), 0.1),
        "a1": nrm((no, 2, DB, D_AAA_LORA), DB ** -0.5),
        "a2": nrm((no, 2, D_AAA_LORA, DB), 0.1 * D_AAA_LORA ** -0.5),
        "g1": nrm((no, DB, D_GATE_LORA), DB ** -0.5),
        "g2": nrm((no, D_GATE_LORA, DB), D_GATE_LORA ** -0.5),
        "k_k": 0.85 + nrm((no, DB), 0.05),
        "k_a": 1.0 + nrm((no, DB), 0.05),
        "r_k": nrm((no, RWKV_HEADS, RWKV_HEAD), 0.1),
        "lnx_g": 1.0 + nrm((no, DB), 0.02),
        "lnx_b": nrm((no, DB), 0.01),
        "conf_dw_w": nrm((no, CONF_CONV_W, DB), CONF_CONV_W ** -0.5),
        "conf_dw_b": nrm((no, DB), 0.01),
        "conf_ln_g": 1.0 + nrm((no, DB), 0.02),
        "conf_ln_b": nrm((no, DB), 0.01),
        "final_g": 1.0 + nrm((D,), 0.02),
    }

def first_block(x, c, ctx, c_ctx,
              ada_w_e, ada_b_e, norm_e, in_e, out_e, pool_w, pool_scale, sconv_w,
              ada_w_o, ada_b_o, norm_o, in_o, out_o, rwkv_mu, w0, w1, w2, a0, a1, a2, g1, g2,
              k_k, k_a, r_k, lnx_g, lnx_b, conf_dw_w, conf_dw_b, conf_ln_g, conf_ln_b,
              final_g):
    xc = ctx
    for i in range(DEPTH):
        j = i // 2
        need_ctx = i < DEPTH - 1
        if i % 2 == 0:
            sh, sc, gt = adaln(c, ada_w_e[j], ada_b_e[j])
            h = modulate(x, norm_e[j], sh, sc)
            y = even_mix(h, in_e[j], out_e[j], pool_w[j], pool_scale[j], sconv_w[j], grid=True)
            if need_ctx:
                shc, scc, gtc = adaln(c_ctx, ada_w_e[j], ada_b_e[j])
                hc = modulate(xc, norm_e[j], shc, scc)
                xc = xc + gtc * even_mix(hc, in_e[j], out_e[j], pool_w[j], pool_scale[j], sconv_w[j], grid=False)
            x = x + gt * y
        else:
            rp = (rwkv_mu[j], w0[j], w1[j], w2[j], a0[j], a1[j], a2[j], g1[j], g2[j],
                  k_k[j], k_a[j], r_k[j], lnx_g[j], lnx_b[j])
            cp = (out_o[j], conf_dw_w[j], conf_dw_b[j], conf_ln_g[j], conf_ln_b[j])
            shc, scc, gtc = adaln(c_ctx, ada_w_o[j], ada_b_o[j])
            hc = modulate(xc, norm_o[j], shc, scc)
            uc, rc, kc, vc, zcc, p1c, p2c, zdc = jnp.split(hc @ in_o[j], 8, axis=-1)
            yc_rwkv, ctx_states = rwkv_branch(uc, rc, kc, vc, *rp, None)
            sh, sc, gt = adaln(c, ada_w_o[j], ada_b_o[j])
            h = modulate(x, norm_o[j], sh, sc)
            u, r, k, v, zc, p1, p2, zd = jnp.split(h @ in_o[j], 8, axis=-1)
            y_rwkv, _ = rwkv_branch(u, r, k, v, *rp, ctx_states)
            y = odd_merge(y_rwkv, zc, p1, p2, zd, *cp, grid=True)
            if need_ctx:
                xc = xc + gtc * odd_merge(yc_rwkv, zcc, p1c, p2c, zdc, *cp, grid=False)
            x = x + gt * y
    return rmsnorm(x, final_g)


_first_inputs = first_inputs


def first_inputs(seed=0):
    import zlib

    import numpy as np

    out = dict(_first_inputs(seed))
    spreads = {}
    factors = {'ctx': 34.216,
     'c_ctx': 52.096,
     'ada_b_e': 6.357,
     'norm_e': 7.007,
     'pool_scale': 50.829,
     'ada_b_o': 8.0,
     'norm_o': 8.0,
     'w1': 200.0,
     'w2': 200.0,
     'a0': 8.0,
     'a1': 8.0,
     'a2': 8.0,
     'k_k': 200.0,
     'k_a': 6.528,
     'lnx_g': 200.0,
     'lnx_b': 200.0,
     'conf_dw_b': 200.0,
     'conf_ln_g': 200.0,
     'conf_ln_b': 200.0,
     'final_g': 26.708,
     'w0': 22.986,
     'conf_dw_w': 7.76}
    for name, (base, spread) in spreads.items():
        noise = np.random.default_rng([zlib.crc32(name.encode()), seed]).standard_normal(out[name].shape)
        drawn = base * np.exp(spread * noise) if base else spread * noise
        out[name] = __import__('jax').numpy.asarray(drawn.astype(out[name].dtype))
    for name, factor in factors.items():
        out[name] = (out[name] * factor).astype(out[name].dtype)
    return out


_narrow_inputs = first_inputs


def first_inputs(seed=0):
    out = dict(_narrow_inputs(seed))
    wider = {'lnx_g': 12.0,
     'lnx_b': 12.0,
     'conf_dw_b': 5.17,
     'conf_ln_g': 12.0,
     'conf_ln_b': 12.0,
     'final_g': 3.38}
    for name, times in wider.items():
        mean = out[name].mean()
        out[name] = (mean + times * (out[name] - mean)).astype(out[name].dtype)
    return out


DEPTH_2 = 1

N_ATT_HEADS = 8
ATT_HEAD_DIM = 64
ATT_WIDTH = N_ATT_HEADS * ATT_HEAD_DIM
KV_LATENT = 128
IDX_HEADS = 4
IDX_DIM = 64
TOPK_MAX = 256
Q_BLOCK = 128
N_MLP_GROUPS = 8
MLP_GROUP_DIM = 64
MLP_WIDTH = N_MLP_GROUPS * MLP_GROUP_DIM
CHUNK = 128
MIX_WIDTH = ATT_WIDTH + MLP_WIDTH
D_FF = 2816
DEEPNORM_ALPHA = float((2 * DEPTH_2) ** 0.25)
DEEPNORM_BETA = float((8 * DEPTH_2) ** -0.25)
LN_EPS = 1e-5
IN_COLS = ATT_WIDTH + KV_LATENT + IDX_HEADS * IDX_DIM + IDX_DIM + IDX_HEADS + 2 * MLP_WIDTH
SPLITS = tuple(np.cumsum([ATT_WIDTH, KV_LATENT, IDX_HEADS * IDX_DIM, IDX_DIM, IDX_HEADS]).tolist())


def _layernorm(x, g, b):
    xf = x.astype(jnp.float32)
    mu = jnp.mean(xf, axis=-1, keepdims=True)
    var = jnp.mean(jnp.square(xf - mu), axis=-1, keepdims=True)
    y = (xf - mu) * lax.rsqrt(var + LN_EPS)
    return (y * g.astype(jnp.float32) + b.astype(jnp.float32)).astype(x.dtype)

def _rmsnorm(x, g):
    xf = x.astype(jnp.float32)
    y = xf * lax.rsqrt(jnp.mean(jnp.square(xf), axis=-1, keepdims=True) + LN_EPS)
    return (y * g.astype(jnp.float32)).astype(x.dtype)

def _swiglu(x, w1, w3, w2):
    return (jax.nn.silu(x @ w1) * (x @ w3)) @ w2

def _sparse_attention(q, c, qi, ki, wi, w_uk, w_uv, topk):
    B, L = q.shape[0], q.shape[1]
    q_abs = jnp.einsum('blhd,hcd->blhc', q, w_uk) * (ATT_HEAD_DIM ** -0.5)
    wi_s = wi.astype(jnp.float32) * (IDX_HEADS ** -0.5)
    ki_f = ki.astype(jnp.float32)
    key_pos = jnp.arange(L)

    def block(i):
        start = i * Q_BLOCK
        qa = lax.dynamic_slice_in_dim(q_abs, start, Q_BLOCK, axis=1)
        qib = lax.dynamic_slice_in_dim(qi, start, Q_BLOCK, axis=1)
        wib = lax.dynamic_slice_in_dim(wi_s, start, Q_BLOCK, axis=1)
        t = start + jnp.arange(Q_BLOCK)
        causal = key_pos[None, :] <= t[:, None]
        logit = jnp.einsum('bqhd,bsd->bqhs', qib.astype(jnp.float32), ki_f) * (IDX_DIM ** -0.5)
        score = jnp.einsum('bqh,bqhs->bqs', wib, jax.nn.relu(logit))
        score = jnp.where(causal[None], score, -jnp.inf)
        _, sel = lax.top_k(score, topk)
        c_sel = jax.vmap(lambda cb, ib: cb[ib])(c, sel)
        valid = sel <= t[None, :, None]
        sc = jnp.einsum('bqhc,bqkc->bqhk', qa.astype(jnp.float32), c_sel.astype(jnp.float32))
        sc = jnp.where(valid[:, :, None, :], sc, -jnp.inf)
        p = jax.nn.softmax(sc, axis=-1).astype(c.dtype)
        o_lat = jnp.einsum('bqhk,bqkc->bqhc', p, c_sel)
        return jnp.einsum('bqhc,hcd->bqhd', o_lat, w_uv)

    out = lax.map(block, jnp.arange(L // Q_BLOCK))
    return out.transpose(1, 0, 2, 3, 4).reshape(B, L, ATT_WIDTH)

def _chunked_gmlp(z, gln_g, gln_b, ws, bs):
    B, L = z.shape[0], z.shape[1]
    z = jax.nn.gelu(z)
    u, v = jnp.split(z, 2, axis=-1)
    v = _layernorm(v, gln_g, gln_b)
    v = v.reshape(B, L // CHUNK, CHUNK, N_MLP_GROUPS, MLP_GROUP_DIM)
    tri = jnp.tril(jnp.ones((CHUNK, CHUNK), dtype=bool))
    ws_c = jnp.where(tri[None], ws, jnp.zeros_like(ws))
    sv = jnp.einsum('gts,bnsgd->bntgd', ws_c, v) + bs.T[None, None, :, :, None]
    return u * sv.reshape(B, L, MLP_WIDTH)

def _mixer(h, w_in, kv_norm_g, w_uk, w_uv, gln_g, gln_b, ws, bs, w_out, topk):
    B, L, _ = h.shape
    proj = h @ w_in
    q, c, qi, ki, wi, z = jnp.split(proj, SPLITS, axis=-1)
    q = q.reshape(B, L, N_ATT_HEADS, ATT_HEAD_DIM)
    c = _rmsnorm(c, kv_norm_g)
    qi = qi.reshape(B, L, IDX_HEADS, IDX_DIM)
    att = _sparse_attention(q, c, qi, ki, wi, w_uk, w_uv, topk)
    gm = _chunked_gmlp(z, gln_g, gln_b, ws, bs)
    return jnp.concatenate([att, gm], axis=-1) @ w_out

def second_inputs(seed: int = 0) -> dict:
    key = jax.random.key(seed)
    ks = jax.random.split(key, 24)
    f32 = jnp.float32

    def nrm(k, shape, scale):
        return jax.random.normal(k, shape, f32) * scale

    def gain(k, shape):
        return 1.0 + 0.01 * jax.random.normal(k, shape, f32)

    L_ = DEPTH_2
    return {
        "x": jax.random.normal(ks[0], (BATCH, SEQ, D_MODEL), f32),
        "ffn1_w1": nrm(ks[1], (L_, D_MODEL, D_FF), D_MODEL ** -0.5),
        "ffn1_w3": nrm(ks[2], (L_, D_MODEL, D_FF), D_MODEL ** -0.5),
        "ffn1_w2": nrm(ks[3], (L_, D_FF, D_MODEL), DEEPNORM_BETA * D_FF ** -0.5),
        "ln1_g": gain(ks[4], (L_, D_MODEL)),
        "ln1_b": nrm(ks[5], (L_, D_MODEL), 0.01),
        "w_in": nrm(ks[6], (L_, D_MODEL, IN_COLS), D_MODEL ** -0.5),
        "kv_norm_g": gain(ks[7], (L_, KV_LATENT)),
        "w_uk": nrm(ks[8], (L_, N_ATT_HEADS, KV_LATENT, ATT_HEAD_DIM), KV_LATENT ** -0.5),
        "w_uv": nrm(ks[9], (L_, N_ATT_HEADS, KV_LATENT, ATT_HEAD_DIM), DEEPNORM_BETA * KV_LATENT ** -0.5),
        "gmlp_ln_g": gain(ks[10], (L_, MLP_WIDTH)),
        "gmlp_ln_b": nrm(ks[11], (L_, MLP_WIDTH), 0.01),
        "gmlp_ws": nrm(ks[12], (L_, N_MLP_GROUPS, CHUNK, CHUNK), 0.5 * CHUNK ** -0.5),
        "gmlp_bs": gain(ks[13], (L_, N_MLP_GROUPS, CHUNK)),
        "w_out": nrm(ks[14], (L_, MIX_WIDTH, D_MODEL), DEEPNORM_BETA * MIX_WIDTH ** -0.5),
        "ln2_g": gain(ks[15], (L_, D_MODEL)),
        "ln2_b": nrm(ks[16], (L_, D_MODEL), 0.01),
        "ffn2_w1": nrm(ks[17], (L_, D_MODEL, D_FF), D_MODEL ** -0.5),
        "ffn2_w3": nrm(ks[18], (L_, D_MODEL, D_FF), D_MODEL ** -0.5),
        "ffn2_w2": nrm(ks[19], (L_, D_FF, D_MODEL), DEEPNORM_BETA * D_FF ** -0.5),
        "ln3_g": gain(ks[20], (L_, D_MODEL)),
        "ln3_b": nrm(ks[21], (L_, D_MODEL), 0.01),
    }

def second_block(x, ffn1_w1, ffn1_w3, ffn1_w2, ln1_g, ln1_b, w_in, kv_norm_g, w_uk, w_uv,
              gmlp_ln_g, gmlp_ln_b, gmlp_ws, gmlp_bs, w_out, ln2_g, ln2_b,
              ffn2_w1, ffn2_w3, ffn2_w2, ln3_g, ln3_b):
    L = x.shape[1]
    topk = min(TOPK_MAX, L // 4)
    for l in range(DEPTH_2):
        x = _layernorm(DEEPNORM_ALPHA * x + 0.5 * _swiglu(x, ffn1_w1[l], ffn1_w3[l], ffn1_w2[l]),
                       ln1_g[l], ln1_b[l])
        m = _mixer(x, w_in[l], kv_norm_g[l], w_uk[l], w_uv[l], gmlp_ln_g[l], gmlp_ln_b[l],
                   gmlp_ws[l], gmlp_bs[l], w_out[l], topk)
        x = _layernorm(DEEPNORM_ALPHA * x + m, ln2_g[l], ln2_b[l])
        x = _layernorm(DEEPNORM_ALPHA * x + 0.5 * _swiglu(x, ffn2_w1[l], ffn2_w3[l], ffn2_w2[l]),
                       ln3_g[l], ln3_b[l])
    return x


_first_inputs_2 = second_inputs


def second_inputs(seed=0):
    import zlib

    import numpy as np

    out = dict(_first_inputs_2(seed))
    spreads = {}
    factors = {'ln1_g': 5.562,
     'ln1_b': 5.116,
     'kv_norm_g': 47.356,
     'gmlp_ln_g': 64.0,
     'gmlp_ln_b': 64.0,
     'gmlp_bs': 44.023,
     'ln2_g': 26.398,
     'ln2_b': 25.997,
     'ln3_g': 35.149,
     'ln3_b': 32.42}
    for name, (base, spread) in spreads.items():
        noise = np.random.default_rng([zlib.crc32(name.encode()), seed]).standard_normal(out[name].shape)
        drawn = base * np.exp(spread * noise) if base else spread * noise
        out[name] = __import__('jax').numpy.asarray(drawn.astype(out[name].dtype))
    for name, factor in factors.items():
        out[name] = (out[name] * factor).astype(out[name].dtype)
    return out


_narrow_inputs_2 = second_inputs


def second_inputs(seed=0):

    out = dict(_narrow_inputs_2(seed))
    wider = {'gmlp_ln_g': 9.99,
     'gmlp_ln_b': 10.02,
     'gmlp_bs': 5.24,
     'ln2_g': 4.62,
     'ln2_b': 4.68,
     'ln3_g': 6.66,
     'ln3_b': 6.7}
    for name, times in wider.items():
        mean = out[name].mean()
        out[name] = (mean + times * (out[name] - mean)).astype(out[name].dtype)
    return out


def setup_inputs(seed=0):
    out = dict(first_inputs(seed))
    for name, value in second_inputs(seed + 1).items():
        if name != "x":
            out[name + "_2"] = value
    return out


def reference(
    x, c, ctx, c_ctx, ada_w_e, ada_b_e, norm_e, in_e, out_e, pool_w, pool_scale, sconv_w,
    ada_w_o, ada_b_o, norm_o, in_o, out_o, rwkv_mu, w0, w1, w2, a0, a1, a2, g1, g2, k_k, k_a,
    r_k, lnx_g, lnx_b, conf_dw_w, conf_dw_b, conf_ln_g, conf_ln_b, final_g, ffn1_w1_2,
    ffn1_w3_2, ffn1_w2_2, ln1_g_2, ln1_b_2, w_in_2, kv_norm_g_2, w_uk_2, w_uv_2, gmlp_ln_g_2,
    gmlp_ln_b_2, gmlp_ws_2, gmlp_bs_2, w_out_2, ln2_g_2, ln2_b_2, ffn2_w1_2, ffn2_w3_2,
    ffn2_w2_2, ln3_g_2, ln3_b_2,
):
    x = first_block(
        x, c, ctx, c_ctx, ada_w_e, ada_b_e, norm_e, in_e, out_e, pool_w, pool_scale, sconv_w,
        ada_w_o, ada_b_o, norm_o, in_o, out_o, rwkv_mu, w0, w1, w2, a0, a1, a2, g1, g2, k_k,
        k_a, r_k, lnx_g, lnx_b, conf_dw_w, conf_dw_b, conf_ln_g, conf_ln_b, final_g,
    )
    return second_block(
        x, ffn1_w1_2, ffn1_w3_2, ffn1_w2_2, ln1_g_2, ln1_b_2, w_in_2, kv_norm_g_2, w_uk_2,
        w_uv_2, gmlp_ln_g_2, gmlp_ln_b_2, gmlp_ws_2, gmlp_bs_2, w_out_2, ln2_g_2, ln2_b_2,
        ffn2_w1_2, ffn2_w3_2, ffn2_w2_2, ln3_g_2, ln3_b_2,
    )


_drawn_inputs = setup_inputs


def setup_inputs(seed=0):
    import zlib

    import numpy as np

    out = dict(_drawn_inputs(seed))
    spreads = {}
    factors = {'kv_norm_g_2': 2.745}
    for name, (base, spread) in spreads.items():
        noise = np.random.default_rng([zlib.crc32(name.encode()), seed]).standard_normal(out[name].shape)
        drawn = base * np.exp(spread * noise) if base else spread * noise
        out[name] = __import__('jax').numpy.asarray(drawn.astype(out[name].dtype))
    for name, factor in factors.items():
        out[name] = (out[name] * factor).astype(out[name].dtype)
    return out
```

```python
from contextlib import ExitStack, contextmanager

import concourse.bass as bass
import numpy as np
from concourse import mybir

P = 128
D = 1024
KD = D // P
SEQ = 1024
CTX = 256
T = SEQ + CTX
DB = 512
JB = DB // P
LINE = 64
PAD_T = SEQ + 2 + CTX
CTX_AT = SEQ + 2
D_FF = 2816
KF = D_FF // P
TOPK = 256
ALPHA = float(2 ** 0.25)
EXP_HALF = float(np.exp(-0.5))
NEG = -1.0e30
MAIN_CHUNKS = [(0, 512), (512, 512)]
ALL_CHUNKS = MAIN_CHUNKS + [(SEQ, CTX)]
PAD_CHUNKS = [(0, 512), (512, 512), (1024, PAD_T - 1024)]
POOL_WINDOWS = (2, 4, 8, 16)
N_LEVELS = 7
IN_TILES_2 = 16

VECS = [("c", 8), ("c_ctx", 8), ("ada_b_e", 24), ("ada_b_o", 24), ("norm_e", 8), ("norm_o", 8), ("pool_scale", 4),
        ("sconv_w", 12), ("rwkv_mu", 24), ("w0", 8), ("a0", 8), ("k_k", 4), ("k_a", 4), ("r_k", 4), ("lnx_g", 4),
        ("lnx_b", 4), ("conf_dw_w", 124), ("conf_dw_b", 4), ("conf_ln_g", 4), ("conf_ln_b", 4), ("final_g", 8),
        ("ln1_g_2", 8), ("ln1_b_2", 8), ("kv_norm_g_2", 1), ("gmlp_ln_g_2", 4), ("gmlp_ln_b_2", 4), ("ln2_g_2", 8),
        ("ln2_b_2", 8), ("ln3_g_2", 8), ("ln3_b_2", 8)]
VCOL = {}
NV = 0
for _name, _n in VECS:
    VCOL[_name] = NV
    NV += _n


class Sem:

    def __init__(self, nc, ctx, name):
        self.h = ctx.enter_context(nc.semaphore(name))
        self.base = 0


class Link:

    def __init__(self, eng, sem):
        self.eng, self.sem, self.loop, self.here = eng, sem, 0, 0

    def __call__(self, ins):
        self.here += 1
        ins.then_inc(self.sem.h, 1)
        self.eng.wait_ge(self.sem.h, self.sem.base + self.here + self.loop)

    @contextmanager
    def fori(self, n, per):
        self.sem.base += self.here
        self.here = 0
        with self.eng.Fori(0, n) as i:
            self.loop = i * per
            yield i
            assert self.here == per, (self.here, per)
        self.loop, self.here = 0, 0
        self.sem.base += n * per

    def end(self):
        self.sem.base += self.here
        self.here = 0


def program(nc, A):
    fp32 = mybir.dt.float32
    ALU = mybir.AluOpType
    ACT = mybir.ActivationFunctionType
    root = ExitStack()
    dram = lambda name, shape: nc.dram_tensor(name, shape, fp32)
    proj_e = dram("proj_e", [24, P, T])
    proj_o = dram("proj_o", [32, P, T])
    scan_in = dram("scan_in", [8, JB, P, PAD_T])
    gate_o = dram("gate_o", [JB, P, PAD_T])
    scan_out = dram("scan_out", [2, P, JB, SEQ])
    proj_2 = dram("proj_2", [IN_TILES_2, P, SEQ])
    S_R, S_K, S_V, S_KK, S_LD0, S_A0, S_LD1, S_A1 = range(8)

    with root:
        def sb(ctx, name, shape):
            return ctx.enter_context(nc.sbuf_tensor(name, shape, fp32))

        def sem(name):
            return Sem(nc, root, name)

        PS = root.enter_context(nc.psum_tensor("PS", [P, 8 * 512], fp32))

        def bank(b, n=512, at=0):
            return PS[:, b * 512 + at:b * 512 + at + n]

        xT = sb(root, "xT", [P, KD, T])
        vec = sb(root, "vec", [P, NV])
        ident = sb(root, "ident", [P, P])
        ones = sb(root, "ones", [P, P])
        head_ones = sb(root, "head_ones", [P, P])
        mods = {w: [sb(root, f"mod_{w}{m}", [P, KD, 2]) for m in "sbg"] for w in "eo"}

        def v(name, j=0, n=1):
            return vec[:, VCOL[name] + j:VCOL[name] + j + n]

        dve_step, act_step, pool_step = sem("dve_step"), sem("act_step"), sem("pool_step")
        loaded = sem("loaded")
        w_loaded = [sem(f"w_loaded{s}") for s in range(2)]
        tile_done = [sem(f"tile_done{s}") for s in range(2)]
        evacuated = [sem(f"evacuated{s}") for s in range(2)]
        gated = [sem(f"gated{s}") for s in range(2)]
        stored = [sem(f"stored{s}") for s in range(2)]
        slot_in = [sem(f"slot_in{s}") for s in range(2)]
        slot_free = [sem(f"slot_free{s}") for s in range(2)]

        epsc = sb(root, "epsc", [P, 4])
        EPS = {1e-6: 0, 1e-5: 1, 64e-5: 2, 0.0: 3}
        o_ready = sem("o_ready")
        credited = tile_done + evacuated + gated + stored + slot_free + [o_ready]
        with nc.Block("start") as block:
            @block.gpsimd
            def _(pool):
                for q in credited:
                    pool.sem_inc(q.h, 1)
                    q.base += 1
                for e, i in EPS.items():
                    nc.gpsimd.memset(epsc[:, i:i + 1], e).then_inc(pool_step.h, 1)
        pool_step.base += 4

        with ExitStack() as ctx:
            ring = sb(ctx, "ada_ring", [P, 2, KD, P])
            cs = sb(ctx, "cs", [P, KD, 2])
            mod = sb(ctx, "mod", [P, 48, 2])
            with nc.Block("setup") as block:
                @block.sync
                def _(sp):
                    sp.dma_start(vec[:, :], A["vecs"]).then_inc(loaded.h, 16)
                    sp.dma_start(ident[:, :], A["ident"]).then_inc(loaded.h, 16)
                    sp.dma_start(ones[:, :], A["ones"]).then_inc(loaded.h, 16)
                    sp.dma_start(head_ones[:, :], A["head_ones"]).then_inc(loaded.h, 16)
                    sp.dma_start(xT[:, :, 0:SEQ], A["x"]).then_inc(loaded.h, 16)
                    sp.dma_start(xT[:, :, SEQ:T], A["ctx"]).then_inc(loaded.h, 16)
                    with sp.Fori(0, 24) as i:
                        for s in range(2):
                            sp.wait_ge(tile_done[s].h, tile_done[s].base + i)
                            sp.dma_start(ring[:, s], A["ada"][i * 2 + s]).then_inc(w_loaded[s].h, 16)

                @block.scalar
                def _(act):
                    act.wait_ge(loaded.h, 6 * 16)
                    for n, name in enumerate(("c", "c_ctx")):
                        nc.scalar.activation(cs[:, :, n], v(name, 0, 8), ACT.Silu).then_inc(act_step.h, 1)

                @block.tensor
                def _(pe):
                    pe.wait_ge(act_step.h, 2)
                    with pe.Fori(0, 24) as i:
                        for s in range(2):
                            pe.wait_ge(w_loaded[s].h, i * 16 + 16)
                            for k in range(KD):
                                last = nc.tensor.matmul(PS[:, bass.ds(i * 4 + 2 * s, 2)], ring[:, s, k, :], cs[:, k, :],
                                                        start=k == 0, stop=k == KD - 1)
                            last.then_inc(tile_done[s].h, 1)

                @block.vector
                def _(dve):
                    link = Link(dve, dve_step)
                    dve.wait_ge(tile_done[0].h, tile_done[0].base + 24)
                    dve.wait_ge(tile_done[1].h, tile_done[1].base + 24)
                    bias = vec[:, VCOL["ada_b_e"]:VCOL["ada_b_e"] + 48].unsqueeze(2).to_broadcast([P, 48, 2])
                    link(nc.vector.tensor_tensor(mod[:, :, :], PS[:, 0:96].rearrange("p (n w) -> p n w", w=2), bias,
                                                 ALU.add))
                    for o, w, norm in ((0, "e", "norm_e"), (24, "o", "norm_o")):
                        scale, shift, gate = mods[w]
                        g = v(norm, 0, 8).unsqueeze(2).to_broadcast([P, KD, 2])
                        link(nc.vector.tensor_copy(shift[:, :, :], mod[:, o:o + 8, :]))
                        link(nc.vector.scalar_tensor_tensor(scale[:, :, :], mod[:, o + 8:o + 16, :], 1.0, g, ALU.add,
                                                            ALU.mult))
                        link(nc.vector.tensor_copy(gate[:, :, :], mod[:, o + 16:o + 24, :]))
                    link.end()
            act_step.base += 2
            loaded.base += 96
            for s in range(2):
                w_loaded[s].base += 24 * 16
                tile_done[s].base += 24

        sq_done, sum_done, std_done, norm_done, mean_done, cen_done = [
            sem(n) for n in ("sq_done", "sum_done", "std_done", "norm_done", "mean_done", "cen_done")]

        def norm_stage(name, src, dst, chunks, kt, eps, centre, gain, bias, out_dram=None):
            n = len(chunks)
            inv = 1.0 / (kt * P)
            with ExitStack() as ctx:
                sq = sb(ctx, f"{name}_sq", [P, kt, 512])
                cen = sb(ctx, f"{name}_cen", [P, kt, 512])
                mean = sb(ctx, f"{name}_mean", [P, 512])
                std = sb(ctx, f"{name}_std", [P, 512])
                rstd = sb(ctx, f"{name}_rstd", [P, 512])
                stored_out = stored[0]
                with nc.Block(name) as block:
                    @block.tensor
                    def _(pe):
                        for c, (t, w) in enumerate(chunks):
                            if centre:
                                if c:
                                    pe.wait_ge(mean_done.h, mean_done.base + c)
                                for k in range(kt):
                                    last = nc.tensor.matmul(bank(1, w), ones[:, :], src[:, k, t:t + w], start=k == 0,
                                                            stop=k == kt - 1)
                                last.then_inc(cen_done.h, 1)
                            pe.wait_ge(sq_done.h, sq_done.base + c + 1)
                            if c:
                                pe.wait_ge(std_done.h, std_done.base + c)
                            for k in range(kt):
                                last = nc.tensor.matmul(bank(0, w), ones[:, :], sq[:, k, 0:w], start=k == 0,
                                                        stop=k == kt - 1)
                            last.then_inc(sum_done.h, 1)

                    @block.vector
                    def _(dve):
                        link = Link(dve, dve_step)
                        for c, (t, w) in enumerate(chunks):
                            x = src[:, :, t:t + w]
                            if c:
                                dve.wait_ge(act_step.h, act_step.base + c * kt)
                            if centre:
                                dve.wait_ge(cen_done.h, cen_done.base + c + 1)
                                link(nc.vector.tensor_scalar(mean[:, 0:w], bank(1, w), inv, None, ALU.mult))
                                m = mean[:, 0:w].unsqueeze(1).to_broadcast([P, kt, w])
                                nc.vector.tensor_tensor(cen[:, :, 0:w], x, m, ALU.subtract).then_inc(mean_done.h, 1)
                                dve.wait_ge(mean_done.h, mean_done.base + c + 1)
                                x = cen[:, :, 0:w]
                            dve.wait_ge(std_done.h, std_done.base + c + 1)
                            link(nc.vector.reciprocal(rstd[:, 0:w], std[:, 0:w]))
                            r = rstd[:, 0:w].unsqueeze(1).to_broadcast([P, kt, w])
                            nc.vector.tensor_tensor(cen[:, :, 0:w], x, r, ALU.mult).then_inc(norm_done.h, 1)
                        link.end()

                    @block.scalar
                    def _(act):
                        link = Link(act, act_step)
                        for c, (t, w) in enumerate(chunks):
                            x = src[:, :, t:t + w]
                            if centre:
                                act.wait_ge(mean_done.h, mean_done.base + c + 1)
                                x = cen[:, :, 0:w]
                            nc.scalar.activation(sq[:, :, 0:w], x, ACT.Square).then_inc(sq_done.h, 1)
                            act.wait_ge(sum_done.h, sum_done.base + c + 1)
                            if c:
                                act.wait_ge(norm_done.h, norm_done.base + c)
                            nc.scalar.activation(std[:, 0:w], bank(0, w), ACT.Sqrt, scale=inv, bias=eps_col(eps))\
                                .then_inc(std_done.h, 1)
                            act.wait_ge(norm_done.h, norm_done.base + c + 1)
                            for k in range(kt):
                                link(nc.scalar.activation(dst[:, k, t:t + w], cen[:, k, 0:w], ACT.Identity,
                                                          scale=gain(k, c), bias=bias(k, c)))
                            if out_dram is not None:
                                act.dma_start(out_dram[:, :, t:t + w], dst[:, :, t:t + w])\
                                    .then_inc(stored_out.h, 16)
                        if out_dram is not None:
                            act.wait_ge(stored_out.h, stored_out.base + 16 * n)
                        norm_stage.act_n = link.here
                act_step.base += n * kt
            if centre:
                mean_done.base += n
                cen_done.base += n
            for q in (sq_done, sum_done, std_done, norm_done):
                q.base += n
            if out_dram is not None:
                stored_out.base += 16 * n

        def eps_col(e):
            return epsc[:, EPS[e]:EPS[e] + 1]

        def zero(k=0, c=0):
            return eps_col(0.0)

        def project_stage(name, w_dram, w_at, n_tiles, rhs, chunks, dst):
            width = chunks[-1][0] + chunks[-1][1]
            half = n_tiles // 2
            with ExitStack() as ctx:
                ring = sb(ctx, f"{name}_ring", [P, 2, KD, P])
                stage = sb(ctx, f"{name}_stage", [P, 2, width])
                with nc.Block(name) as block:
                    @block.sync
                    def _(sp):
                        with sp.Fori(0, half) as i:
                            for s in range(2):
                                sp.wait_ge(tile_done[s].h, tile_done[s].base + i)
                                sp.dma_start(ring[:, s], w_dram[i * 2 + (w_at + s)]).then_inc(w_loaded[s].h, 16)

                    @block.tensor
                    def _(pe):
                        with pe.Fori(0, half) as i:
                            for s in range(2):
                                pe.wait_ge(w_loaded[s].h, w_loaded[s].base + i * 16 + 16)
                                pe.wait_ge(evacuated[s].h, evacuated[s].base + i)
                                for t, w in chunks:
                                    for k in range(KD):
                                        last = nc.tensor.matmul(PS[:, s * 1536 + t:s * 1536 + t + w], ring[:, s, k, :],
                                                                rhs[:, k, t:t + w], start=k == 0, stop=k == KD - 1)
                                last.then_inc(tile_done[s].h, 1)

                    @block.vector
                    def _(dve):
                        with dve.Fori(0, half) as i:
                            for s in range(2):
                                dve.wait_ge(tile_done[s].h, tile_done[s].base + i + 1)
                                dve.wait_ge(stored[s].h, stored[s].base + i * 16)
                                nc.vector.tensor_copy(stage[:, s, :], PS[:, s * 1536:s * 1536 + width])\
                                    .then_inc(evacuated[s].h, 1)

                    @block.scalar
                    def _(act):
                        with act.Fori(0, half) as i:
                            for s in range(2):
                                act.wait_ge(evacuated[s].h, evacuated[s].base + i + 1)
                                act.dma_start(dst[i * 2 + (w_at + s)][:, 0:width], stage[:, s, :])\
                                    .then_inc(stored[s].h, 16)
                        for s in range(2):
                            act.wait_ge(stored[s].h, stored[s].base + half * 16)
            for s in range(2):
                w_loaded[s].base += 16 * half
                tile_done[s].base += half
                evacuated[s].base += half
                stored[s].base += 16 * half

        def combine_stage(name, w_dram, kt, rhs, chunks, update):
            with ExitStack() as ctx:
                ring = sb(ctx, f"{name}_ring", [P, 2, kt, P])
                with nc.Block(name) as block:
                    @block.sync
                    def _(sp):
                        with sp.Fori(0, KD // 2) as i:
                            for s in range(2):
                                sp.wait_ge(tile_done[s].h, tile_done[s].base + i)
                                sp.dma_start(ring[:, s], w_dram[i * 2 + s]).then_inc(w_loaded[s].h, 16)

                    @block.tensor
                    def _(pe):
                        with pe.Fori(0, KD // 2) as i:
                            for s in range(2):
                                pe.wait_ge(w_loaded[s].h, w_loaded[s].base + i * 16 + 16)
                                pe.wait_ge(evacuated[s].h, evacuated[s].base + i)
                                for t, w in chunks:
                                    for k in range(kt):
                                        last = nc.tensor.matmul(PS[:, s * 1536 + t:s * 1536 + t + w], ring[:, s, k, :],
                                                                rhs[:, k, t:t + w], start=k == 0, stop=k == kt - 1)
                                last.then_inc(tile_done[s].h, 1)

                    @block.vector
                    def _(dve):
                        with dve.Fori(0, KD // 2) as i:
                            for s in range(2):
                                dve.wait_ge(tile_done[s].h, tile_done[s].base + i + 1)
                                update(i * 2 + s, s * 1536).then_inc(evacuated[s].h, 1)
            for s in range(2):
                w_loaded[s].base += 16 * (KD // 2)
                tile_done[s].base += KD // 2
                evacuated[s].base += KD // 2

        def gated_update(gate, with_ctx):
            def update(n, at):
                last = None
                for col, t, w in ((0, 0, SEQ), (1, SEQ, CTX))[:2 if with_ctx else 1]:
                    x = xT[:, n, t:t + w]
                    last = nc.vector.scalar_tensor_tensor(x, PS[:, at + t:at + t + w],
                                                          gate[:, n, col:col + 1], x, ALU.mult, ALU.add)
                return last
            return update

        def deepnorm_update(n, at):
            x = xT[:, n, 0:SEQ]
            return nc.vector.scalar_tensor_tensor(x, x, ALPHA, PS[:, at:at + SEQ], ALU.mult, ALU.add)


        def even_branch_stage(yT):
            U, ZA, VB, GB, GC, ZB = range(6)
            LW = LINE + 16
            CW = CTX + 16
            PW = (SEQ // LINE) * LW + CW
            QL = LINE + 2
            QW = (SEQ // LINE) * QL + CTX + 2
            with ExitStack() as ctx:
                tin = sb(ctx, "tin", [P, 2, 6, T])
                pad = sb(ctx, "pool_pad", [P, PW])
                win = sb(ctx, "pool_win", [P, 2, PW])
                pooled = sb(ctx, "pooled", [P, T])
                cpad = sb(ctx, "conv_pad", [P, QW])
                conv = sb(ctx, "conv", [P, QW])
                silus = sb(ctx, "silus", [P, 2, T])
                pool_w = sb(ctx, "pool_w", [P, JB, P])
                inv_count = sb(ctx, "inv_count", [P, JB, LINE + CTX])

                def lines(t, at, lw, off, seg_pad):
                    n = SEQ // LINE
                    return (t[:, 0:n * lw].rearrange("p (l w) -> p l w", w=lw)[:, :, at:at + LINE],
                            t[:, n * lw + at:n * lw + at + CTX])

                def flat(t):
                    return t[:, 0:SEQ].rearrange("p (l w) -> p l w", w=LINE), t[:, SEQ:T]

                with nc.Block("even_branch") as block:
                    @block.sync
                    def _(sp):
                        sp.dma_start(pool_w[:, :, :], A["pool_w"]).then_inc(loaded.h, 16)
                        sp.dma_start(inv_count[:, :, :], A["inv_count"]).then_inc(loaded.h, 16)
                        for i in range(JB):
                            s = i % 2
                            if i >= 2:
                                sp.wait_ge(slot_free[s].h, slot_free[s].base + 1)
                            sp.dma_start(tin[:, s], proj_e[i * 6:i * 6 + 6].rearrange("n p t -> p n t"))\
                                .then_inc(slot_in[s].h, 16)

                    @block.tensor
                    def _(pe):
                        pe.wait_ge(loaded.h, loaded.base + 32)
                        for i in range(JB):
                            pe.wait_ge(gated[0].h, gated[0].base + i + 1)
                            if i:
                                pe.wait_ge(evacuated[0].h, evacuated[0].base + i)
                            for t, w in ALL_CHUNKS:
                                last = nc.tensor.matmul(PS[:, t:t + w], pool_w[:, i, :], pooled[:, t:t + w], start=True,
                                                        stop=True)
                            last.then_inc(tile_done[0].h, 1)

                    @block.scalar
                    def _(act):
                        for i in range(JB):
                            s = i % 2
                            act.wait_ge(slot_in[s].h, slot_in[s].base + 16 * (i // 2 + 1))
                            if i:
                                act.wait_ge(slot_free[1 - s].h, slot_free[1 - s].base + (i + 1) // 2)
                            for n, f in enumerate((ZA, ZB)):
                                nc.scalar.activation(silus[:, n, :], tin[:, s, f, :], ACT.Silu)\
                                    .then_inc(std_done.h, 1)

                    @block.vector
                    def _(dve):
                        link = Link(dve, dve_step)
                        link(nc.vector.memset(pad[:, :], 0.0))
                        link(nc.vector.memset(cpad[:, :], 0.0))
                        dve.wait_ge(loaded.h, loaded.base + 32)
                        for i, window in enumerate(POOL_WINDOWS):
                            s = i % 2
                            dve.wait_ge(slot_in[s].h, slot_in[s].base + 16 * (i // 2 + 1))
                            for o, x in zip(lines(pad, 8, LW, 0, 0), flat(tin[:, s, U, :])):
                                link(nc.vector.tensor_copy(o, x))
                            src, n, width = pad, 1, PW
                            while n < window:
                                o = win[:, (n.bit_length() - 1) % 2, :]
                                width -= n
                                link(nc.vector.tensor_tensor(o[:, 0:width], src[:, 0:width], src[:, n:n + width],
                                                             ALU.add))
                                src, n = o, 2 * n
                            if i:
                                dve.wait_ge(tile_done[0].h, tile_done[0].base + i)
                            counts = (inv_count[:, i, 0:LINE].unsqueeze(1).to_broadcast([P, SEQ // LINE, LINE]),
                                      inv_count[:, i, LINE:LINE + CTX])
                            for o, x, q in zip(flat(pooled), lines(src, 8 - window // 2, LW, 0, 0), counts):
                                link(nc.vector.tensor_tensor(o, x, q, ALU.mult))
                            nc.vector.tensor_tensor(pooled[:, :], pooled[:, :], tin[:, s, U, :], ALU.subtract)\
                                .then_inc(gated[0].h, 1)
                            for o, x, y in zip(lines(cpad, 1, QL, 0, 0), flat(tin[:, s, GC, :]), flat(tin[:, s, VB, :])):
                                link(nc.vector.tensor_tensor(o, x, y, ALU.mult))
                            link(nc.vector.tensor_scalar(conv[:, 1:QW - 1], cpad[:, 0:QW - 2], v("sconv_w", i), None,
                                                         ALU.mult))
                            for tap in (1, 2):
                                link(nc.vector.scalar_tensor_tensor(conv[:, 1:QW - 1], cpad[:, tap:QW - 2 + tap],
                                                                    v("sconv_w", 4 * tap + i), conv[:, 1:QW - 1],
                                                                    ALU.mult, ALU.add))
                            for o, x, y in zip(flat(yT[:, JB + i, :]), lines(conv, 1, QL, 0, 0),
                                               flat(tin[:, s, GB, :])):
                                link(nc.vector.tensor_tensor(o, x, y, ALU.mult))
                            dve.wait_ge(std_done.h, std_done.base + 2 * i + 2)
                            link(nc.vector.tensor_tensor(yT[:, JB + i, :], yT[:, JB + i, :], silus[:, 1, :], ALU.mult))
                            dve.wait_ge(tile_done[0].h, tile_done[0].base + i + 1)
                            nc.vector.scalar_tensor_tensor(yT[:, i, :], PS[:, 0:T], v("pool_scale", i), silus[:, 0, :],
                                                           ALU.mult, ALU.mult).then_inc(evacuated[0].h, 1)
                            dve.wait_ge(evacuated[0].h, evacuated[0].base + i + 1)
                            dve.sem_inc(slot_free[s].h, 1)
                        link.end()
            loaded.base += 32
            for s in range(2):
                slot_in[s].base += 32
                slot_free[s].base += 2
            gated[0].base += JB
            evacuated[0].base += JB
            tile_done[0].base += JB
            std_done.base += 2 * JB

        def mix_stage():
            U_AT, K_AT, V_AT, R_AT = 0, 4, 8, 12
            with ExitStack() as ctx:
                um = sb(ctx, "um", [P, 3, JB, PAD_T])
                zin = sb(ctx, "zin", [P, 2, PAD_T + 2])
                nb = sb(ctx, "nb", [P, PAD_T])
                zout = sb(ctx, "zout", [P, 2, PAD_T])
                kkr = sb(ctx, "kkr", [P, PAD_T])
                sq = sb(ctx, "kk_sq", [P, PAD_T])
                nrm = sb(ctx, "kk_norm", [P, PAD_T])
                mu_half = sb(ctx, "mu_half", [P, 24])
                mu_rest = sb(ctx, "mu_rest", [P, 24])
                hid = [sb(ctx, f"hid{n}", [P, PAD_T]) for n in range(3)]
                low1 = [sb(ctx, f"low1_{n}", [P, JB, m]) for n, m in ((0, 64), (1, 64), (2, 96))]
                low2 = [sb(ctx, f"low2_{n}", [m, DB]) for n, m in ((0, 64), (1, 64), (2, 96))]
                tiles = [(U_AT + j, None, (3, 4, 5), j) for j in range(JB)]
                for at, arr, mu in ((R_AT, S_R, 0), (K_AT, S_K, 1), (V_AT, S_V, 2)):
                    tiles += [(at + j, arr, (mu,), j) for j in range(JB)]
                n_z = len(tiles)
                lows = [(n, d, j) for n in (0, 1) for d in range(2) for j in range(JB)] + [(2, 0, j) for j in range(JB)]
                with nc.Block("mix") as block:
                    @block.sync
                    def _(sp):
                        for n in range(3):
                            sp.dma_start(low1[n][:, :, :], A["low1"][n]).then_inc(loaded.h, 16)
                            sp.dma_start(low2[n][:, :], A["low2"][n]).then_inc(loaded.h, 16)
                        sp.wait_ge(pool_step.h, pool_step.base + 1)
                        for q, (at, arr, mus, j) in enumerate(tiles):
                            s = q % 2
                            if q >= 2:
                                sp.wait_ge(slot_free[s].h, slot_free[s].base + q // 2)
                            sp.dma_start(zin[:, s, 1:SEQ + 1], proj_o[at][:, 0:SEQ]).then_inc(slot_in[s].h, 16)
                            if arr == S_R:
                                continue
                            sp.dma_start(zin[:, s, CTX_AT + 1:CTX_AT + CTX + 1], proj_o[at][:, SEQ:T])\
                                .then_inc(slot_in[s].h, 16)

                    @block.gpsimd
                    def _(pool):
                        nc.gpsimd.memset(zin[:, :, :], 0.0).then_inc(pool_step.h, 1)

                    def z_arrived(eng, q):
                        n = [32 if tiles[p][1] != S_R else 16 for p in range(q % 2, q + 1, 2)]
                        eng.wait_ge(slot_in[q % 2].h, slot_in[q % 2].base + sum(n))

                    @block.vector
                    def _(dve):
                        link = Link(dve, dve_step)
                        link(nc.vector.tensor_scalar(mu_half[:, :], v("rwkv_mu", 0, 24), 0.5, None, ALU.mult))
                        link(nc.vector.tensor_scalar(mu_rest[:, :], v("rwkv_mu", 0, 24), -1.0, 1.0, ALU.mult, ALU.add))
                        zq = kq = 0
                        for q, (at, arr, mus, j) in enumerate(tiles):
                            s = q % 2
                            z_arrived(dve, q)
                            link(nc.vector.tensor_tensor(nb[:, :], zin[:, s, 0:PAD_T], zin[:, s, 2:PAD_T + 2], ALU.add))
                            for n, mu in enumerate(mus):
                                col = mu * 4 + j
                                if arr is None:
                                    o = um[:, n, j, :]
                                else:
                                    o = zout[:, zq % 2, :]
                                    if zq >= 2:
                                        dve.wait_ge(stored[zq % 2].h, stored[zq % 2].base + 16 * (zq // 2))
                                link(nc.vector.tensor_scalar(o, zin[:, s, 1:PAD_T + 1], mu_rest[:, col:col + 1], None,
                                                             ALU.mult))
                                nc.vector.scalar_tensor_tensor(o, nb[:, :], mu_half[:, col:col + 1], o, ALU.mult,
                                                               ALU.add).then_inc(norm_done.h, 1)
                            done = norm_done.base + min(q + 1, JB) * 3 + max(q + 1 - JB, 0)
                            dve.wait_ge(norm_done.h, done)
                            dve.sem_inc(slot_free[s].h, 1)
                            if arr is not None:
                                if arr == S_K:
                                    if kq:
                                        dve.wait_ge(gated[1].h, gated[1].base + 16 * kq)
                                    nc.vector.tensor_scalar(kkr[:, :], o, v("k_k", j), None, ALU.mult)\
                                        .then_inc(mean_done.h, 1)
                                    dve.wait_ge(std_done.h, std_done.base + kq + 1)
                                    link(nc.vector.tensor_scalar(nrm[:, :], nrm[:, :], 1e-12, None, ALU.max))
                                    link(nc.vector.reciprocal(nrm[:, :], nrm[:, :]))
                                    nc.vector.tensor_tensor(kkr[:, :], kkr[:, :], nrm[:, :], ALU.mult)\
                                        .then_inc(cen_done.h, 1)
                                    dve.wait_ge(cen_done.h, cen_done.base + kq + 1)
                                    kq += 1
                                zq += 1
                        for m, (n, d, j) in enumerate(lows[:8]):
                            dve.wait_ge(sum_done.h, sum_done.base + m + 1)
                            nc.vector.tensor_scalar(zout[:, m % 2, :], zout[:, m % 2, :], -EXP_HALF, None, ALU.mult)\
                                .then_inc(gated[0].h, 1)
                        link.end()

                    @block.scalar
                    def _(act):
                        for n, f in enumerate((ACT.Tanh, ACT.Copy, ACT.Sigmoid)):
                            m = (64, 64, 96)[n]
                            act.wait_ge(tile_done[0].h, tile_done[0].base + n + 1)
                            nc.scalar.activation(hid[n][0:m, :], PS[0:m, 0:PAD_T], f).then_inc(evacuated[0].h, 1)
                        zq = kq = 0
                        for q, (at, arr, mus, j) in enumerate(tiles[JB:]):
                            act.wait_ge(norm_done.h, norm_done.base + 3 * JB + q + 1)
                            act.dma_start(scan_in[arr, j], zout[:, zq % 2, :]).then_inc(stored[zq % 2].h, 16)
                            zq += 1
                            if arr == S_K:
                                act.wait_ge(mean_done.h, mean_done.base + kq + 1)
                                nc.scalar.activation(sq[:, :], kkr[:, :], ACT.Square).then_inc(sq_done.h, 1)
                                act.wait_ge(tile_done[1].h, tile_done[1].base + kq + 1)
                                nc.scalar.activation(nrm[:, :], PS[:, 1536:1536 + PAD_T], ACT.Sqrt)\
                                    .then_inc(std_done.h, 1)
                                act.wait_ge(cen_done.h, cen_done.base + kq + 1)
                                act.dma_start(scan_in[S_KK, j], kkr[:, :]).then_inc(gated[1].h, 16)
                                kq += 1
                        for m, (n, d, j) in enumerate(lows):
                            s = m % 2
                            act.wait_ge(tile_done[s].h, tile_done[s].base + (3 if s == 0 else 4) + m // 2 + 1)
                            act.wait_ge(stored[s].h, stored[s].base + 16 * (6 + m // 2))
                            o = zout[:, s, :]
                            x = PS[:, s * 1536:s * 1536 + PAD_T]
                            if n == 2:
                                nc.scalar.activation(o, x, ACT.Copy).then_inc(sum_done.h, 1)
                                dst = gate_o[j]
                            else:
                                nc.scalar.activation(o, x, ACT.Sigmoid, bias=v(("w0", "a0")[n], d * 4 + j))\
                                    .then_inc(sum_done.h, 1)
                                dst = scan_in[(S_LD0, S_LD1, S_A0, S_A1)[n * 2 + d], j]
                            act.wait_ge(sum_done.h, sum_done.base + m + 1)
                            if n == 0:
                                act.wait_ge(gated[0].h, gated[0].base + m + 1)
                            act.dma_start(dst, o).then_inc(stored[s].h, 16)
                        for s in range(2):
                            act.wait_ge(stored[s].h, stored[s].base + 16 * 16)
                        act.wait_ge(gated[1].h, gated[1].base + 16 * JB)

                    @block.tensor
                    def _(pe):
                        pe.wait_ge(loaded.h, loaded.base + 96)
                        pe.wait_ge(norm_done.h, norm_done.base + 3 * JB)
                        for n, m in enumerate((64, 64, 96)):
                            if n:
                                pe.wait_ge(evacuated[0].h, evacuated[0].base + n)
                            for t, w in PAD_CHUNKS:
                                for k in range(JB):
                                    last = nc.tensor.matmul(PS[0:m, t:t + w], low1[n][:, k, :], um[:, n, k, t:t + w],
                                                            start=k == 0, stop=k == JB - 1)
                            last.then_inc(tile_done[0].h, 1)
                        for kq in range(JB):
                            pe.wait_ge(sq_done.h, sq_done.base + kq + 1)
                            if kq:
                                pe.wait_ge(std_done.h, std_done.base + kq)
                            for t, w in PAD_CHUNKS:
                                last = nc.tensor.matmul(PS[:, 1536 + t:1536 + t + w], head_ones[:, :], sq[:, t:t + w],
                                                        start=True, stop=True)
                            last.then_inc(tile_done[1].h, 1)
                        pe.wait_ge(evacuated[0].h, evacuated[0].base + 3)
                        pe.wait_ge(std_done.h, std_done.base + JB)
                        for m, (n, d, j) in enumerate(lows):
                            s = m % 2
                            if m >= 2:
                                pe.wait_ge(sum_done.h, sum_done.base + m - 1)
                            lo, hi = (32 * d, 32 * d + 32) if n < 2 else (0, 96)
                            for t, w in PAD_CHUNKS:
                                last = nc.tensor.matmul(PS[:, s * 1536 + t:s * 1536 + t + w],
                                                        low2[n][lo:hi, j * P:j * P + P], hid[n][lo:hi, t:t + w],
                                                        start=True, stop=True)
                            last.then_inc(tile_done[s].h, 1)
            loaded.base += 96
            pool_step.base += 1
            for s in range(2):
                slot_in[s].base += 32 * (JB // 2) + 16 * (JB // 2) + 32 * JB
                slot_free[s].base += n_z // 2
                stored[s].base += 16 * (3 * JB // 2 + len(lows) // 2)
            tile_done[0].base += 3 + len(lows) // 2
            tile_done[1].base += JB + len(lows) // 2
            evacuated[0].base += 3
            norm_done.base += 3 * JB + 3 * JB
            mean_done.base += JB
            std_done.base += JB
            cen_done.base += JB
            sq_done.base += JB
            gated[1].base += 16 * JB
            gated[0].base += 8
            sum_done.base += len(lows)

        def scan_stage():
            N_DMA = 3
            with ExitStack() as ctx:
                tin = sb(ctx, "scan_tin", [P, 2, 12, JB, P])
                AR = sb(ctx, "AR", [P, 2, JB, 2, P])
                Bc = sb(ctx, "Bc", [P, 2, JB, P])
                Kc = sb(ctx, "Kc", [P, 2, JB, P])
                cum = sb(ctx, "cum", [P, 2, JB, P])
                cex = sb(ctx, "cex", [P, 2, JB, P])
                tok = sb(ctx, "tok", [P, 3, 2, JB, P])
                plog = sb(ctx, "plog", [P, 2, 2, JB])
                pexp = sb(ctx, "pexp", [P, 2, 2, JB])
                LM = sb(ctx, "LM", [P, JB, 2, 2, 4, P])
                Lf = sb(ctx, "Lf", [P, JB, 2, 2, P])
                X = sb(ctx, "X", [P, JB, 2, 2, P])
                XT = sb(ctx, "XT", [P, JB, 2, 2, P])
                TT = sb(ctx, "TT", [P, JB, 2, 2, P])
                E1 = TT[:, 0:2].rearrange("p a h d t -> p (a h d t)").rearrange("p (d j t) -> p d j t", d=2, j=JB)
                rhs = TT[:, 0:2].rearrange("p a h d t -> p a (h d t)")
                SA = TT[:, 2:4].rearrange("p a h d t -> p a (h d t)")
                ST = sb(ctx, "ST", [P, 2, JB, 64])
                osb = X[:, :].rearrange("p j h d t -> p (j h d t)")[:, 0:1024].rearrange(
                    "p (d j t) -> p d j t", d=2, j=JB)
                reset = sb(ctx, "reset", [P, JB, P])
                evmask = sb(ctx, "evmask", [P, 2, 4, P])
                invmask = sb(ctx, "invmask", [P, N_LEVELS, 2, P])
                sems = {n: sem(n) for n in ("cum_ready", "exp_ready", "pre_ready", "transposed", "tok_ready", "products",
                                            "masked", "lower_done", "lower_masked", "first_level", "t_done", "t_ready",
                                            "x_done", "x_ready", "rhs_done", "rhs_ready", "sa_done",
                                            "sa_ready", "o_done", "u_done")}
                S = {n: q.h for n, q in sems.items()}
                scan_stored = stored[0]
                kab = v("k_a", 0, 4).unsqueeze(2).to_broadcast([P, JB, P])

                with nc.Block("scan") as block:
                    @block.sync
                    def _(sp):
                        sp.dma_start(reset[:, :, :], A["reset"]).then_inc(loaded.h, 16)
                        sp.dma_start(evmask[:, :, :, :], A["evmask"]).then_inc(loaded.h, 16)
                        sp.dma_start(invmask[:, :, :, :], A["invmask"]).then_inc(loaded.h, 16)
                        flat_in = scan_in[:].rearrange("a j p t -> p (a j) t")

                        def load_turn(s, fwd, bwd):
                            to = tin[:, s].rearrange("p f j t -> p (f j) t")
                            for lo, hi, at, t in ((0, 6, 0, fwd), (6, 10, 0, bwd), (10, 12, 6, bwd)):
                                sp.dma_start(to[:, lo * JB:hi * JB, :],
                                             flat_in[:, at * JB:(at + hi - lo) * JB, bass.ds(t, P)])\
                                    .then_inc(slot_in[s].h, 16)

                        for s in range(2):
                            load_turn(s, CTX_AT + s * P, CTX_AT + (1 - s) * P)
                        with sp.Fori(0, SEQ // P // 2) as i2:
                            for s in range(2):
                                sp.wait_ge(S["transposed"], i2 * 12 + (6 + 6 * s))
                                load_turn(s, i2 * 256 + s * P, i2 * -256 + (SEQ - P - s * P))

                    @block.vector
                    def _(dve):
                        link = Link(dve, dve_step)
                        link(nc.vector.memset(ST[:, :, :, :], 0.0))
                        dve.wait_ge(loaded.h, loaded.base + 48)

                        def body(g, s, k):
                            dve.wait_ge(slot_in[s].h, slot_in[s].base + k * (16 * N_DMA) + 16 * N_DMA)
                            dve.wait_ge(S["u_done"], g)
                            r, kk_, vv, kk, ld, aa = range(6)
                            for d in range(2):
                                f = lambda q: tin[:, s, 6 * d + q]
                                c, ce = cum[:, d], cex[:, d]
                                link(nc.vector.tensor_tensor_scan(
                                    c.rearrange("p j t -> p (j t)"), reset[:, :, :].rearrange("p j t -> p (j t)"),
                                    f(ld).rearrange("p j t -> p (j t)"), 0.0, ALU.mult, ALU.add))
                                if d == 0:
                                    mid, end = c[:, :, 63:64], c[:, :, 127:128]
                                    link(nc.vector.tensor_copy(plog[:, d, 0, :], mid.squeeze(2)))
                                    link(nc.vector.tensor_tensor(c, c, plog[:, d, 0, :].unsqueeze(2).to_broadcast(
                                        [P, JB, P]), ALU.subtract))
                                    link(nc.vector.tensor_copy(plog[:, d, 1, :], end.squeeze(2)))
                                else:
                                    link(nc.vector.tensor_tensor(ce, c, f(ld), ALU.subtract))
                                    link(nc.vector.tensor_copy(plog[:, d, 1, :], ce[:, :, 64:65].squeeze(2)))
                                    link(nc.vector.tensor_tensor(plog[:, d, 0, :], c[:, :, 127:128].squeeze(2),
                                                                 plog[:, d, 1, :], ALU.subtract))
                                    link(nc.vector.tensor_tensor(c, plog[:, d, 1, :].unsqueeze(2).to_broadcast(
                                        [P, JB, P]), ce, ALU.subtract))
                                nc.vector.tensor_tensor(ce, c, f(ld), ALU.subtract).then_inc(S["cum_ready"], 1)
                                link(nc.vector.scalar_tensor_tensor(Kc[:, d], f(aa), -1.0, kab, ALU.add, ALU.mult))
                                link(nc.vector.scalar_tensor_tensor(Kc[:, d], Kc[:, d], 1.0, f(kk_), ALU.add, ALU.mult))
                                link(nc.vector.tensor_tensor(Bc[:, d], f(kk), f(aa), ALU.mult))
                                dve.wait_ge(S["exp_ready"], g * 2 + (d + 1))
                                nc.vector.tensor_tensor(Kc[:, d], Kc[:, d], c, ALU.mult)
                                nc.vector.tensor_tensor(Bc[:, d], Bc[:, d], c, ALU.mult)
                                nc.vector.scalar_tensor_tensor(AR[:, d, :, 0, :], f(kk), -1.0, E1[:, d], ALU.mult, ALU.mult)
                                nc.vector.tensor_tensor(AR[:, d, :, 1, :], f(r), ce, ALU.mult)
                                nc.vector.tensor_tensor(ST[:, d], ST[:, d],
                                                        pexp[:, d, 0, :].unsqueeze(2).to_broadcast([P, JB, 64]),
                                                        ALU.mult).then_inc(S["pre_ready"], 1)
                            for j in range(JB):
                                for h in range(2):
                                    for d in range(2):
                                        u = (j * 2 + h) * 2 + d
                                        dve.wait_ge(S["products"], g * 16 + (u + 1))
                                        nc.vector.tensor_tensor(LM[:, j, h, d].rearrange("p q t -> p (q t)"),
                                                                bank(h * 2 + d),
                                                                evmask[:, d].rearrange("p q t -> p (q t)"), ALU.mult)\
                                            .then_inc(S["masked"], 1)
                                dve.wait_ge(S["lower_done"], g * JB + (j + 1))
                                for h in range(2):
                                    for d in range(2):
                                        last = nc.vector.tensor_tensor(Lf[:, j, h, d], bank(4 + h + 2 * (j % 2), P, d * P),
                                                                       evmask[:, 1 - d, 0], ALU.mult)
                                last.then_inc(S["lower_masked"], 1)
                            for lv in range(1, N_LEVELS):
                                for j in range(JB):
                                    dve.wait_ge(S["t_done"], g * (4 * (N_LEVELS - 1)) + (4 * (lv - 1) + j + 1))
                                    m = invmask[:, lv].unsqueeze(1).to_broadcast([P, 2, 2, P])
                                    nc.vector.tensor_tensor(TT[:, j], bank(j).rearrange("p (h d t) -> p h d t", h=2, d=2),
                                                            m, ALU.mult).then_inc(S["t_ready"], 1)
                            dve.wait_ge(S["sa_done"], g * 2 + 2)
                            nc.vector.tensor_copy(SA, PS[:, 2 * 512:4 * 512].rearrange("p (h c) -> p h c", h=2))\
                                .then_inc(S["sa_ready"], 1)
                            dve.wait_ge(S["u_done"], g + 1)
                            st = ST[:, :, :, :].rearrange("p d j v -> p (d j v)")
                            link(nc.vector.tensor_tensor(st, st, bank(0), ALU.add))
                            st = ST[:, :, :, :]
                            link(nc.vector.tensor_tensor(st, st, pexp[:, :, 1, :].unsqueeze(3).to_broadcast(
                                [P, 2, JB, 64]), ALU.mult))

                        for s in range(2):
                            body(s, s, 0)
                        with link.fori(SEQ // P // 2, 2 * 17) as i2:
                            for s in range(2):
                                body(i2 * 2 + (2 + s), s, i2 + 1)
                        link.end()

                    @block.scalar
                    def _(act):
                        link = Link(act, act_step)

                        def body(g, out):
                            for d in range(2):
                                act.wait_ge(S["cum_ready"], g * 2 + (d + 1))
                                link(nc.scalar.activation(E1[:, d], cex[:, d], ACT.Exp))
                                link(nc.scalar.activation(cex[:, d], cum[:, d], ACT.Exp))
                                nc.scalar.activation(cum[:, d], cum[:, d], ACT.Exp, scale=-1.0)
                                nc.scalar.activation(pexp[:, d], plog[:, d], ACT.Exp).then_inc(S["exp_ready"], 1)
                            for m in range(6):
                                act.wait_ge(S["transposed"], g * 6 + (m + 1))
                                nc.scalar.activation(tok[:, m % 3, m // 3].rearrange("p j t -> p (j t)"), bank(m),
                                                     ACT.Copy).then_inc(S["tok_ready"], 1)
                            for lv in range(1, N_LEVELS):
                                for j in range(JB):
                                    for which, buf in enumerate((X, XT)):
                                        act.wait_ge(S["x_done"], g * (8 * (N_LEVELS - 1)) +
                                                    (8 * (lv - 1) + 2 * j + which + 1))
                                        nc.scalar.activation(buf[:, j].rearrange("p h d t -> p (h d t)"),
                                                             bank(4 + 2 * which + j % 2), ACT.Copy)\
                                            .then_inc(S["x_ready"], 1)
                            act.wait_ge(S["rhs_done"], g + 1)
                            nc.scalar.activation(rhs, PS[:, 0:1024].rearrange("p (h c) -> p h c", h=2), ACT.Copy)\
                                .then_inc(S["rhs_ready"], 1)
                            if out is None:
                                return
                            for h in range(2):
                                for d in range(2):
                                    act.wait_ge(S["o_done"], out * 4 + (h * 2 + d + 1))
                                    hp = slice(h * 64, h * 64 + 64)
                                    nc.scalar.activation(osb[hp, d].rearrange("p j t -> p (j t)"),
                                                         PS[hp, (4 + h * 2 + d) * 512:(5 + h * 2 + d) * 512],
                                                         ACT.Copy).then_inc(o_ready.h, 1)
                            act.wait_ge(o_ready.h, o_ready.base + out * 4 + 4)
                            for d in range(2):
                                t = out * P if d == 0 else out * -P + (SEQ - P)
                                act.dma_start(scan_out[d][:, :, bass.ds(t, P)], osb[:, d]).then_inc(scan_stored.h, 16)
                            act.wait_ge(scan_stored.h, scan_stored.base + out * 32 + 32)

                        for s in range(2):
                            body(s, None)
                        with link.fori(SEQ // P // 2, 2 * 4) as i2:
                            for s in range(2):
                                body(i2 * 2 + (2 + s), i2 * 2 + s)
                        link.end()

                    @block.gpsimd
                    def _(pool):
                        link = Link(pool, pool_step)

                        def body(g):
                            for j in range(JB):
                                pool.wait_ge(S["masked"], g * 16 + (4 * j + 4))
                                pool.wait_ge(S["lower_masked"], g * 4 + (j + 1))
                                idt = ident[:, :].unsqueeze(1).to_broadcast([P, 2, P])
                                for h in range(2):
                                    link(nc.gpsimd.tensor_tensor(LM[:, j, h, :, 0, :], LM[:, j, h, :, 0, :], idt,
                                                                 ALU.add))
                                    link(nc.gpsimd.tensor_tensor(Lf[:, j, h], Lf[:, j, h], idt, ALU.add))
                                for h in range(2):
                                    nc.gpsimd.tensor_tensor(X[:, j, h], Lf[:, j, h], invmask[:, 0], ALU.mult)
                                    for d in range(2):
                                        last = nc.gpsimd.tensor_tensor(XT[:, j, h, d], LM[:, j, h, d, 0],
                                                                       invmask[:, 0, 1 - d], ALU.mult)
                                last.then_inc(S["first_level"], 1)

                        for s in range(2):
                            body(s)
                        with link.fori(SEQ // P // 2, 2 * 16) as i2:
                            for s in range(2):
                                body(i2 * 2 + (2 + s))
                        link.end()

                    @block.tensor
                    def _(pe):
                        def body(g, s, k, out):
                            pe.wait_ge(slot_in[s].h, slot_in[s].base + k * (16 * N_DMA) + 16 * N_DMA)
                            if out is not None:
                                pe.wait_ge(o_ready.h, o_ready.base + out * 4)
                            for d in range(2):
                                pe.wait_ge(S["pre_ready"], g * 2 + (d + 1))
                                for m, src in enumerate((Bc[:, d], Kc[:, d], tin[:, s, 6 * d + 2])):
                                    for j in range(JB):
                                        last = nc.tensor.transpose(bank(d * 3 + m, P, j * P), src[:, j, :], ident[:, :])
                                    last.then_inc(S["transposed"], 1)
                            pe.wait_ge(S["tok_ready"], g * 6 + 6)
                            for j in range(JB):
                                for h in range(2):
                                    hp = slice(h * 64, h * 64 + 64)
                                    for d in range(2):
                                        b = h * 2 + d
                                        if j:
                                            pe.wait_ge(S["masked"], g * 16 + (4 * (j - 1) + b + 1))
                                        ar = AR[hp, d, j].rearrange("p q t -> p (q t)")
                                        nc.tensor.matmul(bank(b, 256), Bc[hp, d, j], ar, start=True, stop=True)
                                        nc.tensor.matmul(bank(b, 256, 256), Kc[hp, d, j], ar, start=True, stop=True)\
                                            .then_inc(S["products"], 1)
                                if j >= 2:
                                    pe.wait_ge(S["lower_masked"], g * 4 + (j - 1))
                                for h in range(2):
                                    hp = slice(h * 64, h * 64 + 64)
                                    for d in range(2):
                                        last = nc.tensor.matmul(bank(4 + h + 2 * (j % 2), P, d * P), AR[hp, d, j, 0],
                                                                Bc[hp, d, j], start=True, stop=True)
                                last.then_inc(S["lower_done"], 1)
                            for lv in range(1, N_LEVELS):
                                for j in range(JB):
                                    if lv == 1:
                                        pe.wait_ge(S["first_level"], g * 4 + (j + 1))
                                        if j == 0:
                                            pe.wait_ge(S["masked"], g * 16 + 16)
                                    else:
                                        pe.wait_ge(S["x_ready"], g * (8 * (N_LEVELS - 1)) + (8 * (lv - 2) + 2 * j + 2))
                                    for h in range(2):
                                        for d in range(2):
                                            last = nc.tensor.matmul(bank(j, P, (h * 2 + d) * P), LM[:, j, h, d, 0],
                                                                    X[:, j, h, d], start=True, stop=True)
                                    last.then_inc(S["t_done"], 1)
                                for j in range(JB):
                                    pe.wait_ge(S["t_ready"], g * (4 * (N_LEVELS - 1)) + (4 * (lv - 1) + j + 1))
                                    if lv == 1 and j == 0:
                                        pe.wait_ge(S["lower_masked"], g * 4 + 4)
                                    done = 8 * (lv - 1) + 2 * j
                                    if done >= 4:
                                        pe.wait_ge(S["x_ready"], g * (8 * (N_LEVELS - 1)) + (done - 2))
                                    for which in range(2):
                                        for h in range(2):
                                            for d in range(2):
                                                a, b = (XT, TT) if which == 0 else (TT, XT)
                                                last = nc.tensor.matmul(
                                                    bank(4 + 2 * which + j % 2, P, (h * 2 + d) * P),
                                                    a[:, j, h, d], b[:, j, h, d], start=True, stop=True)
                                        last.then_inc(S["x_done"], 1)
                            for h in range(2):
                                hp = slice(h * 64, h * 64 + 64)
                                for d in range(2):
                                    for j in range(JB):
                                        o = bank(h, 64, (d * JB + j) * 64)
                                        nc.tensor.matmul(o, AR[hp, d, j, 0], ST[hp, d, j], start=True, stop=False)
                                        last = nc.tensor.matmul(o, LM[:, j, h, d, 2], tok[:, 2, d, j, hp], start=False,
                                                                stop=True)
                            last.then_inc(S["rhs_done"], 1)
                            pe.wait_ge(S["x_ready"], g * (8 * (N_LEVELS - 1)) + 8 * (N_LEVELS - 1))
                            pe.wait_ge(S["rhs_ready"], g + 1)
                            for h in range(2):
                                for d in range(2):
                                    for j in range(JB):
                                        at = (d * JB + j) * 64
                                        last = nc.tensor.matmul(bank(2 + h, 64, at), XT[:, j, h, d],
                                                                rhs[:, h, at:at + 64], start=True, stop=True)
                                last.then_inc(S["sa_done"], 1)
                            pe.wait_ge(S["sa_ready"], g + 1)
                            for h in range(2):
                                hp = slice(h * 64, h * 64 + 64)
                                for d in range(2):
                                    for j in range(JB):
                                        at = (d * JB + j) * 64
                                        if out is None:
                                            continue
                                        o = PS[hp, (4 + h * 2 + d) * 512 + j * P:(4 + h * 2 + d) * 512 + j * P + P]
                                        nc.tensor.matmul(o, SA[:, h, at:at + 64], LM[:, j, h, d, 1], start=True,
                                                         stop=False)
                                        nc.tensor.matmul(o, ST[hp, d, j], AR[hp, d, j, 1], start=False, stop=False)
                                        last = nc.tensor.matmul(o, tok[:, 2, d, j, hp], LM[:, j, h, d, 3],
                                                                start=False, stop=True)
                                    if out is not None:
                                        last.then_inc(S["o_done"], 1)
                            for h in range(2):
                                hp = slice(h * 64, h * 64 + 64)
                                for d in range(2):
                                    for j in range(JB):
                                        at = (d * JB + j) * 64
                                        o = PS[hp, at:at + 64]
                                        nc.tensor.matmul(o, tok[:, 0, d, j, hp], SA[:, h, at:at + 64], start=True,
                                                         stop=False)
                                        last = nc.tensor.matmul(o, tok[:, 1, d, j, hp], tok[:, 2, d, j, hp],
                                                                start=False, stop=True)
                            last.then_inc(S["u_done"], 1)

                        for s in range(2):
                            body(s, s, 0, None)
                        with pe.Fori(0, SEQ // P // 2) as i2:
                            for s in range(2):
                                body(i2 * 2 + (2 + s), s, i2 + 1, i2 * 2 + s)
            loaded.base += 48
            for s in range(2):
                slot_in[s].base += 48 * 5
            stored[0].base += 32 * (SEQ // P)

        def rwkv_out_stage(yT):
            OF, OB, R, K, V, A0, A1, G, Z = range(9)
            ZC_AT = 16
            with ExitStack() as ctx:
                tin = sb(ctx, "ro_tin", [P, 2, 9, SEQ])
                o = sb(ctx, "ro_o", [P, SEQ])
                mean = sb(ctx, "ro_mean", [P, SEQ])
                sq = sb(ctx, "ro_sq", [P, SEQ])
                std = sb(ctx, "ro_std", [P, SEQ])
                bon = sb(ctx, "ro_bon", [P, SEQ])
                sz = sb(ctx, "ro_silu", [P, SEQ])
                with nc.Block("rwkv_out") as block:
                    @block.sync
                    def _(sp):
                        for j in range(JB):
                            s = j % 2
                            if j >= 2:
                                sp.wait_ge(slot_free[s].h, slot_free[s].base + 1)
                            srcs = [scan_out[0][:, j], scan_out[1][:, j]]
                            srcs += [scan_in[a, j][:, 0:SEQ] for a in (S_R, S_K, S_V, S_A0, S_A1)]
                            srcs += [gate_o[j][:, 0:SEQ], proj_o[ZC_AT + j][:, 0:SEQ]]
                            for n, src in enumerate(srcs):
                                sp.dma_start(tin[:, s, n], src).then_inc(slot_in[s].h, 16)

                    @block.tensor
                    def _(pe):
                        def head_sums(b, x):
                            for c in range(2):
                                last = nc.tensor.matmul(bank(b + c), head_ones[:, :], x[:, c * 512:(c + 1) * 512],
                                                        start=True, stop=True)
                            last.then_inc(sum_done.h, 1)

                        for j in range(JB):
                            pe.wait_ge(norm_done.h, norm_done.base + 3 * j + 1)
                            head_sums(0, o)
                            pe.wait_ge(norm_done.h, norm_done.base + 3 * j + 2)
                            head_sums(4, bon)
                            pe.wait_ge(sq_done.h, sq_done.base + j + 1)
                            head_sums(2, sq)

                    @block.vector
                    def _(dve):
                        link = Link(dve, dve_step)
                        for j in range(JB):
                            s = j % 2
                            f = lambda q: tin[:, s, q]
                            dve.wait_ge(slot_in[s].h, slot_in[s].base + 16 * 9 * (j // 2 + 1))
                            nc.vector.tensor_tensor(o[:, :], f(OF), f(OB), ALU.add).then_inc(norm_done.h, 1)
                            link(nc.vector.tensor_tensor(bon[:, :], f(A0), f(A1), ALU.add))
                            link(nc.vector.tensor_scalar(bon[:, :], bon[:, :], -2.0, v("k_a", j), ALU.add, ALU.mult))
                            link(nc.vector.scalar_tensor_tensor(bon[:, :], bon[:, :], 2.0, f(K), ALU.add, ALU.mult))
                            nc.vector.scalar_tensor_tensor(bon[:, :], bon[:, :], v("r_k", j), f(R), ALU.mult,
                                                           ALU.mult).then_inc(norm_done.h, 1)
                            dve.wait_ge(sum_done.h, sum_done.base + 3 * j + 1)
                            link(nc.vector.tensor_scalar(mean[:, :], PS[:, 0:SEQ], 1.0 / 64, None, ALU.mult))
                            nc.vector.tensor_tensor(o[:, :], o[:, :], mean[:, :], ALU.subtract)\
                                .then_inc(norm_done.h, 1)
                            dve.wait_ge(std_done.h, std_done.base + 2 * j + 2)
                            link(nc.vector.reciprocal(std[:, :], std[:, :]))
                            link(nc.vector.tensor_tensor(o[:, :], o[:, :], std[:, :], ALU.mult))
                            link(nc.vector.tensor_scalar(o[:, :], o[:, :], v("lnx_g", j), v("lnx_b", j), ALU.mult,
                                                         ALU.add))
                            link(nc.vector.tensor_tensor(bon[:, :], PS[:, 4 * 512:6 * 512], f(V), ALU.mult))
                            link(nc.vector.tensor_tensor(o[:, :], o[:, :], bon[:, :], ALU.add))
                            link(nc.vector.tensor_tensor(o[:, :], o[:, :], f(G), ALU.mult))
                            nc.vector.tensor_tensor(yT[:, j, 0:SEQ], o[:, :], sz[:, :], ALU.mult)\
                                .then_inc(evacuated[0].h, 1)
                            dve.wait_ge(evacuated[0].h, evacuated[0].base + j + 1)
                            dve.sem_inc(slot_free[s].h, 1)
                        link.end()

                    @block.scalar
                    def _(act):
                        for j in range(JB):
                            s = j % 2
                            act.wait_ge(slot_in[s].h, slot_in[s].base + 16 * 9 * (j // 2 + 1))
                            if j:
                                act.wait_ge(evacuated[0].h, evacuated[0].base + j)
                            nc.scalar.activation(sz[:, :], tin[:, s, Z], ACT.Silu).then_inc(std_done.h, 1)
                            act.wait_ge(norm_done.h, norm_done.base + 3 * j + 3)
                            nc.scalar.activation(sq[:, :], o[:, :], ACT.Square).then_inc(sq_done.h, 1)
                            act.wait_ge(sum_done.h, sum_done.base + 3 * j + 3)
                            nc.scalar.activation(std[:, :], PS[:, 1024:2048], ACT.Sqrt, scale=1.0 / 64,
                                                 bias=eps_col(64e-5)).then_inc(std_done.h, 1)
            for s in range(2):
                slot_in[s].base += 16 * 9 * 2
                slot_free[s].base += 2
            norm_done.base += 3 * JB
            sum_done.base += 3 * JB
            std_done.base += 2 * JB
            sq_done.base += JB
            evacuated[0].base += JB

        def conformer_conv_stage(cv):
            P1_AT, P2_AT = 20, 24
            HALF = 15
            with ExitStack() as ctx:
                tin = sb(ctx, "cf_tin", [P, 2, 2, SEQ])
                hg = sb(ctx, "cf_h", [P, 2, SEQ])
                with nc.Block("conformer_conv") as block:
                    @block.sync
                    def _(sp):
                        for j in range(JB):
                            s = j % 2
                            if j >= 2:
                                sp.wait_ge(gated[0].h, gated[0].base + j - 1)
                            for n, at in enumerate((P1_AT, P2_AT)):
                                sp.dma_start(tin[:, s, n], proj_o[at + j][:, 0:SEQ]).then_inc(slot_in[s].h, 16)

                    @block.scalar
                    def _(act):
                        for j in range(JB):
                            s = j % 2
                            act.wait_ge(slot_in[s].h, slot_in[s].base + 32 * (j // 2 + 1))
                            nc.scalar.activation(tin[:, s, 1], tin[:, s, 1], ACT.Sigmoid).then_inc(sq_done.h, 1)

                    @block.vector
                    def _(dve):
                        link = Link(dve, dve_step)
                        for j in range(JB):
                            s = j % 2
                            dve.wait_ge(slot_in[s].h, slot_in[s].base + 32 * (j // 2 + 1))
                            dve.wait_ge(sq_done.h, sq_done.base + j + 1)
                            h = hg[:, s]
                            nc.vector.tensor_tensor(h, tin[:, s, 0], tin[:, s, 1], ALU.mult).then_inc(gated[0].h, 1)
                            dve.wait_ge(gated[0].h, gated[0].base + j + 1)
                            link(nc.vector.tensor_scalar(cv[:, j, :], h, v("conf_dw_w", 4 * HALF + j), v("conf_dw_b", j),
                                                         ALU.mult, ALU.add))
                            for tap in range(2 * HALF + 1):
                                d = (tap - HALF) * LINE
                                if d == 0:
                                    continue
                                w = SEQ - abs(d)
                                o = cv[:, j, max(0, -d):max(0, -d) + w]
                                link(nc.vector.scalar_tensor_tensor(o, h[:, max(0, d):max(0, d) + w],
                                                                    v("conf_dw_w", 4 * tap + j), o, ALU.mult, ALU.add))
                        link.end()
            for s in range(2):
                slot_in[s].base += 32 * 2
            gated[0].base += JB
            sq_done.base += JB

        def conformer_gate_stage(cv, yT):
            ZD_AT = 28
            with ExitStack() as ctx:
                zd = sb(ctx, "zd", [P, JB, SEQ])
                with nc.Block("conformer_gate") as block:
                    @block.sync
                    def _(sp):
                        sp.dma_start(zd[:, :, :], proj_o[ZD_AT:ZD_AT + JB].rearrange("j p t -> p j t")[:, :, 0:SEQ])\
                            .then_inc(loaded.h, 16)

                    @block.scalar
                    def _(act):
                        nc.scalar.activation(cv[:, :, :], cv[:, :, :], ACT.Silu).then_inc(act_step.h, 1)
                        act.wait_ge(loaded.h, loaded.base + 16)
                        nc.scalar.activation(zd[:, :, :], zd[:, :, :], ACT.Silu).then_inc(act_step.h, 1)

                    @block.vector
                    def _(dve):
                        dve.wait_ge(act_step.h, act_step.base + 2)
                        nc.vector.tensor_tensor(yT[:, JB:2 * JB, 0:SEQ], cv[:, :, :], zd[:, :, :], ALU.mult)\
                            .then_inc(dve_step.h, 1)
            act_step.base += 2
            dve_step.base += 1
            loaded.base += 16

        def ffn_stage(name, w_up, w_down):
            with ExitStack() as ctx:
                hid = sb(ctx, f"{name}_hid", [P, KF, SEQ])
                with ExitStack() as up:
                    ring = sb(up, f"{name}_ring", [P, 2, 2, KD, P])
                    sg = sb(up, f"{name}_silu", [P, 2, SEQ])
                    with nc.Block(f"{name}_up") as block:
                        @block.sync
                        def _(sp):
                            with sp.Fori(0, KF // 2) as i:
                                for s in range(2):
                                    sp.wait_ge(tile_done[s].h, tile_done[s].base + i)
                                    sp.dma_start(ring[:, s], w_up[i * 2 + s]).then_inc(w_loaded[s].h, 16)

                        @block.tensor
                        def _(pe):
                            with pe.Fori(0, KF // 2) as i:
                                for s in range(2):
                                    pe.wait_ge(w_loaded[s].h, w_loaded[s].base + i * 16 + 16)
                                    pe.wait_ge(evacuated[s].h, evacuated[s].base + i)
                                    for m in range(2):
                                        for t, w in MAIN_CHUNKS:
                                            for k in range(KD):
                                                at = s * 2048 + m * 1024 + t
                                                last = nc.tensor.matmul(PS[:, at:at + w], ring[:, s, m, k, :],
                                                                        xT[:, k, t:t + w], start=k == 0,
                                                                        stop=k == KD - 1)
                                    last.then_inc(tile_done[s].h, 1)

                        @block.scalar
                        def _(act):
                            with act.Fori(0, KF // 2) as i:
                                for s in range(2):
                                    act.wait_ge(tile_done[s].h, tile_done[s].base + i + 1)
                                    act.wait_ge(evacuated[s].h, evacuated[s].base + i)
                                    nc.scalar.activation(sg[:, s], PS[:, s * 2048:s * 2048 + SEQ], ACT.Silu)\
                                        .then_inc(gated[s].h, 1)

                        @block.vector
                        def _(dve):
                            with dve.Fori(0, KF // 2) as i:
                                for s in range(2):
                                    dve.wait_ge(gated[s].h, gated[s].base + i + 1)
                                    nc.vector.scalar_tensor_tensor(hid[:, i * 2 + s, :], sg[:, s], 0.5,
                                                                   PS[:, s * 2048 + 1024:s * 2048 + 2048], ALU.mult,
                                                                   ALU.mult).then_inc(evacuated[s].h, 1)
                for s in range(2):
                    w_loaded[s].base += 16 * (KF // 2)
                    for q in (tile_done, evacuated, gated):
                        q[s].base += KF // 2
                combine_stage(f"{name}_down", w_down, KF, hid, MAIN_CHUNKS, deepnorm_update)

        def gmlp_stage(mT):
            with ExitStack() as ctx:
                z = sb(ctx, "gz", [P, 8, SEQ])
                ws = sb(ctx, "gws", [P, 8, P])
                bs = sb(ctx, "gbs", [1, 8, P])
                tri = sb(ctx, "tri", [P, P])
                vt = sb(ctx, "vt", [P, 2, DB])
                with nc.Block("gmlp_gelu") as block:
                    @block.sync
                    def _(sp):
                        sp.dma_start(z[:, :, :], proj_2[8:16].rearrange("n p t -> p n t")).then_inc(loaded.h, 16)
                        sp.dma_start(ws[:, :, :], A["gmlp_ws"]).then_inc(loaded.h, 16)
                        sp.dma_start(bs[:, :, :], A["gmlp_bs"]).then_inc(loaded.h, 16)
                        sp.dma_start(tri[:, :], A["tri"]).then_inc(loaded.h, 16)

                    @block.scalar
                    def _(act):
                        act.wait_ge(loaded.h, loaded.base + 64)
                        nc.scalar.activation(z[:, :, :].rearrange("p n t -> p (n t)"),
                                             z[:, :, :].rearrange("p n t -> p (n t)"), ACT.Gelu_apprx_tanh)\
                            .then_inc(act_step.h, 1)

                    @block.vector
                    def _(dve):
                        dve.wait_ge(loaded.h, loaded.base + 64)
                        nc.vector.tensor_tensor(ws[:, :, :], ws[:, :, :], tri[:, :].unsqueeze(1).to_broadcast([P, 8, P]),
                                                ALU.mult).then_inc(dve_step.h, 1)
                act_step.base += 1
                dve_step.base += 1
                loaded.base += 64
                zv = z[:, 4:8, :]
                norm_stage("gmlp_ln", zv, zv, MAIN_CHUNKS, 4, 1e-5, True, lambda k, c: v("gmlp_ln_g_2", k),
                           lambda k, c: v("gmlp_ln_b_2", k))
                with nc.Block("gmlp_mix") as block:
                    @block.tensor
                    def _(pe):
                        for n in range(SEQ // P):
                            s = n % 2
                            if n >= 2:
                                pe.wait_ge(act_step.h, act_step.base + n - 1)
                            for k in range(4):
                                last = nc.tensor.transpose(bank(s, P, k * P), z[:, 4 + k, n * P:n * P + P], ident[:, :])
                            last.then_inc(tile_done[0].h, 1)
                            pe.wait_ge(act_step.h, act_step.base + n + 1)
                            if n >= 2:
                                pe.wait_ge(dve_step.h, dve_step.base + n - 1)
                            for g in range(8):
                                hp = slice((g % 2) * 64, (g % 2) * 64 + 64)
                                o = PS[hp, (2 + s) * 512 + (g // 2) * P:(2 + s) * 512 + (g // 2) * P + P]
                                nc.tensor.matmul(o, vt[:, s, g * 64:g * 64 + 64], ws[:, g, :], start=True, stop=False)
                                last = nc.tensor.matmul(o, ones[0:1, 0:64], bs[:, g, :], start=False, stop=True)
                            last.then_inc(tile_done[1].h, 1)

                    @block.scalar
                    def _(act):
                        for n in range(SEQ // P):
                            s = n % 2
                            act.wait_ge(tile_done[0].h, tile_done[0].base + n + 1)
                            if n >= 2:
                                act.wait_ge(tile_done[1].h, tile_done[1].base + n - 1)
                            nc.scalar.activation(vt[:, s, :], bank(s), ACT.Copy).then_inc(act_step.h, 1)

                    @block.vector
                    def _(dve):
                        for n in range(SEQ // P):
                            s = n % 2
                            dve.wait_ge(tile_done[1].h, tile_done[1].base + n + 1)
                            nc.vector.tensor_tensor(mT[:, 4:8, n * P:n * P + P], z[:, 0:4, n * P:n * P + P],
                                                    bank(2 + s).rearrange("p (k t) -> p k t", k=4), ALU.mult)\
                                .then_inc(dve_step.h, 1)
            for q in (act_step, dve_step, tile_done[0], tile_done[1]):
                q.base += SEQ // P

        def attention_stage(mT):
            NQ = SEQ // P
            NH = 8
            with ExitStack() as ctx:
                qT = sb(ctx, "qT", [P, 4, SEQ])
                cT = sb(ctx, "cT", [P, 1, SEQ])
                qi = sb(ctx, "qi", [P, 2, SEQ])
                ki = sb(ctx, "ki", [P, SEQ])
                wi = sb(ctx, "wi", [4, SEQ])
                uk = sb(ctx, "uk", [P, 4, P])
                uv = sb(ctx, "uv", [P, NH, 64])
                neg = sb(ctx, "neg", [P, P])
                one_row = sb(ctx, "one_row", [P, SEQ])
                with nc.Block("att_load") as block:
                    @block.sync
                    def _(sp):
                        sp.dma_start(qT[:, :, :], proj_2[0:4].rearrange("n p t -> p n t")).then_inc(loaded.h, 16)
                        sp.dma_start(cT[:, 0, :], proj_2[4]).then_inc(loaded.h, 16)
                        sp.dma_start(qi[:, :, :], proj_2[5:7].rearrange("n p t -> p n t")).then_inc(loaded.h, 16)
                        for h in range(2):
                            sp.dma_start(ki[h * 64:h * 64 + 64, :], proj_2[7][0:64, :]).then_inc(loaded.h, 16)
                        sp.dma_start(wi[:, :], proj_2[7][64:68, :]).then_inc(loaded.h, 16)
                        sp.dma_start(uk[:, :, :], A["w_uk"]).then_inc(loaded.h, 16)
                        sp.dma_start(uv[:, :, :], A["w_uv"]).then_inc(loaded.h, 16)
                        sp.dma_start(neg[:, :], A["neg"]).then_inc(loaded.h, 16)
                        sp.wait_ge(loaded.h, loaded.base + 16 * 9)

                    @block.vector
                    def _(dve):
                        nc.vector.memset(one_row[:, :], 1.0).then_inc(dve_step.h, 1)
                loaded.base += 16 * 9
                dve_step.base += 1
                norm_stage("kv_norm", cT, cT, MAIN_CHUNKS, 1, 1e-5, False, lambda k, c: v("kv_norm_g_2"), zero)
                qabs = sb(ctx, "qabs", [P, NH, SEQ])
                ctok = sb(ctx, "ctok", [P, NQ, P])
                wis = sb(ctx, "wis", [P, NQ, 4])
                with nc.Block("att_prepare") as block:
                    @block.tensor
                    def _(pe):
                        for h in range(NH):
                            s = h % 2
                            hp = slice(s * 64, s * 64 + 64)
                            if h >= 2:
                                pe.wait_ge(act_step.h, act_step.base + h - 1)
                            for c in range(2):
                                last = nc.tensor.matmul(bank(2 * s + c), uk[hp, h // 2, :],
                                                        qT[hp, h // 2, c * 512:c * 512 + 512], start=True, stop=True)
                            last.then_inc(tile_done[0].h, 1)
                        for n in range(NQ):
                            nc.tensor.transpose(bank(4 + n // 4, P, (n % 4) * P), cT[:, 0, n * P:n * P + P],
                                                ident[:, :])
                        for n in range(NQ):
                            last = nc.tensor.transpose(bank(6, 4, n * 4), wi[0:4, n * P:n * P + P], ident[0:4, 0:4])
                        last.then_inc(tile_done[1].h, 1)

                    @block.scalar
                    def _(act):
                        for h in range(NH):
                            act.wait_ge(tile_done[0].h, tile_done[0].base + h + 1)
                            s = h % 2
                            nc.scalar.activation(qabs[:, h, :], PS[:, s * 1024:s * 1024 + 1024], ACT.Copy, scale=0.125)\
                                .then_inc(act_step.h, 1)

                    @block.vector
                    def _(dve):
                        dve.wait_ge(tile_done[1].h, tile_done[1].base + 1)
                        nc.vector.tensor_copy(ctok[:, :, :].rearrange("p n c -> p (n c)"), PS[:, 2048:3072])
                        nc.vector.tensor_scalar(wis[:, :, :].rearrange("p n h -> p (n h)"), bank(6, 32), 0.5, None,
                                                ALU.mult).then_inc(dve_step.h, 1)
                act_step.base += NH
                dve_step.base += 1
                tile_done[0].base += NH
                tile_done[1].base += 1

                names = ("a_scored", "a_relu", "a_summed", "a_bias", "a_added", "a_exp", "a_prob", "a_transposed",
                         "a_turned", "a_latent", "a_latcopy", "a_value", "a_stored")
                S = {n: sem(n).h for n in names}
                rl = sb(ctx, "rl", [P, 2, SEQ])
                score = sb(ctx, "score", [P, SEQ])
                work = sb(ctx, "work", [P, SEQ])
                best = sb(ctx, "best", [P, 8])
                eq = sb(ctx, "eq", [P, SEQ])
                bias = sb(ctx, "bias", [P, SEQ])
                count = sb(ctx, "count", [P, 2])
                sm = sb(ctx, "sm", [P, 2, SEQ])
                pr = sb(ctx, "pr", [P, 2, SEQ])
                pT = sb(ctx, "pT", [P, 2, NQ, P])
                mx = sb(ctx, "mx", [P, 2])
                nmx = sb(ctx, "nmx", [P, 2])
                rs = sb(ctx, "rs", [P, 2])
                ri = sb(ctx, "ri", [P, 2])
                lat = sb(ctx, "lat", [P, 4, P])
                with nc.Block("attention") as block:
                    def pieces(width):
                        return [(c, min(512, width - c)) for c in range(0, width, 512)]

                    @block.tensor
                    def _(pe):
                        def score_banks_free(n):
                            if n < 2:
                                return
                            b, u = divmod(n - 2, 12)
                            if u < 4:
                                pe.wait_ge(S["a_relu"], 4 * b + u + 1)
                            else:
                                pe.wait_ge(S["a_added"], 8 * b + u - 4 + 1)

                        for b in range(NQ):
                            width = (b + 1) * P
                            q = slice(b * P, b * P + P)
                            for h in range(4):
                                hp = slice((h % 2) * 64, (h % 2) * 64 + 64)
                                score_banks_free(12 * b + h)
                                for c, w in pieces(width):
                                    last = nc.tensor.matmul(PS[:, (h % 2) * 1024 + c:(h % 2) * 1024 + c + w],
                                                            qi[hp, h // 2, q], ki[hp, c:c + w], start=True, stop=True)
                                last.then_inc(S["a_scored"], 1)

                            def scores(h):
                                score_banks_free(12 * b + 4 + h)
                                for c, w in pieces(width):
                                    last = nc.tensor.matmul(PS[:, (h % 2) * 1024 + c:(h % 2) * 1024 + c + w],
                                                            qabs[:, h, q], cT[:, 0, c:c + w], start=True, stop=True)
                                last.then_inc(S["a_scored"], 1)

                            scores(0)
                            for h in range(NH):
                                if h + 1 < NH:
                                    scores(h + 1)
                                n = NH * b + h
                                pe.wait_ge(S["a_prob"], n + 1)
                                if n:
                                    pe.wait_ge(S["a_turned"], n)
                                for k in range(b + 1):
                                    last = nc.tensor.transpose(PS[:, 2048 + k * P:2048 + k * P + P],
                                                               pr[:, h % 2, k * P:k * P + P], ident[:, :])
                                last.then_inc(S["a_transposed"], 1)
                                pe.wait_ge(S["a_turned"], n + 1)
                                if h % 4 == 0 and n:
                                    pe.wait_ge(S["a_latcopy"], n // 4)
                                for k in range(b + 1):
                                    last = nc.tensor.matmul(bank(6, P, (h % 4) * P), ctok[:, k, :], pT[:, h % 2, k, :],
                                                            start=k == 0, stop=k == b)
                                if h % 4 == 3:
                                    last.then_inc(S["a_latent"], 1)
                                    pe.wait_ge(S["a_latcopy"], 2 * b + h // 4 + 1)
                                    if h == 3 and b:
                                        pe.wait_ge(S["a_stored"], b)
                                    for g in range(h - 3, h + 1):
                                        hp = slice((g % 2) * 64, (g % 2) * 64 + 64)
                                        last = nc.tensor.matmul(PS[hp, 7 * 512 + (g // 2) * P:7 * 512 + (g // 2) * P + P],
                                                                uv[:, g, :], lat[:, g % 4, :], start=True, stop=True)
                                    last.then_inc(S["a_value"], 1)

                    @block.scalar
                    def _(act):
                        for b in range(NQ):
                            width = (b + 1) * P
                            for h in range(4):
                                act.wait_ge(S["a_scored"], 12 * b + h + 1)
                                n = 4 * b + h
                                if n >= 2:
                                    act.wait_ge(S["a_summed"], n - 1)
                                nc.scalar.activation(rl[:, h % 2, 0:width], PS[:, (h % 2) * 1024:(h % 2) * 1024 + width],
                                                     ACT.Relu, scale=0.125).then_inc(S["a_relu"], 1)

                            def turn(h):
                                n = NH * b + h
                                act.wait_ge(S["a_transposed"], n + 1)
                                nc.scalar.activation(pT[:, h % 2, 0:b + 1, :].rearrange("p k t -> p (k t)"),
                                                     PS[:, 2048:2048 + width], ACT.Copy).then_inc(S["a_turned"], 1)
                                if h % 4 == 3:
                                    m = 2 * b + h // 4
                                    act.wait_ge(S["a_latent"], m + 1)
                                    if m:
                                        act.wait_ge(S["a_value"], m)
                                    nc.scalar.activation(lat[:, :, :].rearrange("p h t -> p (h t)"), bank(6), ACT.Copy)\
                                        .then_inc(S["a_latcopy"], 1)

                            for h in range(NH):
                                n = NH * b + h
                                act.wait_ge(S["a_added"], n + 1)
                                if n >= 2:
                                    act.wait_ge(S["a_transposed"], n - 1)
                                nc.scalar.activation(pr[:, h % 2, 0:width], sm[:, h % 2, 0:width], ACT.Exp,
                                                     bias=nmx[:, h % 2:h % 2 + 1], accum_out=rs[:, h % 2:h % 2 + 1])\
                                    .then_inc(S["a_exp"], 1)
                                if h:
                                    turn(h - 1)
                            turn(NH - 1)
                            act.wait_ge(S["a_value"], 2 * b + 2)
                            nc.scalar.activation(mT[:, 0:4, b * P:b * P + P], bank(7).rearrange("p (k t) -> p k t", k=4),
                                                 ACT.Copy).then_inc(S["a_stored"], 1)

                    @block.vector
                    def _(dve):
                        link = Link(dve, dve_step)
                        for b in range(NQ):
                            width = (b + 1) * P
                            full = slice(0, width)
                            for h in range(4):
                                dve.wait_ge(S["a_relu"], 4 * b + h + 1)
                                if h == 0:
                                    ins = nc.vector.tensor_scalar(score[:, full], rl[:, 0, full], wis[:, b, 0:1], None,
                                                                  ALU.mult)
                                else:
                                    ins = nc.vector.scalar_tensor_tensor(score[:, full], rl[:, h % 2, full],
                                                                         wis[:, b, h:h + 1], score[:, full], ALU.mult,
                                                                         ALU.add)
                                ins.then_inc(S["a_summed"], 1)
                                dve.wait_ge(S["a_summed"], 4 * b + h + 1)
                            diag = slice(b * P, b * P + P)
                            if width > TOPK:
                                link(nc.vector.tensor_tensor(score[:, diag], score[:, diag], neg[:, :], ALU.add))
                                src = score
                                for r in range(TOPK // 8):
                                    link(nc.vector.max(best[:, :], src[:, full]))
                                    if r + 1 < TOPK // 8:
                                        link(nc.vector.match_replace(work[:, full], best[:, :], src[:, full], -3.0e38))
                                    src = work
                                thr = best[:, 7:8]
                                link(nc.vector.tensor_scalar(bias[:, full], score[:, full], thr, 0.0, ALU.is_gt, ALU.add,
                                                             accum_out=count[:, 0:1]))
                                link(nc.vector.tensor_scalar(count[:, 1:2], count[:, 0:1], -1.0, float(TOPK), ALU.mult,
                                                             ALU.add))
                                link(nc.vector.tensor_scalar(eq[:, full], score[:, full], thr, None, ALU.is_equal))
                                link(nc.vector.tensor_tensor_scan(work[:, full], one_row[:, full], eq[:, full], 0.0,
                                                                  ALU.mult, ALU.add))
                                link(nc.vector.scalar_tensor_tensor(eq[:, full], work[:, full], count[:, 1:2],
                                                                    eq[:, full], ALU.is_le, ALU.mult))
                                link(nc.vector.tensor_tensor(bias[:, full], bias[:, full], eq[:, full], ALU.add))
                                link(nc.vector.tensor_scalar(bias[:, full], bias[:, full], -NEG, NEG, ALU.mult, ALU.add))
                                link(nc.vector.tensor_tensor(bias[:, diag], bias[:, diag], neg[:, :], ALU.add))
                            else:
                                if b:
                                    link(nc.vector.memset(bias[:, 0:b * P], 0.0))
                                link(nc.vector.tensor_copy(bias[:, diag], neg[:, :]))

                            def add(h):
                                s = h % 2
                                n = NH * b + h
                                dve.wait_ge(S["a_scored"], 12 * b + 4 + h + 1)
                                if n >= 2:
                                    dve.wait_ge(S["a_exp"], n - 1)
                                link(nc.vector.tensor_tensor_reduce(
                                    out=sm[:, s, full], in0=PS[:, s * 1024:s * 1024 + width], in1=bias[:, full],
                                    scale=1.0, scalar=-3.0e38, op0=ALU.add, op1=ALU.max, accum_out=mx[:, s:s + 1]))
                                nc.vector.tensor_scalar(nmx[:, s:s + 1], mx[:, s:s + 1], -1.0, None, ALU.mult)\
                                    .then_inc(S["a_added"], 1)

                            add(0)
                            for h in range(NH):
                                if h + 1 < NH:
                                    add(h + 1)
                                s = h % 2
                                dve.wait_ge(S["a_exp"], NH * b + h + 1)
                                link(nc.vector.reciprocal(ri[:, s:s + 1], rs[:, s:s + 1]))
                                nc.vector.tensor_scalar(pr[:, s, full], pr[:, s, full], ri[:, s:s + 1], None, ALU.mult)\
                                    .then_inc(S["a_prob"], 1)
                        link.end()

        def mod_cols(w):
            scale, shift, _ = mods[w]
            return (lambda k, c: scale[:, k, c // 2:c // 2 + 1]), (lambda k, c: shift[:, k, c // 2:c // 2 + 1])

        with ExitStack() as first:
            hT = sb(first, "hT", [P, KD, T])
            norm_stage("norm_e", xT, hT, ALL_CHUNKS, KD, 1e-6, False, *mod_cols("e"))
            project_stage("in_e", A["in_e"], 0, 24, hT, ALL_CHUNKS, proj_e)
            even_branch_stage(hT)
            combine_stage("out_e", A["out_e"], KD, hT, ALL_CHUNKS, gated_update(mods["e"][2], True))
            norm_stage("norm_o", xT, hT, ALL_CHUNKS, KD, 1e-6, False, *mod_cols("o"))
            project_stage("in_o", A["in_o"], 0, 12, hT, ALL_CHUNKS, proj_o)
            project_stage("in_o2", A["in_o"], 12, 20, hT, MAIN_CHUNKS, proj_o)
        mix_stage()
        scan_stage()
        with ExitStack() as odd:
            yT = sb(odd, "yT", [P, KD, SEQ])
            rwkv_out_stage(yT)
            with ExitStack() as conf:
                cv = sb(conf, "cv", [P, JB, SEQ])
                conformer_conv_stage(cv)
                norm_stage("conf_ln", cv, cv, MAIN_CHUNKS, JB, 1e-5, True, lambda k, c: v("conf_ln_g", k),
                           lambda k, c: v("conf_ln_b", k))
                conformer_gate_stage(cv, yT)
            combine_stage("out_o", A["out_o"], KD, yT, MAIN_CHUNKS, gated_update(mods["o"][2], False))
        norm_stage("final_norm", xT, xT, MAIN_CHUNKS, KD, 1e-6, False, lambda k, c: v("final_g", k), zero)
        ffn_stage("ffn1", A["ffn1_up"], A["ffn1_down"])
        norm_stage("ln1", xT, xT, MAIN_CHUNKS, KD, 1e-5, True, lambda k, c: v("ln1_g_2", k),
                   lambda k, c: v("ln1_b_2", k))
        project_stage("in_2", A["w_in"], 0, IN_TILES_2, xT, MAIN_CHUNKS, proj_2)
        with ExitStack() as mixer:
            mT = sb(mixer, "mT", [P, KD, SEQ])
            gmlp_stage(mT)
            with ExitStack():
                attention_stage(mT)
            combine_stage("out_2", A["w_out"], KD, mT, MAIN_CHUNKS, deepnorm_update)
        norm_stage("ln2", xT, xT, MAIN_CHUNKS, KD, 1e-5, True, lambda k, c: v("ln2_g_2", k),
                   lambda k, c: v("ln2_b_2", k))
        ffn_stage("ffn2", A["ffn2_up"], A["ffn2_down"])
        norm_stage("ln3", xT, xT, MAIN_CHUNKS, KD, 1e-5, True, lambda k, c: v("ln3_g_2", k),
                   lambda k, c: v("ln3_b_2", k), out_dram=A["out"])


def constants():
    i = np.arange(P)
    same_head = (i[:, None] // 64 == i[None, :] // 64)
    before = (i[:, None] < i[None, :])
    eye = np.eye(P)
    ev = np.stack([np.stack([m, m + eye, m, m + eye]) for m in (before * 1.0, before.T * 1.0)])
    inv = []
    for lv in range(N_LEVELS):
        b = i >> lv
        lower = (b[:, None] % 2 == 1) & (b[None, :] == b[:, None] - 1)
        inv.append(np.stack([lower + eye, lower.T + eye]))
    reset = np.ones((P, JB, P))
    reset[:, :, 0] = 0
    counts = []
    for w in POOL_WINDOWS:
        for length in (LINE, CTX):
            t = np.arange(length)
            lo, hi = np.clip(t - w // 2, 0, length), np.clip(t - w // 2 + w, 0, length)
            counts.append(1.0 / (hi - lo))
    counts = np.concatenate(counts).reshape(1, JB, LINE + CTX)
    f = lambda a: np.ascontiguousarray(np.asarray(a, np.float32))
    return {"ident": f(eye), "ones": f(np.ones((P, P))), "head_ones": f(same_head), "tri": f(before + eye),
            "neg": f(np.where(before, NEG, 0.0)), "reset": f(reset), "evmask": f(ev.transpose(2, 0, 1, 3)),
            "invmask": f(np.stack(inv).transpose(2, 0, 1, 3)),
            "inv_count": f(np.broadcast_to(counts, (P, JB, LINE + CTX)))}


def kernel(**inputs):
    import concourse.bacc as bacc
    from concourse.bass_utils import run_bass_kernel_spmd

    g = {k: np.asarray(a) for k, a in inputs.items()}

    def tiles(w, order=None):
        k, n = w.shape
        t = w.reshape(k // P, P, n // P, P).transpose(2, 1, 0, 3)
        return t if order is None else t[order]

    def columns(a):
        return a.reshape(-1, P).T

    def features_first(a):
        return a.T.reshape(-1, P, a.shape[0]).transpose(1, 0, 2)

    a = {"vecs": np.concatenate([columns(g[n]) for n, _ in VECS], axis=1)}
    a["x"] = features_first(g["x"][0])
    a["ctx"] = features_first(g["ctx"][0])
    a["ada"] = np.concatenate([tiles(g["ada_w_e"][0]), tiles(g["ada_w_o"][0])])
    a["in_e"] = tiles(g["in_e"][0], [q * JB + i for i in range(JB) for q in range(6)])
    a["out_e"] = tiles(g["out_e"][0])
    a["pool_w"] = g["pool_w"][0].transpose(1, 0, 2)
    a["in_o"] = tiles(g["in_o"][0], [q * JB + i for q in (0, 2, 3, 1, 4, 5, 6, 7) for i in range(JB)])
    a["out_o"] = tiles(g["out_o"][0])
    by_k = lambda w: w.reshape(-1, P, w.shape[-1]).transpose(1, 0, 2)
    for n, (first, second) in enumerate((("w1", "w2"), ("a1", "a2"))):
        a[f"low1_{n}"] = by_k(np.concatenate([g[first][0, 0], g[first][0, 1]], axis=1))
        a[f"low2_{n}"] = np.concatenate([g[second][0, 0], g[second][0, 1]], axis=0)
    a["low1_2"], a["low2_2"] = by_k(g["g1"][0]), g["g2"][0]
    for n in (1, 2):
        up = [tiles(g[f"ffn{n}_w{m}_2"][0]) for m in (1, 3)]
        a[f"ffn{n}_up"] = np.stack(up, axis=2)
        a[f"ffn{n}_down"] = tiles(g[f"ffn{n}_w2_2"][0])
    w_in = g["w_in_2"][0]
    pad = np.zeros((D, IN_TILES_2 * P - w_in.shape[1]), w_in.dtype)
    a["w_in"] = tiles(np.concatenate([w_in[:, :964], pad, w_in[:, 964:]], axis=1))
    a["w_out"] = tiles(g["w_out_2"][0])
    a["w_uk"] = g["w_uk_2"][0].transpose(0, 2, 1).reshape(4, P, P).transpose(1, 0, 2)
    a["w_uv"] = g["w_uv_2"][0].transpose(1, 0, 2)
    a["gmlp_ws"] = g["gmlp_ws_2"][0].transpose(2, 0, 1)
    a["gmlp_bs"] = g["gmlp_bs_2"][0][None]
    a = {n: np.ascontiguousarray(x) for n, x in a.items()}
    a.update(constants())

    nc = bacc.Bacc("TRN2", target_bir_lowering=False, num_devices=1)
    fp32 = mybir.dt.float32
    A = {n: nc.dram_tensor("in_" + n, x.shape, fp32, kind="ExternalInput").ap() for n, x in a.items()}
    A["low1"] = [A[f"low1_{n}"] for n in range(3)]
    A["low2"] = [A[f"low2_{n}"] for n in range(3)]
    A["out"] = nc.dram_tensor("out", (P, KD, SEQ), fp32, kind="ExternalOutput").ap()
    program(nc, A)
    r = run_bass_kernel_spmd(nc, [{"in_" + n: x for n, x in a.items()}], core_ids=[0])
    y = r.results[0]["out"]
    return np.ascontiguousarray(y.transpose(1, 0, 2).reshape(D, SEQ).T)[None]
```

```python
from contextlib import ExitStack, contextmanager

import concourse.bass as bass
import numpy as np
from concourse import mybir

P = 128
D = 1024
KD = D // P
SEQ = 1024
CTX = 256
T = SEQ + CTX
DB = 512
JB = DB // P
LINE = 64
PAD_T = SEQ + 2 + CTX
CTX_AT = SEQ + 2
D_FF = 2816
KF = D_FF // P
TOPK = 256
ALPHA = float(2 ** 0.25)
EXP_HALF = float(np.exp(-0.5))
NEG = -1.0e30
MAIN_CHUNKS = [(0, 512), (512, 512)]
ALL_CHUNKS = MAIN_CHUNKS + [(SEQ, CTX)]
PAD_CHUNKS = [(0, 512), (512, 512), (1024, PAD_T - 1024)]
POOL_WINDOWS = (2, 4, 8, 16)
N_LEVELS = 7
IN_TILES_2 = 16

VECS = [("c", 8), ("c_ctx", 8), ("ada_b_e", 24), ("ada_b_o", 24), ("norm_e", 8), ("norm_o", 8), ("pool_scale", 4),
        ("sconv_w", 12), ("rwkv_mu", 24), ("w0", 8), ("a0", 8), ("k_k", 4), ("k_a", 4), ("r_k", 4), ("lnx_g", 4),
        ("lnx_b", 4), ("conf_dw_w", 124), ("conf_dw_b", 4), ("conf_ln_g", 4), ("conf_ln_b", 4), ("final_g", 8),
        ("ln1_g_2", 8), ("ln1_b_2", 8), ("kv_norm_g_2", 1), ("gmlp_ln_g_2", 4), ("gmlp_ln_b_2", 4), ("ln2_g_2", 8),
        ("ln2_b_2", 8), ("ln3_g_2", 8), ("ln3_b_2", 8)]
VCOL = {}
NV = 0
for _name, _n in VECS:
    VCOL[_name] = NV
    NV += _n


class Sem:

    def __init__(self, nc, ctx, name):
        self.h = ctx.enter_context(nc.semaphore(name))
        self.base = 0


class Link:

    def __init__(self, eng, sem):
        self.eng, self.sem, self.loop, self.here = eng, sem, 0, 0

    def __call__(self, ins):
        self.here += 1
        ins.then_inc(self.sem.h, 1)
        self.eng.wait_ge(self.sem.h, self.sem.base + self.here + self.loop)

    @contextmanager
    def fori(self, n, per):
        self.sem.base += self.here
        self.here = 0
        with self.eng.Fori(0, n) as i:
            self.loop = i * per
            yield i
            assert self.here == per, (self.here, per)
        self.loop, self.here = 0, 0
        self.sem.base += n * per

    def end(self):
        self.sem.base += self.here
        self.here = 0


def program(nc, A):
    fp32 = mybir.dt.float32
    fp32r = mybir.dt.float32r
    ALU = mybir.AluOpType
    ACT = mybir.ActivationFunctionType
    root = ExitStack()
    dram = lambda name, shape: nc.dram_tensor(name, shape, fp32)
    proj_e = dram("proj_e", [24, P, T])
    proj_o = dram("proj_o", [32, P, T])
    scan_in = dram("scan_in", [8, JB, P, PAD_T])
    gate_o = dram("gate_o", [JB, P, PAD_T])
    scan_out = dram("scan_out", [2, P, JB, SEQ])
    proj_2 = dram("proj_2", [IN_TILES_2, P, SEQ])
    S_R, S_K, S_V, S_KK, S_LD0, S_A0, S_LD1, S_A1 = range(8)

    with root:
        def sb(ctx, name, shape):
            return ctx.enter_context(nc.sbuf_tensor(name, shape, fp32))

        def sem(name):
            return Sem(nc, root, name)

        PS = root.enter_context(nc.psum_tensor("PS", [P, 8 * 512], fp32))

        def bank(b, n=512, at=0):
            return PS[:, b * 512 + at:b * 512 + at + n]

        xT = sb(root, "xT", [P, KD, T])
        vec = sb(root, "vec", [P, NV])
        ident = sb(root, "ident", [P, P])
        ones = sb(root, "ones", [P, P])
        head_ones = sb(root, "head_ones", [P, P])
        mods = {w: [sb(root, f"mod_{w}{m}", [P, KD, 2]) for m in "sbg"] for w in "eo"}

        def v(name, j=0, n=1):
            return vec[:, VCOL[name] + j:VCOL[name] + j + n]

        dve_step, act_step, pool_step = sem("dve_step"), sem("act_step"), sem("pool_step")
        loaded = sem("loaded")
        w_loaded = [sem(f"w_loaded{s}") for s in range(2)]
        tile_done = [sem(f"tile_done{s}") for s in range(2)]
        evacuated = [sem(f"evacuated{s}") for s in range(2)]
        gated = [sem(f"gated{s}") for s in range(2)]
        stored = [sem(f"stored{s}") for s in range(2)]
        w_high = [sem(f"w_high{s}") for s in range(2)]
        w_low = [sem(f"w_low{s}") for s in range(2)]
        parts_ready = sem("parts_ready")
        high_ready = sem("high_ready")
        slot_in = [sem(f"slot_in{s}") for s in range(2)]
        slot_free = [sem(f"slot_free{s}") for s in range(2)]

        epsc = sb(root, "epsc", [P, 4])
        EPS = {1e-6: 0, 1e-5: 1, 64e-5: 2, 0.0: 3}
        o_ready = sem("o_ready")
        credited = tile_done + evacuated + gated + stored + slot_free + w_high + w_low + [o_ready]
        with nc.Block("start") as block:
            @block.gpsimd
            def _(pool):
                for q in credited:
                    pool.sem_inc(q.h, 1)
                    q.base += 1
                for e, i in EPS.items():
                    nc.gpsimd.memset(epsc[:, i:i + 1], e).then_inc(pool_step.h, 1)
        pool_step.base += 4

        with ExitStack() as ctx:
            ring = sb(ctx, "ada_ring", [P, 2, KD, P])
            cs = sb(ctx, "cs", [P, KD, 2])
            mod = sb(ctx, "mod", [P, 48, 2])
            with nc.Block("setup") as block:
                @block.sync
                def _(sp):
                    sp.dma_start(vec[:, :], A["vecs"]).then_inc(loaded.h, 16)
                    sp.dma_start(ident[:, :], A["ident"]).then_inc(loaded.h, 16)
                    sp.dma_start(ones[:, :], A["ones"]).then_inc(loaded.h, 16)
                    sp.dma_start(head_ones[:, :], A["head_ones"]).then_inc(loaded.h, 16)
                    sp.dma_start(xT[:, :, 0:SEQ], A["x"]).then_inc(loaded.h, 16)
                    sp.dma_start(xT[:, :, SEQ:T], A["ctx"]).then_inc(loaded.h, 16)
                    with sp.Fori(0, 24) as i:
                        for s in range(2):
                            sp.wait_ge(tile_done[s].h, tile_done[s].base + i)
                            sp.dma_start(ring[:, s], A["ada"][i * 2 + s]).then_inc(w_loaded[s].h, 16)

                @block.scalar
                def _(act):
                    act.wait_ge(loaded.h, 6 * 16)
                    for n, name in enumerate(("c", "c_ctx")):
                        nc.scalar.activation(cs[:, :, n], v(name, 0, 8), ACT.Silu).then_inc(act_step.h, 1)

                @block.tensor
                def _(pe):
                    pe.wait_ge(act_step.h, 2)
                    with pe.Fori(0, 24) as i:
                        for s in range(2):
                            pe.wait_ge(w_loaded[s].h, i * 16 + 16)
                            for k in range(KD):
                                last = nc.tensor.matmul(PS[:, bass.ds(i * 4 + 2 * s, 2)], ring[:, s, k, :], cs[:, k, :],
                                                        start=k == 0, stop=k == KD - 1)
                            last.then_inc(tile_done[s].h, 1)

                @block.vector
                def _(dve):
                    link = Link(dve, dve_step)
                    dve.wait_ge(tile_done[0].h, tile_done[0].base + 24)
                    dve.wait_ge(tile_done[1].h, tile_done[1].base + 24)
                    bias = vec[:, VCOL["ada_b_e"]:VCOL["ada_b_e"] + 48].unsqueeze(2).to_broadcast([P, 48, 2])
                    link(nc.vector.tensor_tensor(mod[:, :, :], PS[:, 0:96].rearrange("p (n w) -> p n w", w=2), bias,
                                                 ALU.add))
                    for o, w, norm in ((0, "e", "norm_e"), (24, "o", "norm_o")):
                        scale, shift, gate = mods[w]
                        g = v(norm, 0, 8).unsqueeze(2).to_broadcast([P, KD, 2])
                        link(nc.vector.tensor_copy(shift[:, :, :], mod[:, o:o + 8, :]))
                        link(nc.vector.scalar_tensor_tensor(scale[:, :, :], mod[:, o + 8:o + 16, :], 1.0, g, ALU.add,
                                                            ALU.mult))
                        link(nc.vector.tensor_copy(gate[:, :, :], mod[:, o + 16:o + 24, :]))
                    link.end()
            act_step.base += 2
            loaded.base += 96
            for s in range(2):
                w_loaded[s].base += 24 * 16
                tile_done[s].base += 24

        sq_done, sum_done, std_done, norm_done, mean_done, cen_done = [
            sem(n) for n in ("sq_done", "sum_done", "std_done", "norm_done", "mean_done", "cen_done")]

        def norm_stage(name, src, dst, chunks, kt, eps, centre, gain, bias, out_dram=None):
            n = len(chunks)
            inv = 1.0 / (kt * P)
            with ExitStack() as ctx:
                sq = sb(ctx, f"{name}_sq", [P, kt, 512])
                cen = sb(ctx, f"{name}_cen", [P, kt, 512])
                mean = sb(ctx, f"{name}_mean", [P, 512])
                std = sb(ctx, f"{name}_std", [P, 512])
                rstd = sb(ctx, f"{name}_rstd", [P, 512])
                stored_out = stored[0]
                with nc.Block(name) as block:
                    @block.tensor
                    def _(pe):
                        for c, (t, w) in enumerate(chunks):
                            if centre:
                                if c:
                                    pe.wait_ge(mean_done.h, mean_done.base + c)
                                for k in range(kt):
                                    last = nc.tensor.matmul(bank(1, w), ones[:, :], src[:, k, t:t + w], start=k == 0,
                                                            stop=k == kt - 1)
                                last.then_inc(cen_done.h, 1)
                            pe.wait_ge(sq_done.h, sq_done.base + c + 1)
                            if c:
                                pe.wait_ge(std_done.h, std_done.base + c)
                            for k in range(kt):
                                last = nc.tensor.matmul(bank(0, w), ones[:, :], sq[:, k, 0:w], start=k == 0,
                                                        stop=k == kt - 1)
                            last.then_inc(sum_done.h, 1)

                    @block.vector
                    def _(dve):
                        link = Link(dve, dve_step)
                        for c, (t, w) in enumerate(chunks):
                            x = src[:, :, t:t + w]
                            if c:
                                dve.wait_ge(act_step.h, act_step.base + c * kt)
                            if centre:
                                dve.wait_ge(cen_done.h, cen_done.base + c + 1)
                                link(nc.vector.tensor_scalar(mean[:, 0:w], bank(1, w), inv, None, ALU.mult))
                                m = mean[:, 0:w].unsqueeze(1).to_broadcast([P, kt, w])
                                nc.vector.tensor_tensor(cen[:, :, 0:w], x, m, ALU.subtract).then_inc(mean_done.h, 1)
                                dve.wait_ge(mean_done.h, mean_done.base + c + 1)
                                x = cen[:, :, 0:w]
                            dve.wait_ge(std_done.h, std_done.base + c + 1)
                            link(nc.vector.reciprocal(rstd[:, 0:w], std[:, 0:w]))
                            r = rstd[:, 0:w].unsqueeze(1).to_broadcast([P, kt, w])
                            nc.vector.tensor_tensor(cen[:, :, 0:w], x, r, ALU.mult).then_inc(norm_done.h, 1)
                        link.end()

                    @block.scalar
                    def _(act):
                        link = Link(act, act_step)
                        for c, (t, w) in enumerate(chunks):
                            x = src[:, :, t:t + w]
                            if centre:
                                act.wait_ge(mean_done.h, mean_done.base + c + 1)
                                x = cen[:, :, 0:w]
                            nc.scalar.activation(sq[:, :, 0:w], x, ACT.Square).then_inc(sq_done.h, 1)
                            act.wait_ge(sum_done.h, sum_done.base + c + 1)
                            if c:
                                act.wait_ge(norm_done.h, norm_done.base + c)
                            nc.scalar.activation(std[:, 0:w], bank(0, w), ACT.Sqrt, scale=inv, bias=eps_col(eps))\
                                .then_inc(std_done.h, 1)
                            act.wait_ge(norm_done.h, norm_done.base + c + 1)
                            for k in range(kt):
                                link(nc.scalar.activation(dst[:, k, t:t + w], cen[:, k, 0:w], ACT.Identity,
                                                          scale=gain(k, c), bias=bias(k, c)))
                            if out_dram is not None:
                                act.dma_start(out_dram[:, :, t:t + w], dst[:, :, t:t + w])\
                                    .then_inc(stored_out.h, 16)
                        if out_dram is not None:
                            act.wait_ge(stored_out.h, stored_out.base + 16 * n)
                        norm_stage.act_n = link.here
                act_step.base += n * kt
            if centre:
                mean_done.base += n
                cen_done.base += n
            for q in (sq_done, sum_done, std_done, norm_done):
                q.base += n
            if out_dram is not None:
                stored_out.base += 16 * n

        def eps_col(e):
            return epsc[:, EPS[e]:EPS[e] + 1]

        def zero(k=0, c=0):
            return eps_col(0.0)


        class Parts:

            def __init__(self, ctx, name, kt, width):
                self.high = ctx.enter_context(nc.sbuf_tensor(f"{name}_high", [P, kt, width], fp32r))
                self.low = ctx.enter_context(nc.sbuf_tensor(f"{name}_low", [P, kt, width], fp32r))

        def high_part(out, x):
            return nc.scalar.activation(out, x, ACT.Copy)

        def low_part(out, x, high):
            return nc.vector.tensor_tensor(out, x, high.bitcast(fp32), ALU.subtract)

        class Weights:

            def __init__(self, ctx, name, kt):
                self.raw = sb(ctx, f"{name}_raw", [P, 2, kt, P])
                self.high = ctx.enter_context(nc.sbuf_tensor(f"{name}_wh", [P, 2, kt, P], fp32r))
                self.low = ctx.enter_context(nc.sbuf_tensor(f"{name}_wl", [P, 2, kt, P], fp32r))

            def load(self, sp, n, s, src):
                sp.wait_ge(w_low[s].h, w_low[s].base + n)
                sp.dma_start(self.raw[:, s], src).then_inc(w_loaded[s].h, 16)

            def cut_high(self, act, n, s):
                act.wait_ge(w_loaded[s].h, w_loaded[s].base + n * 16 + 16)
                act.wait_ge(tile_done[s].h, tile_done[s].base + n)
                high_part(self.high[:, s], self.raw[:, s]).then_inc(w_high[s].h, 1)

            def cut_low(self, dve, n, s):
                dve.wait_ge(w_high[s].h, w_high[s].base + n + 1)
                low_part(self.low[:, s], self.raw[:, s], self.high[:, s]).then_inc(w_low[s].h, 1)

            def product(self, pe, out, s, parts, k0, kt, t, w):
                for k in range(kt):
                    wh, wl = self.high[:, s, k, :], self.low[:, s, k, :]
                    xh, xl = parts.high[:, k0 + k, t:t + w], parts.low[:, k0 + k, t:t + w]
                    nc.tensor.matmul(out, wh, xh, start=k == 0, stop=False)
                    nc.tensor.matmul(out, wh, xl, start=False, stop=False)
                    last = nc.tensor.matmul(out, wl, xh, start=False, stop=k == kt - 1)
                return last

        def ahead(eng, n_tiles, unroll, prepare, finish):
            def call(f, i, q):
                if q == unroll:
                    i, q = i + 1, 0
                f(i, q, q % 2, i * (unroll // 2) + q // 2)

            turns = n_tiles // unroll
            if prepare:
                call(prepare, 0, 0)
            if turns > 1:
                with eng.Fori(0, turns - 1) as i:
                    for q in range(unroll):
                        if prepare:
                            call(prepare, i, q + 1)
                        call(finish, i, q)
            for q in range(unroll):
                if prepare and q + 1 < unroll:
                    call(prepare, turns - 1, q + 1)
                call(finish, turns - 1, q)

        def cut_parts(name, src, parts, kt, chunks):
            def on_act(act):
                for t, w in chunks:
                    high_part(parts.high[:, :, t:t + w], src[:, 0:kt, t:t + w]).then_inc(high_ready.h, 1)

            def on_dve(dve):
                for c, (t, w) in enumerate(chunks):
                    dve.wait_ge(high_ready.h, high_ready.base + c + 1)
                    low_part(parts.low[:, :, t:t + w], src[:, 0:kt, t:t + w], parts.high[:, :, t:t + w])\
                        .then_inc(parts_ready.h, 1)
            return on_act, on_dve

        def product_stage(name, weights_of, n_tiles, kt, src, parts, chunks, finish, store=None):
            with ExitStack() as ctx:
                ring = Weights(ctx, name, kt)
                cut = src is not None
                if cut:
                    parts = Parts(ctx, name, kt, chunks[-1][0] + chunks[-1][1])
                    cut_act, cut_dve = cut_parts(name, src, parts, kt, chunks)
                with nc.Block(name) as block:
                    @block.sync
                    def _(sp):
                        with sp.Fori(0, n_tiles // 2) as i:
                            for s in range(2):
                                ring.load(sp, i, s, weights_of(i * 2 + s))

                    @block.scalar
                    def _(act):
                        def prepare(i, q, s, n):
                            ring.cut_high(act, n, s)
                            if cut and isinstance(i, int) and i == q == 0:
                                cut_act(act)

                        def finish_tile(i, q, s, n):
                            if store:
                                act.wait_ge(evacuated[s].h, evacuated[s].base + n + 1)
                                store(act, i * 2 + q, s)
                        ahead(act, n_tiles, 2, prepare, finish_tile)
                        if store:
                            for s in range(2):
                                act.wait_ge(stored[s].h, stored[s].base + n_tiles // 2 * 16)

                    @block.vector
                    def _(dve):
                        def prepare(i, q, s, n):
                            ring.cut_low(dve, n, s)
                            if cut and isinstance(i, int) and i == q == 0:
                                cut_dve(dve)

                        def finish_tile(i, q, s, n):
                            dve.wait_ge(tile_done[s].h, tile_done[s].base + n + 1)
                            if store:
                                dve.wait_ge(stored[s].h, stored[s].base + n * 16)
                            finish(i * 2 + q, s).then_inc(evacuated[s].h, 1)
                        ahead(dve, n_tiles, 2, prepare, finish_tile)

                    @block.tensor
                    def _(pe):
                        with pe.Fori(0, n_tiles // 2) as i:
                            for s in range(2):
                                pe.wait_ge(w_low[s].h, w_low[s].base + i + 1)
                                pe.wait_ge(evacuated[s].h, evacuated[s].base + i)
                                for c, (t, w) in enumerate(chunks):
                                    if cut and s == 0:
                                        pe.wait_ge(parts_ready.h, parts_ready.base + c + 1)
                                    at = s * 1536 + t
                                    last = ring.product(pe, PS[:, at:at + w], s, parts, 0, kt, t, w)
                                last.then_inc(tile_done[s].h, 1)
            for s in range(2):
                w_loaded[s].base += 16 * (n_tiles // 2)
                for q in (w_high, w_low, tile_done, evacuated):
                    q[s].base += n_tiles // 2
                if store:
                    stored[s].base += 16 * (n_tiles // 2)
            if cut:
                high_ready.base += len(chunks)
                parts_ready.base += len(chunks)

        def project_stage(name, w_dram, w_at, n_tiles, rhs, chunks, dst):
            width = chunks[-1][0] + chunks[-1][1]
            with ExitStack() as ctx:
                stage = sb(ctx, f"{name}_stage", [P, 2, width])

                def finish(m, s):
                    return nc.vector.tensor_copy(stage[:, s, :], PS[:, s * 1536:s * 1536 + width])

                def store(act, m, s):
                    act.dma_start(dst[m + w_at][:, 0:width], stage[:, s, :]).then_inc(stored[s].h, 16)

                product_stage(name, lambda m: w_dram[m + w_at], n_tiles, KD, rhs, None, chunks, finish, store)

        def combine_stage(name, w_dram, rhs, chunks, update):
            product_stage(name, lambda m: w_dram[m], KD, KD, rhs, None, chunks, lambda m, s: update(m, s * 1536))

        def gated_update(gate, with_ctx):
            def update(n, at):
                last = None
                for col, t, w in ((0, 0, SEQ), (1, SEQ, CTX))[:2 if with_ctx else 1]:
                    x = xT[:, n, t:t + w]
                    last = nc.vector.scalar_tensor_tensor(x, PS[:, at + t:at + t + w],
                                                          gate[:, n, col:col + 1], x, ALU.mult, ALU.add)
                return last
            return update

        def deepnorm_update(n, at, alpha=ALPHA):
            x = xT[:, n, 0:SEQ]
            return nc.vector.scalar_tensor_tensor(x, x, alpha, PS[:, at:at + SEQ], ALU.mult, ALU.add)


        def even_branch_stage(yT):
            U, ZA, VB, GB, GC, ZB = range(6)
            LW = LINE + 16
            CW = CTX + 16
            PW = (SEQ // LINE) * LW + CW
            QL = LINE + 2
            QW = (SEQ // LINE) * QL + CTX + 2
            with ExitStack() as ctx:
                tin = sb(ctx, "tin", [P, 2, 6, T])
                pad = sb(ctx, "pool_pad", [P, PW])
                win = sb(ctx, "pool_win", [P, 2, PW])
                pooled = sb(ctx, "pooled", [P, T])
                cpad = sb(ctx, "conv_pad", [P, QW])
                conv = sb(ctx, "conv", [P, QW])
                silus = sb(ctx, "silus", [P, 2, T])
                pool_w = sb(ctx, "pool_w", [P, JB, P])
                inv_count = sb(ctx, "inv_count", [P, JB, LINE + CTX])

                def lines(t, at, lw, off, seg_pad):
                    n = SEQ // LINE
                    return (t[:, 0:n * lw].rearrange("p (l w) -> p l w", w=lw)[:, :, at:at + LINE],
                            t[:, n * lw + at:n * lw + at + CTX])

                def flat(t):
                    return t[:, 0:SEQ].rearrange("p (l w) -> p l w", w=LINE), t[:, SEQ:T]

                with nc.Block("even_branch") as block:
                    @block.sync
                    def _(sp):
                        sp.dma_start(pool_w[:, :, :], A["pool_w"]).then_inc(loaded.h, 16)
                        sp.dma_start(inv_count[:, :, :], A["inv_count"]).then_inc(loaded.h, 16)
                        for i in range(JB):
                            s = i % 2
                            if i >= 2:
                                sp.wait_ge(slot_free[s].h, slot_free[s].base + 1)
                            sp.dma_start(tin[:, s], proj_e[i * 6:i * 6 + 6].rearrange("n p t -> p n t"))\
                                .then_inc(slot_in[s].h, 16)

                    @block.tensor
                    def _(pe):
                        pe.wait_ge(loaded.h, loaded.base + 32)
                        for i in range(JB):
                            pe.wait_ge(gated[0].h, gated[0].base + i + 1)
                            if i:
                                pe.wait_ge(evacuated[0].h, evacuated[0].base + i)
                            for t, w in ALL_CHUNKS:
                                last = nc.tensor.matmul(PS[:, t:t + w], pool_w[:, i, :], pooled[:, t:t + w], start=True,
                                                        stop=True)
                            last.then_inc(tile_done[0].h, 1)

                    @block.scalar
                    def _(act):
                        for i in range(JB):
                            s = i % 2
                            act.wait_ge(slot_in[s].h, slot_in[s].base + 16 * (i // 2 + 1))
                            if i:
                                act.wait_ge(slot_free[1 - s].h, slot_free[1 - s].base + (i + 1) // 2)
                            for n, f in enumerate((ZA, ZB)):
                                nc.scalar.activation(silus[:, n, :], tin[:, s, f, :], ACT.Silu)\
                                    .then_inc(std_done.h, 1)

                    @block.vector
                    def _(dve):
                        link = Link(dve, dve_step)
                        link(nc.vector.memset(pad[:, :], 0.0))
                        link(nc.vector.memset(cpad[:, :], 0.0))
                        dve.wait_ge(loaded.h, loaded.base + 32)
                        for i, window in enumerate(POOL_WINDOWS):
                            s = i % 2
                            dve.wait_ge(slot_in[s].h, slot_in[s].base + 16 * (i // 2 + 1))
                            for o, x in zip(lines(pad, 8, LW, 0, 0), flat(tin[:, s, U, :])):
                                link(nc.vector.tensor_copy(o, x))
                            src, n, width = pad, 1, PW
                            while n < window:
                                o = win[:, (n.bit_length() - 1) % 2, :]
                                width -= n
                                link(nc.vector.tensor_tensor(o[:, 0:width], src[:, 0:width], src[:, n:n + width],
                                                             ALU.add))
                                src, n = o, 2 * n
                            if i:
                                dve.wait_ge(tile_done[0].h, tile_done[0].base + i)
                            counts = (inv_count[:, i, 0:LINE].unsqueeze(1).to_broadcast([P, SEQ // LINE, LINE]),
                                      inv_count[:, i, LINE:LINE + CTX])
                            for o, x, q in zip(flat(pooled), lines(src, 8 - window // 2, LW, 0, 0), counts):
                                link(nc.vector.tensor_tensor(o, x, q, ALU.mult))
                            nc.vector.tensor_tensor(pooled[:, :], pooled[:, :], tin[:, s, U, :], ALU.subtract)\
                                .then_inc(gated[0].h, 1)
                            for o, x, y in zip(lines(cpad, 1, QL, 0, 0), flat(tin[:, s, GC, :]), flat(tin[:, s, VB, :])):
                                link(nc.vector.tensor_tensor(o, x, y, ALU.mult))
                            link(nc.vector.tensor_scalar(conv[:, 1:QW - 1], cpad[:, 0:QW - 2], v("sconv_w", i), None,
                                                         ALU.mult))
                            for tap in (1, 2):
                                link(nc.vector.scalar_tensor_tensor(conv[:, 1:QW - 1], cpad[:, tap:QW - 2 + tap],
                                                                    v("sconv_w", 4 * tap + i), conv[:, 1:QW - 1],
                                                                    ALU.mult, ALU.add))
                            for o, x, y in zip(flat(yT[:, JB + i, :]), lines(conv, 1, QL, 0, 0),
                                               flat(tin[:, s, GB, :])):
                                link(nc.vector.tensor_tensor(o, x, y, ALU.mult))
                            dve.wait_ge(std_done.h, std_done.base + 2 * i + 2)
                            link(nc.vector.tensor_tensor(yT[:, JB + i, :], yT[:, JB + i, :], silus[:, 1, :], ALU.mult))
                            dve.wait_ge(tile_done[0].h, tile_done[0].base + i + 1)
                            nc.vector.scalar_tensor_tensor(yT[:, i, :], PS[:, 0:T], v("pool_scale", i), silus[:, 0, :],
                                                           ALU.mult, ALU.mult).then_inc(evacuated[0].h, 1)
                            dve.wait_ge(evacuated[0].h, evacuated[0].base + i + 1)
                            dve.sem_inc(slot_free[s].h, 1)
                        link.end()
            loaded.base += 32
            for s in range(2):
                slot_in[s].base += 32
                slot_free[s].base += 2
            gated[0].base += JB
            evacuated[0].base += JB
            tile_done[0].base += JB
            std_done.base += 2 * JB

        def mix_stage():
            U_AT, K_AT, V_AT, R_AT = 0, 4, 8, 12
            with ExitStack() as ctx:
                um = sb(ctx, "um", [P, 3, JB, PAD_T])
                zin = sb(ctx, "zin", [P, 2, PAD_T + 2])
                nb = sb(ctx, "nb", [P, PAD_T])
                zout = sb(ctx, "zout", [P, 2, PAD_T])
                kkr = sb(ctx, "kkr", [P, PAD_T])
                sq = sb(ctx, "kk_sq", [P, PAD_T])
                nrm = sb(ctx, "kk_norm", [P, PAD_T])
                mu_half = sb(ctx, "mu_half", [P, 24])
                mu_rest = sb(ctx, "mu_rest", [P, 24])
                hid = [sb(ctx, f"hid{n}", [P, PAD_T]) for n in range(3)]
                low1 = [sb(ctx, f"low1_{n}", [P, JB, m]) for n, m in ((0, 64), (1, 64), (2, 96))]
                low2 = [sb(ctx, f"low2_{n}", [m, DB]) for n, m in ((0, 64), (1, 64), (2, 96))]
                tiles = [(U_AT + j, None, (3, 4, 5), j) for j in range(JB)]
                for at, arr, mu in ((R_AT, S_R, 0), (K_AT, S_K, 1), (V_AT, S_V, 2)):
                    tiles += [(at + j, arr, (mu,), j) for j in range(JB)]
                n_z = len(tiles)
                lows = [(n, d, j) for n in (0, 1) for d in range(2) for j in range(JB)] + [(2, 0, j) for j in range(JB)]
                with nc.Block("mix") as block:
                    @block.sync
                    def _(sp):
                        for n in range(3):
                            sp.dma_start(low1[n][:, :, :], A["low1"][n]).then_inc(loaded.h, 16)
                            sp.dma_start(low2[n][:, :], A["low2"][n]).then_inc(loaded.h, 16)
                        sp.wait_ge(pool_step.h, pool_step.base + 1)
                        for q, (at, arr, mus, j) in enumerate(tiles):
                            s = q % 2
                            if q >= 2:
                                sp.wait_ge(slot_free[s].h, slot_free[s].base + q // 2)
                            sp.dma_start(zin[:, s, 1:SEQ + 1], proj_o[at][:, 0:SEQ]).then_inc(slot_in[s].h, 16)
                            if arr == S_R:
                                continue
                            sp.dma_start(zin[:, s, CTX_AT + 1:CTX_AT + CTX + 1], proj_o[at][:, SEQ:T])\
                                .then_inc(slot_in[s].h, 16)

                    @block.gpsimd
                    def _(pool):
                        nc.gpsimd.memset(zin[:, :, :], 0.0).then_inc(pool_step.h, 1)

                    def z_arrived(eng, q):
                        n = [32 if tiles[p][1] != S_R else 16 for p in range(q % 2, q + 1, 2)]
                        eng.wait_ge(slot_in[q % 2].h, slot_in[q % 2].base + sum(n))

                    @block.vector
                    def _(dve):
                        link = Link(dve, dve_step)
                        link(nc.vector.tensor_scalar(mu_half[:, :], v("rwkv_mu", 0, 24), 0.5, None, ALU.mult))
                        link(nc.vector.tensor_scalar(mu_rest[:, :], v("rwkv_mu", 0, 24), -1.0, 1.0, ALU.mult, ALU.add))
                        zq = kq = 0
                        for q, (at, arr, mus, j) in enumerate(tiles):
                            s = q % 2
                            z_arrived(dve, q)
                            link(nc.vector.tensor_tensor(nb[:, :], zin[:, s, 0:PAD_T], zin[:, s, 2:PAD_T + 2], ALU.add))
                            for n, mu in enumerate(mus):
                                col = mu * 4 + j
                                if arr is None:
                                    o = um[:, n, j, :]
                                else:
                                    o = zout[:, zq % 2, :]
                                    if zq >= 2:
                                        dve.wait_ge(stored[zq % 2].h, stored[zq % 2].base + 16 * (zq // 2))
                                link(nc.vector.tensor_scalar(o, zin[:, s, 1:PAD_T + 1], mu_rest[:, col:col + 1], None,
                                                             ALU.mult))
                                nc.vector.scalar_tensor_tensor(o, nb[:, :], mu_half[:, col:col + 1], o, ALU.mult,
                                                               ALU.add).then_inc(norm_done.h, 1)
                            done = norm_done.base + min(q + 1, JB) * 3 + max(q + 1 - JB, 0)
                            dve.wait_ge(norm_done.h, done)
                            dve.sem_inc(slot_free[s].h, 1)
                            if arr is not None:
                                if arr == S_K:
                                    if kq:
                                        dve.wait_ge(gated[1].h, gated[1].base + 16 * kq)
                                    nc.vector.tensor_scalar(kkr[:, :], o, v("k_k", j), None, ALU.mult)\
                                        .then_inc(mean_done.h, 1)
                                    dve.wait_ge(std_done.h, std_done.base + kq + 1)
                                    link(nc.vector.tensor_scalar(nrm[:, :], nrm[:, :], 1e-12, None, ALU.max))
                                    link(nc.vector.reciprocal(nrm[:, :], nrm[:, :]))
                                    nc.vector.tensor_tensor(kkr[:, :], kkr[:, :], nrm[:, :], ALU.mult)\
                                        .then_inc(cen_done.h, 1)
                                    dve.wait_ge(cen_done.h, cen_done.base + kq + 1)
                                    kq += 1
                                zq += 1
                        for m, (n, d, j) in enumerate(lows[:8]):
                            dve.wait_ge(sum_done.h, sum_done.base + m + 1)
                            nc.vector.tensor_scalar(zout[:, m % 2, :], zout[:, m % 2, :], -EXP_HALF, None, ALU.mult)\
                                .then_inc(gated[0].h, 1)
                        link.end()

                    @block.scalar
                    def _(act):
                        for n, f in enumerate((ACT.Tanh, ACT.Copy, ACT.Sigmoid)):
                            m = (64, 64, 96)[n]
                            act.wait_ge(tile_done[0].h, tile_done[0].base + n + 1)
                            nc.scalar.activation(hid[n][0:m, :], PS[0:m, 0:PAD_T], f).then_inc(evacuated[0].h, 1)
                        zq = kq = 0
                        for q, (at, arr, mus, j) in enumerate(tiles[JB:]):
                            act.wait_ge(norm_done.h, norm_done.base + 3 * JB + q + 1)
                            act.dma_start(scan_in[arr, j], zout[:, zq % 2, :]).then_inc(stored[zq % 2].h, 16)
                            zq += 1
                            if arr == S_K:
                                act.wait_ge(mean_done.h, mean_done.base + kq + 1)
                                nc.scalar.activation(sq[:, :], kkr[:, :], ACT.Square).then_inc(sq_done.h, 1)
                                act.wait_ge(tile_done[1].h, tile_done[1].base + kq + 1)
                                nc.scalar.activation(nrm[:, :], PS[:, 1536:1536 + PAD_T], ACT.Sqrt)\
                                    .then_inc(std_done.h, 1)
                                act.wait_ge(cen_done.h, cen_done.base + kq + 1)
                                act.dma_start(scan_in[S_KK, j], kkr[:, :]).then_inc(gated[1].h, 16)
                                kq += 1
                        for m, (n, d, j) in enumerate(lows):
                            s = m % 2
                            act.wait_ge(tile_done[s].h, tile_done[s].base + (3 if s == 0 else 4) + m // 2 + 1)
                            act.wait_ge(stored[s].h, stored[s].base + 16 * (6 + m // 2))
                            o = zout[:, s, :]
                            x = PS[:, s * 1536:s * 1536 + PAD_T]
                            if n == 2:
                                nc.scalar.activation(o, x, ACT.Copy).then_inc(sum_done.h, 1)
                                dst = gate_o[j]
                            else:
                                nc.scalar.activation(o, x, ACT.Sigmoid, bias=v(("w0", "a0")[n], d * 4 + j))\
                                    .then_inc(sum_done.h, 1)
                                dst = scan_in[(S_LD0, S_LD1, S_A0, S_A1)[n * 2 + d], j]
                            act.wait_ge(sum_done.h, sum_done.base + m + 1)
                            if n == 0:
                                act.wait_ge(gated[0].h, gated[0].base + m + 1)
                            act.dma_start(dst, o).then_inc(stored[s].h, 16)
                        for s in range(2):
                            act.wait_ge(stored[s].h, stored[s].base + 16 * 16)
                        act.wait_ge(gated[1].h, gated[1].base + 16 * JB)

                    @block.tensor
                    def _(pe):
                        pe.wait_ge(loaded.h, loaded.base + 96)
                        pe.wait_ge(norm_done.h, norm_done.base + 3 * JB)
                        for n, m in enumerate((64, 64, 96)):
                            if n:
                                pe.wait_ge(evacuated[0].h, evacuated[0].base + n)
                            for t, w in PAD_CHUNKS:
                                for k in range(JB):
                                    last = nc.tensor.matmul(PS[0:m, t:t + w], low1[n][:, k, :], um[:, n, k, t:t + w],
                                                            start=k == 0, stop=k == JB - 1)
                            last.then_inc(tile_done[0].h, 1)
                        for kq in range(JB):
                            pe.wait_ge(sq_done.h, sq_done.base + kq + 1)
                            if kq:
                                pe.wait_ge(std_done.h, std_done.base + kq)
                            for t, w in PAD_CHUNKS:
                                last = nc.tensor.matmul(PS[:, 1536 + t:1536 + t + w], head_ones[:, :], sq[:, t:t + w],
                                                        start=True, stop=True)
                            last.then_inc(tile_done[1].h, 1)
                        pe.wait_ge(evacuated[0].h, evacuated[0].base + 3)
                        pe.wait_ge(std_done.h, std_done.base + JB)
                        for m, (n, d, j) in enumerate(lows):
                            s = m % 2
                            if m >= 2:
                                pe.wait_ge(sum_done.h, sum_done.base + m - 1)
                            lo, hi = (32 * d, 32 * d + 32) if n < 2 else (0, 96)
                            for t, w in PAD_CHUNKS:
                                last = nc.tensor.matmul(PS[:, s * 1536 + t:s * 1536 + t + w],
                                                        low2[n][lo:hi, j * P:j * P + P], hid[n][lo:hi, t:t + w],
                                                        start=True, stop=True)
                            last.then_inc(tile_done[s].h, 1)
            loaded.base += 96
            pool_step.base += 1
            for s in range(2):
                slot_in[s].base += 32 * (JB // 2) + 16 * (JB // 2) + 32 * JB
                slot_free[s].base += n_z // 2
                stored[s].base += 16 * (3 * JB // 2 + len(lows) // 2)
            tile_done[0].base += 3 + len(lows) // 2
            tile_done[1].base += JB + len(lows) // 2
            evacuated[0].base += 3
            norm_done.base += 3 * JB + 3 * JB
            mean_done.base += JB
            std_done.base += JB
            cen_done.base += JB
            sq_done.base += JB
            gated[1].base += 16 * JB
            gated[0].base += 8
            sum_done.base += len(lows)

        def scan_stage():
            LV = N_LEVELS - 1
            LINKS = 16
            N_T, N_X, N_XT = 4 * LV, 4 * LV, 4 * (LV - 1)
            LOADS = 48
            CTX_TURNS, MAIN_TURNS = CTX // P, SEQ // P
            LAST = CTX_TURNS + MAIN_TURNS - 1
            TOK_BANKS = (1, 2, 3, 4, 5, 6)
            with ExitStack() as ctx:
                tin = sb(ctx, "scan_tin", [P, 12, JB, P])
                AR = sb(ctx, "AR", [P, 2, 2, JB, 2, P])
                Bc = sb(ctx, "Bc", [P, 2, 2, JB, P])
                Kc = sb(ctx, "Kc", [P, 2, 2, JB, P])
                cum = sb(ctx, "cum", [P, 2, JB, P])
                cex = sb(ctx, "cex", [P, 2, JB, P])
                E1 = sb(ctx, "E1", [P, 2, JB, P])
                tok = sb(ctx, "tok", [P, 3, 2, JB, P])
                plog = sb(ctx, "plog", [P, 2, 2, JB])
                pexp = sb(ctx, "pexp", [P, 2, 2, 2, JB])
                LM = sb(ctx, "LM", [P, JB, 2, 2, 4, P])
                Lf = sb(ctx, "Lf", [P, JB, 2, 2, P])
                X = sb(ctx, "X", [P, JB, 2, 2, P])
                XT = sb(ctx, "XT", [P, JB, 2, 2, P])
                TT = sb(ctx, "TT", [P, JB, 2, 2, P])
                rhs = TT[:, 0:2].rearrange("p a h d t -> p a (h d t)")
                SA = TT[:, 2:4].rearrange("p a h d t -> p a (h d t)")
                osb = Lf[:, 0:2].rearrange("p a h d t -> p (a h d t)").rearrange("p (d j t) -> p d j t", d=2, j=JB)
                ST = sb(ctx, "ST", [P, 2, JB, 64])
                reset = sb(ctx, "reset", [P, JB, P])
                evmask = sb(ctx, "evmask", [P, 2, 4, P])
                invmask = sb(ctx, "invmask", [P, N_LEVELS + 1, 2, P])
                names = ("cum_ready", "exp_ready", "prepared", "transposed", "tok_ready", "products", "masked",
                         "lower_done", "lower_masked", "ident_added", "first_level", "t_done", "t_ready", "x_done",
                         "x_ready", "xt_done", "xt_ready", "rhs_done", "rhs_ready", "sa_done", "sa_ready", "o_done",
                         "u_done", "u_used", "st_ready")
                S = {n: sem(n).h for n in names}
                scan_stored, scan_in_sem = stored[0], slot_in[0]
                kab = v("k_a", 0, 4).unsqueeze(2).to_broadcast([P, JB, P])

                def all_turns(fori, body):
                    for g in range(CTX_TURNS):
                        body(g, g % 2, None)
                    with fori(MAIN_TURNS // 2 - 1) as i2:
                        for s in range(2):
                            body(i2 * 2 + (CTX_TURNS + s), s, i2 * 2 + s)
                    for g in (LAST - 1, LAST):
                        body(g, g % 2, g - CTX_TURNS)

                with nc.Block("scan") as block:
                    @block.sync
                    def _(sp):
                        sp.dma_start(reset[:, :, :], A["reset"]).then_inc(loaded.h, 16)
                        sp.dma_start(evmask[:, :, :, :], A["evmask"]).then_inc(loaded.h, 16)
                        sp.dma_start(invmask[:, :, :, :], A["invmask"]).then_inc(loaded.h, 16)
                        flat_in = scan_in[:].rearrange("a j p t -> p (a j) t")
                        to = tin[:, :].rearrange("p f j t -> p (f j) t")

                        def load_turn(fwd, bwd):
                            for lo, hi, at, t in ((0, 6, 0, fwd), (6, 10, 0, bwd), (10, 12, 6, bwd)):
                                sp.dma_start(to[:, lo * JB:hi * JB, :],
                                             flat_in[:, at * JB:(at + hi - lo) * JB, bass.ds(t, P)])\
                                    .then_inc(scan_in_sem.h, 16)

                        load_turn(CTX_AT, CTX_AT + P)
                        sp.wait_ge(S["transposed"], 6)
                        load_turn(CTX_AT + P, CTX_AT)
                        with sp.Fori(0, MAIN_TURNS // 2) as i2:
                            for s in range(2):
                                sp.wait_ge(S["transposed"], i2 * 12 + 6 * (CTX_TURNS + s))
                                load_turn(i2 * 256 + s * P, i2 * -256 + (SEQ - P - s * P))

                    @block.vector
                    def _(dve):
                        link = Link(dve, dve_step)
                        link(nc.vector.memset(ST[:, :, :, :], 0.0))
                        dve.wait_ge(loaded.h, loaded.base + 48)
                        r, k_, vv, kk, ld, aa = range(6)

                        def prepare(g, p):
                            dve.wait_ge(scan_in_sem.h, g * LOADS + (scan_in_sem.base + LOADS))
                            for d in range(2):
                                f = lambda q: tin[:, 6 * d + q]
                                c, ce = cum[:, d], cex[:, d]
                                link(nc.vector.tensor_tensor_scan(
                                    c.rearrange("p j t -> p (j t)"), reset[:, :, :].rearrange("p j t -> p (j t)"),
                                    f(ld).rearrange("p j t -> p (j t)"), 0.0, ALU.mult, ALU.add))
                                yield
                                if d == 0:
                                    link(nc.vector.tensor_copy(plog[:, d, 0, :], c[:, :, 63:64].squeeze(2)))
                                    link(nc.vector.tensor_tensor(c, c, plog[:, d, 0, :].unsqueeze(2).to_broadcast(
                                        [P, JB, P]), ALU.subtract))
                                    link(nc.vector.tensor_copy(plog[:, d, 1, :], c[:, :, 127:128].squeeze(2)))
                                else:
                                    link(nc.vector.tensor_tensor(ce, c, f(ld), ALU.subtract))
                                    link(nc.vector.tensor_copy(plog[:, d, 1, :], ce[:, :, 64:65].squeeze(2)))
                                    yield
                                    link(nc.vector.tensor_tensor(plog[:, d, 0, :], c[:, :, 127:128].squeeze(2),
                                                                 plog[:, d, 1, :], ALU.subtract))
                                    link(nc.vector.tensor_tensor(c, plog[:, d, 1, :].unsqueeze(2).to_broadcast(
                                        [P, JB, P]), ce, ALU.subtract))
                                yield
                                nc.vector.tensor_tensor(ce, c, f(ld), ALU.subtract).then_inc(S["cum_ready"], 1)
                                yield
                                kc, bc = Kc[:, p, d], Bc[:, p, d]
                                link(nc.vector.scalar_tensor_tensor(kc, f(aa), -1.0, kab, ALU.add, ALU.mult))
                                yield
                                link(nc.vector.scalar_tensor_tensor(kc, kc, 1.0, f(k_), ALU.add, ALU.mult))
                                link(nc.vector.tensor_tensor(bc, f(kk), f(aa), ALU.mult))
                                yield
                            for d in range(2):
                                f = lambda q: tin[:, 6 * d + q]
                                dve.wait_ge(S["exp_ready"], g * 2 + (d + 1))
                                kc, bc = Kc[:, p, d], Bc[:, p, d]
                                nc.vector.tensor_tensor(kc, kc, cum[:, d], ALU.mult)
                                yield
                                nc.vector.tensor_tensor(bc, bc, cum[:, d], ALU.mult)
                                nc.vector.scalar_tensor_tensor(AR[:, p, d, :, 0, :], f(kk), -1.0, E1[:, d], ALU.mult,
                                                               ALU.mult)
                                yield
                                nc.vector.tensor_tensor(AR[:, p, d, :, 1, :], f(r), cex[:, d], ALU.mult)\
                                    .then_inc(S["prepared"], 1)
                                yield

                        def scale_state(p):
                            st = ST[:, :, :, :]
                            nc.vector.tensor_tensor(st, st, pexp[:, p, :, 0, :].unsqueeze(3).to_broadcast(
                                [P, 2, JB, 64]), ALU.mult).then_inc(S["st_ready"], 1)

                        for _ in prepare(0, 0):
                            pass
                        scale_state(0)

                        def body(g, p, out):
                            last = isinstance(g, int) and g == LAST
                            steps = iter(()) if last else prepare(g + 1, 1 - p)

                            def first_level(j):
                                dve.wait_ge(S["ident_added"], g * JB + (j + 1))
                                m, mT_ = [invmask[:, q].unsqueeze(1).to_broadcast([P, 2, 2, P]) for q in (0, N_LEVELS)]
                                nc.vector.tensor_tensor(X[:, j], Lf[:, j], m, ALU.mult)
                                nc.vector.tensor_tensor(XT[:, j], LM[:, j, :, :, 0, :], mT_, ALU.mult)\
                                    .then_inc(S["first_level"], 1)

                            if out is not None and not (isinstance(out, int) and out == 0):
                                dve.wait_ge(scan_stored.h, out * 32 + scan_stored.base)
                            for j in range(JB):
                                for h in range(2):
                                    for d in range(2):
                                        u = (j * 2 + h) * 2 + d
                                        dve.wait_ge(S["products"], g * 16 + (u + 1))
                                        nc.vector.tensor_tensor(LM[:, j, h, d].rearrange("p q t -> p (q t)"),
                                                                bank(h * 2 + d),
                                                                evmask[:, d].rearrange("p q t -> p (q t)"), ALU.mult)\
                                            .then_inc(S["masked"], 1)
                                dve.wait_ge(S["lower_done"], g * JB + (j + 1))
                                for h in range(2):
                                    for d in range(2):
                                        ins = nc.vector.tensor_tensor(Lf[:, j, h, d], bank(4 + h + 2 * (j % 2), P, d * P),
                                                                      evmask[:, 1 - d, 0], ALU.mult)
                                ins.then_inc(S["lower_masked"], 1)
                                if j:
                                    first_level(j - 1)
                            first_level(JB - 1)
                            for lv in range(1, N_LEVELS):
                                for j in range(JB):
                                    dve.wait_ge(S["t_done"], g * N_T + (4 * (lv - 1) + j + 1))
                                    m = invmask[:, lv].unsqueeze(1).to_broadcast([P, 2, 2, P])
                                    nc.vector.tensor_tensor(TT[:, j], bank(j).rearrange("p (h d t) -> p h d t", h=2, d=2),
                                                            m, ALU.mult).then_inc(S["t_ready"], 1)
                                    next(steps, None)
                            for _ in steps:
                                pass
                            dve.wait_ge(S["sa_done"], g * 2 + 2)
                            nc.vector.tensor_copy(SA, PS[:, 2 * 512:4 * 512].rearrange("p (h c) -> p h c", h=2))\
                                .then_inc(S["sa_ready"], 1)
                            if last:
                                return
                            dve.wait_ge(S["u_done"], g + 1)
                            st = ST[:, :, :, :].rearrange("p d j v -> p (d j v)")
                            nc.vector.tensor_tensor(st, st, bank(0), ALU.add).then_inc(S["u_used"], 1)
                            dve.wait_ge(S["u_used"], g + 1)
                            st = ST[:, :, :, :]
                            link(nc.vector.tensor_tensor(st, st, pexp[:, p, :, 1, :].unsqueeze(3).to_broadcast(
                                [P, 2, JB, 64]), ALU.mult))
                            scale_state(1 - p)

                        all_turns(lambda n: link.fori(n, 2 * LINKS), body)
                        link.end()

                    @block.scalar
                    def _(act):
                        link = Link(act, act_step)

                        def exponentials(g, p, d):
                            act.wait_ge(S["cum_ready"], g * 2 + (d + 1))
                            link(nc.scalar.activation(E1[:, d], cex[:, d], ACT.Exp))
                            yield
                            link(nc.scalar.activation(cex[:, d], cum[:, d], ACT.Exp))
                            yield
                            nc.scalar.activation(cum[:, d], cum[:, d], ACT.Exp, scale=-1.0)
                            yield
                            nc.scalar.activation(pexp[:, p, d], plog[:, d], ACT.Exp).then_inc(S["exp_ready"], 1)

                        for d in range(2):
                            for _ in exponentials(0, 0, d):
                                pass

                        def body(g, p, out):
                            last = isinstance(g, int) and g == LAST
                            for m in range(6):
                                act.wait_ge(S["transposed"], g * 6 + (m + 1))
                                nc.scalar.activation(tok[:, m % 3, m // 3].rearrange("p j t -> p (j t)"),
                                                     bank(TOK_BANKS[m]), ACT.Copy).then_inc(S["tok_ready"], 1)
                            steps = [] if last else [exponentials(g + 1, 1 - p, d) for d in range(2)]

                            def move(dst, b, done, ready, n):
                                act.wait_ge(S[done], n)
                                nc.scalar.activation(dst.rearrange("p h d t -> p (h d t)"), bank(b), ACT.Copy)\
                                    .then_inc(S[ready], 1)

                            for lv in range(1, N_LEVELS):
                                for j in range(JB):
                                    n = 4 * (lv - 1) + j
                                    final = lv == N_LEVELS - 1
                                    move((XT if final else X)[:, j], 4 + j % 2, "x_done", "x_ready", g * N_X + (n + 1))
                                    if j and not final:
                                        move(XT[:, j - 1], 6 + (j - 1) % 2, "xt_done", "xt_ready", g * N_XT + n)
                                    if steps and lv in (2, 3):
                                        next(steps[lv - 2], None)
                                if not final:
                                    move(XT[:, JB - 1], 6 + (JB - 1) % 2, "xt_done", "xt_ready", g * N_XT + 4 * lv)
                            act.wait_ge(S["rhs_done"], g + 1)
                            nc.scalar.activation(rhs, PS[:, 0:1024].rearrange("p (h c) -> p h c", h=2), ACT.Copy)\
                                .then_inc(S["rhs_ready"], 1)
                            if out is None:
                                return
                            for h in range(2):
                                for d in range(2):
                                    act.wait_ge(S["o_done"], out * 4 + (h * 2 + d + 1))
                                    hp = slice(h * 64, h * 64 + 64)
                                    nc.scalar.activation(osb[hp, d].rearrange("p j t -> p (j t)"),
                                                         PS[hp, (4 + h * 2 + d) * 512:(5 + h * 2 + d) * 512],
                                                         ACT.Copy).then_inc(o_ready.h, 1)
                            act.wait_ge(o_ready.h, o_ready.base + out * 4 + 4)
                            for d in range(2):
                                t = out * P if d == 0 else out * -P + (SEQ - P)
                                act.dma_start(scan_out[d][:, :, bass.ds(t, P)], osb[:, d]).then_inc(scan_stored.h, 16)

                        all_turns(lambda n: link.fori(n, 2 * 4), body)
                        link.end()
                        act.wait_ge(scan_stored.h, scan_stored.base + 32 * MAIN_TURNS)

                    @block.gpsimd
                    def _(pool):
                        def body(g, p, out):
                            for j in range(JB):
                                pool.wait_ge(S["masked"], g * 16 + (4 * j + 4))
                                pool.wait_ge(S["lower_masked"], g * 4 + (j + 1))
                                idt = ident[:, :].unsqueeze(1).to_broadcast([P, 4, P])
                                for x in (LM[:, j, :, :, 0, :].rearrange("p h d t -> p (h d) t"),
                                          Lf[:, j].rearrange("p h d t -> p (h d) t")):
                                    last = nc.gpsimd.tensor_tensor(x, x, idt, ALU.add)
                                last.then_inc(S["ident_added"], 1)

                        all_turns(lambda n: pool.Fori(0, n), body)

                    @block.tensor
                    def _(pe):
                        def body(g, p, out):
                            last_turn = isinstance(g, int) and g == LAST
                            first_turn = isinstance(g, int) and g == 0
                            for d in range(2):
                                pe.wait_ge(S["prepared"], g * 2 + (d + 1))
                                for m, src in enumerate((Bc[:, p, d], Kc[:, p, d], tin[:, 6 * d + 2])):
                                    if d == 1 and m == 0 and out is not None:
                                        pe.wait_ge(o_ready.h, o_ready.base + out * 4)
                                    for j in range(JB):
                                        last = nc.tensor.transpose(bank(TOK_BANKS[d * 3 + m], P, j * P), src[:, j, :],
                                                                   ident[:, :])
                                    last.then_inc(S["transposed"], 1)
                            if not first_turn:
                                pe.wait_ge(S["u_used"], g)
                            for j in range(JB):
                                for h in range(2):
                                    hp = slice(h * 64, h * 64 + 64)
                                    for d in range(2):
                                        b = h * 2 + d
                                        if j:
                                            pe.wait_ge(S["masked"], g * 16 + (4 * (j - 1) + b + 1))
                                        elif b:
                                            pe.wait_ge(S["tok_ready"], g * 6 + b)
                                        ar = AR[hp, p, d, j].rearrange("p q t -> p (q t)")
                                        nc.tensor.matmul(bank(b, 256), Bc[hp, p, d, j], ar, start=True, stop=True)
                                        nc.tensor.matmul(bank(b, 256, 256), Kc[hp, p, d, j], ar, start=True, stop=True)\
                                            .then_inc(S["products"], 1)
                                if j == 0:
                                    pe.wait_ge(S["tok_ready"], g * 6 + 6)
                                if j >= 2:
                                    pe.wait_ge(S["lower_masked"], g * 4 + (j - 1))
                                for h in range(2):
                                    hp = slice(h * 64, h * 64 + 64)
                                    for d in range(2):
                                        last = nc.tensor.matmul(bank(4 + h + 2 * (j % 2), P, d * P), AR[hp, p, d, j, 0],
                                                                Bc[hp, p, d, j], start=True, stop=True)
                                last.then_inc(S["lower_done"], 1)

                            def units(bank_at, lhsT, rhs_, name):
                                for h in range(2):
                                    for d in range(2):
                                        last = nc.tensor.matmul(bank(bank_at, P, (h * 2 + d) * P), lhsT[:, h, d],
                                                                rhs_[:, h, d], start=True, stop=True)
                                last.then_inc(S[name], 1)

                            def t_product(lv, j):
                                if lv == 1:
                                    pe.wait_ge(S["first_level"], g * 4 + (j + 1))
                                    if j == 0:
                                        pe.wait_ge(S["masked"], g * 16 + 16)
                                else:
                                    pe.wait_ge(S["x_ready"], g * N_X + (4 * (lv - 2) + j + 1))
                                units(j, LM[:, j, :, :, 0, :], X[:, j], "t_done")

                            def x_product(lv, j):
                                pe.wait_ge(S["t_ready"], g * N_T + (4 * (lv - 1) + j + 1))
                                n = 4 * (lv - 1) + j
                                if n >= 2:
                                    pe.wait_ge(S["x_ready"], g * N_X + (n - 1))
                                elif n == 0:
                                    pe.wait_ge(S["lower_masked"], g * 4 + 4)
                                if lv > 1:
                                    pe.wait_ge(S["xt_ready"], g * N_XT + (4 * (lv - 2) + j + 1))
                                if lv == N_LEVELS - 1:
                                    units(4 + j % 2, TT[:, j], XT[:, j], "x_done")
                                else:
                                    units(4 + j % 2, XT[:, j], TT[:, j], "x_done")

                            def x_transpose(lv, j):
                                pe.wait_ge(S["x_ready"], g * N_X + (4 * (lv - 1) + j + 1))
                                n = 4 * (lv - 1) + j
                                if n >= 2:
                                    pe.wait_ge(S["xt_ready"], g * N_XT + (n - 1))
                                for h in range(2):
                                    for d in range(2):
                                        last = nc.tensor.transpose(bank(6 + j % 2, P, (h * 2 + d) * P), X[:, j, h, d],
                                                                   ident[:, :])
                                last.then_inc(S["xt_done"], 1)

                            for j in range(JB):
                                t_product(1, j)
                            for lv in range(1, N_LEVELS):
                                final = lv == N_LEVELS - 1
                                x_product(lv, 0)
                                for j in range(1, JB):
                                    x_product(lv, j)
                                    if not final:
                                        x_transpose(lv, j - 1)
                                if not final:
                                    t_product(lv + 1, 0)
                                    x_transpose(lv, JB - 1)
                                    for j in range(1, JB):
                                        t_product(lv + 1, j)
                            pe.wait_ge(S["st_ready"], g + 1)
                            for h in range(2):
                                hp = slice(h * 64, h * 64 + 64)
                                for d in range(2):
                                    for j in range(JB):
                                        o = bank(h, 64, (d * JB + j) * 64)
                                        nc.tensor.matmul(o, AR[hp, p, d, j, 0], ST[hp, d, j], start=True, stop=False)
                                        last = nc.tensor.matmul(o, LM[:, j, h, d, 2], tok[:, 2, d, j, hp], start=False,
                                                                stop=True)
                            last.then_inc(S["rhs_done"], 1)
                            pe.wait_ge(S["x_ready"], g * N_X + N_X)
                            pe.wait_ge(S["rhs_ready"], g + 1)
                            for h in range(2):
                                for d in range(2):
                                    for j in range(JB):
                                        at = (d * JB + j) * 64
                                        last = nc.tensor.matmul(bank(2 + h, 64, at), XT[:, j, h, d],
                                                                rhs[:, h, at:at + 64], start=True, stop=True)
                                last.then_inc(S["sa_done"], 1)
                            pe.wait_ge(S["sa_ready"], g + 1)
                            for h in range(2):
                                hp = slice(h * 64, h * 64 + 64)
                                for d in range(2):
                                    if out is None:
                                        continue
                                    for j in range(JB):
                                        at = (d * JB + j) * 64
                                        o = PS[hp, (4 + h * 2 + d) * 512 + j * P:(4 + h * 2 + d) * 512 + j * P + P]
                                        nc.tensor.matmul(o, SA[:, h, at:at + 64], LM[:, j, h, d, 1], start=True,
                                                         stop=False)
                                        nc.tensor.matmul(o, ST[hp, d, j], AR[hp, p, d, j, 1], start=False, stop=False)
                                        last = nc.tensor.matmul(o, tok[:, 2, d, j, hp], LM[:, j, h, d, 3],
                                                                start=False, stop=True)
                                    last.then_inc(S["o_done"], 1)
                            if last_turn:
                                return
                            for h in range(2):
                                hp = slice(h * 64, h * 64 + 64)
                                for d in range(2):
                                    for j in range(JB):
                                        at = (d * JB + j) * 64
                                        o = PS[hp, at:at + 64]
                                        nc.tensor.matmul(o, tok[:, 0, d, j, hp], SA[:, h, at:at + 64], start=True,
                                                         stop=False)
                                        last = nc.tensor.matmul(o, tok[:, 1, d, j, hp], tok[:, 2, d, j, hp],
                                                                start=False, stop=True)
                            last.then_inc(S["u_done"], 1)

                        all_turns(lambda n: pe.Fori(0, n), body)
            loaded.base += 48
            slot_in[0].base += LOADS * (LAST + 1)
            stored[0].base += 32 * MAIN_TURNS
            o_ready.base += 4 * MAIN_TURNS

        def rwkv_out_stage(yT):
            OF, OB, R, K, V, A0, A1, G, Z = range(9)
            ZC_AT = 16
            with ExitStack() as ctx:
                tin = sb(ctx, "ro_tin", [P, 2, 9, SEQ])
                o = sb(ctx, "ro_o", [P, SEQ])
                mean = sb(ctx, "ro_mean", [P, SEQ])
                sq = sb(ctx, "ro_sq", [P, SEQ])
                std = sb(ctx, "ro_std", [P, SEQ])
                bon = sb(ctx, "ro_bon", [P, SEQ])
                sz = sb(ctx, "ro_silu", [P, SEQ])
                with nc.Block("rwkv_out") as block:
                    @block.sync
                    def _(sp):
                        for j in range(JB):
                            s = j % 2
                            if j >= 2:
                                sp.wait_ge(slot_free[s].h, slot_free[s].base + 1)
                            srcs = [scan_out[0][:, j], scan_out[1][:, j]]
                            srcs += [scan_in[a, j][:, 0:SEQ] for a in (S_R, S_K, S_V, S_A0, S_A1)]
                            srcs += [gate_o[j][:, 0:SEQ], proj_o[ZC_AT + j][:, 0:SEQ]]
                            for n, src in enumerate(srcs):
                                sp.dma_start(tin[:, s, n], src).then_inc(slot_in[s].h, 16)

                    @block.tensor
                    def _(pe):
                        def head_sums(b, x):
                            for c in range(2):
                                last = nc.tensor.matmul(bank(b + c), head_ones[:, :], x[:, c * 512:(c + 1) * 512],
                                                        start=True, stop=True)
                            last.then_inc(sum_done.h, 1)

                        for j in range(JB):
                            pe.wait_ge(norm_done.h, norm_done.base + 3 * j + 1)
                            head_sums(0, o)
                            pe.wait_ge(norm_done.h, norm_done.base + 3 * j + 2)
                            head_sums(4, bon)
                            pe.wait_ge(sq_done.h, sq_done.base + j + 1)
                            head_sums(2, sq)

                    @block.vector
                    def _(dve):
                        link = Link(dve, dve_step)
                        for j in range(JB):
                            s = j % 2
                            f = lambda q: tin[:, s, q]
                            dve.wait_ge(slot_in[s].h, slot_in[s].base + 16 * 9 * (j // 2 + 1))
                            nc.vector.tensor_tensor(o[:, :], f(OF), f(OB), ALU.add).then_inc(norm_done.h, 1)
                            link(nc.vector.tensor_tensor(bon[:, :], f(A0), f(A1), ALU.add))
                            link(nc.vector.tensor_scalar(bon[:, :], bon[:, :], -2.0, v("k_a", j), ALU.add, ALU.mult))
                            link(nc.vector.scalar_tensor_tensor(bon[:, :], bon[:, :], 2.0, f(K), ALU.add, ALU.mult))
                            nc.vector.scalar_tensor_tensor(bon[:, :], bon[:, :], v("r_k", j), f(R), ALU.mult,
                                                           ALU.mult).then_inc(norm_done.h, 1)
                            dve.wait_ge(sum_done.h, sum_done.base + 3 * j + 1)
                            link(nc.vector.tensor_scalar(mean[:, :], PS[:, 0:SEQ], 1.0 / 64, None, ALU.mult))
                            nc.vector.tensor_tensor(o[:, :], o[:, :], mean[:, :], ALU.subtract)\
                                .then_inc(norm_done.h, 1)
                            dve.wait_ge(std_done.h, std_done.base + 2 * j + 2)
                            link(nc.vector.reciprocal(std[:, :], std[:, :]))
                            link(nc.vector.tensor_tensor(o[:, :], o[:, :], std[:, :], ALU.mult))
                            link(nc.vector.tensor_scalar(o[:, :], o[:, :], v("lnx_g", j), v("lnx_b", j), ALU.mult,
                                                         ALU.add))
                            link(nc.vector.tensor_tensor(bon[:, :], PS[:, 4 * 512:6 * 512], f(V), ALU.mult))
                            link(nc.vector.tensor_tensor(o[:, :], o[:, :], bon[:, :], ALU.add))
                            link(nc.vector.tensor_tensor(o[:, :], o[:, :], f(G), ALU.mult))
                            nc.vector.tensor_tensor(yT[:, j, 0:SEQ], o[:, :], sz[:, :], ALU.mult)\
                                .then_inc(evacuated[0].h, 1)
                            dve.wait_ge(evacuated[0].h, evacuated[0].base + j + 1)
                            dve.sem_inc(slot_free[s].h, 1)
                        link.end()

                    @block.scalar
                    def _(act):
                        for j in range(JB):
                            s = j % 2
                            act.wait_ge(slot_in[s].h, slot_in[s].base + 16 * 9 * (j // 2 + 1))
                            if j:
                                act.wait_ge(evacuated[0].h, evacuated[0].base + j)
                            nc.scalar.activation(sz[:, :], tin[:, s, Z], ACT.Silu).then_inc(std_done.h, 1)
                            act.wait_ge(norm_done.h, norm_done.base + 3 * j + 3)
                            nc.scalar.activation(sq[:, :], o[:, :], ACT.Square).then_inc(sq_done.h, 1)
                            act.wait_ge(sum_done.h, sum_done.base + 3 * j + 3)
                            nc.scalar.activation(std[:, :], PS[:, 1024:2048], ACT.Sqrt, scale=1.0 / 64,
                                                 bias=eps_col(64e-5)).then_inc(std_done.h, 1)
            for s in range(2):
                slot_in[s].base += 16 * 9 * 2
                slot_free[s].base += 2
            norm_done.base += 3 * JB
            sum_done.base += 3 * JB
            std_done.base += 2 * JB
            sq_done.base += JB
            evacuated[0].base += JB

        def conformer_conv_stage(cv):
            P1_AT, P2_AT = 20, 24
            HALF = 15
            with ExitStack() as ctx:
                tin = sb(ctx, "cf_tin", [P, 2, 2, SEQ])
                hg = sb(ctx, "cf_h", [P, 2, SEQ])
                with nc.Block("conformer_conv") as block:
                    @block.sync
                    def _(sp):
                        for j in range(JB):
                            s = j % 2
                            if j >= 2:
                                sp.wait_ge(gated[0].h, gated[0].base + j - 1)
                            for n, at in enumerate((P1_AT, P2_AT)):
                                sp.dma_start(tin[:, s, n], proj_o[at + j][:, 0:SEQ]).then_inc(slot_in[s].h, 16)

                    @block.scalar
                    def _(act):
                        for j in range(JB):
                            s = j % 2
                            act.wait_ge(slot_in[s].h, slot_in[s].base + 32 * (j // 2 + 1))
                            nc.scalar.activation(tin[:, s, 1], tin[:, s, 1], ACT.Sigmoid).then_inc(sq_done.h, 1)

                    @block.vector
                    def _(dve):
                        link = Link(dve, dve_step)
                        for j in range(JB):
                            s = j % 2
                            dve.wait_ge(slot_in[s].h, slot_in[s].base + 32 * (j // 2 + 1))
                            dve.wait_ge(sq_done.h, sq_done.base + j + 1)
                            h = hg[:, s]
                            nc.vector.tensor_tensor(h, tin[:, s, 0], tin[:, s, 1], ALU.mult).then_inc(gated[0].h, 1)
                            dve.wait_ge(gated[0].h, gated[0].base + j + 1)
                            link(nc.vector.tensor_scalar(cv[:, j, :], h, v("conf_dw_w", 4 * HALF + j), v("conf_dw_b", j),
                                                         ALU.mult, ALU.add))
                            for tap in range(2 * HALF + 1):
                                d = (tap - HALF) * LINE
                                if d == 0:
                                    continue
                                w = SEQ - abs(d)
                                o = cv[:, j, max(0, -d):max(0, -d) + w]
                                link(nc.vector.scalar_tensor_tensor(o, h[:, max(0, d):max(0, d) + w],
                                                                    v("conf_dw_w", 4 * tap + j), o, ALU.mult, ALU.add))
                        link.end()
            for s in range(2):
                slot_in[s].base += 32 * 2
            gated[0].base += JB
            sq_done.base += JB

        def conformer_gate_stage(cv, yT):
            ZD_AT = 28
            with ExitStack() as ctx:
                zd = sb(ctx, "zd", [P, JB, SEQ])
                with nc.Block("conformer_gate") as block:
                    @block.sync
                    def _(sp):
                        sp.dma_start(zd[:, :, :], proj_o[ZD_AT:ZD_AT + JB].rearrange("j p t -> p j t")[:, :, 0:SEQ])\
                            .then_inc(loaded.h, 16)

                    @block.scalar
                    def _(act):
                        nc.scalar.activation(cv[:, :, :], cv[:, :, :], ACT.Silu).then_inc(act_step.h, 1)
                        act.wait_ge(loaded.h, loaded.base + 16)
                        nc.scalar.activation(zd[:, :, :], zd[:, :, :], ACT.Silu).then_inc(act_step.h, 1)

                    @block.vector
                    def _(dve):
                        dve.wait_ge(act_step.h, act_step.base + 2)
                        nc.vector.tensor_tensor(yT[:, JB:2 * JB, 0:SEQ], cv[:, :, :], zd[:, :, :], ALU.mult)\
                            .then_inc(dve_step.h, 1)
            act_step.base += 2
            dve_step.base += 1
            loaded.base += 16

        def ffn_stage(name, w_up, w_down):
            PIECES = [(0, 8), (8, 8), (16, 6)]
            gate = [xT[:, 4 * b:4 * b + 4, SEQ:T] for b in range(2)]
            with ExitStack() as ctx:
                x = Parts(ctx, f"{name}_x", KD, SEQ)
                hid = Parts(ctx, f"{name}_hid", 8, SEQ)
                for p, (first, n_hid) in enumerate(PIECES):
                    with ExitStack() as up:
                        ring = Weights(up, f"{name}_up{p}", KD)
                        cut_act, cut_dve = cut_parts(name, xT, x, KD, MAIN_CHUNKS)
                        cut = p == 0
                        hv = lambda part, n: part[:, n, :].rearrange("p (a t) -> p a t", a=4)
                        with nc.Block(f"{name}_up{p}") as block:
                            @block.sync
                            def _(sp):
                                with sp.Fori(0, n_hid) as i:
                                    for s in range(2):
                                        ring.load(sp, i, s, w_up[i * 2 + (2 * first + s)])

                            @block.tensor
                            def _(pe):
                                with pe.Fori(0, n_hid // 2) as i:
                                    for b in range(2):
                                        for s in range(2):
                                            pe.wait_ge(w_low[s].h, w_low[s].base + i * 2 + (b + 1))
                                            if s == 0:
                                                pe.wait_ge(evacuated[b].h, evacuated[b].base + i)
                                            for c, (t, w) in enumerate(MAIN_CHUNKS):
                                                if cut and b == s == 0:
                                                    pe.wait_ge(parts_ready.h, parts_ready.base + c + 1)
                                                at = b * 2048 + s * 1024 + t
                                                last = ring.product(pe, PS[:, at:at + w], s, x, 0, KD, t, w)
                                            last.then_inc(tile_done[s].h, 1)

                            @block.scalar
                            def _(act):
                                def prepare(i, q, s, n):
                                    ring.cut_high(act, n, s)
                                    if cut and isinstance(i, int) and i == q == 0:
                                        cut_act(act)

                                def finish(i, q, s, n):
                                    b = q // 2
                                    if s == 0:
                                        act.wait_ge(tile_done[0].h, tile_done[0].base + n + 1)
                                        act.wait_ge(stored[b].h, stored[b].base + i)
                                        nc.scalar.activation(gate[b], PS[:, b * 2048:b * 2048 + SEQ].rearrange(
                                            "p (a t) -> p a t", a=4), ACT.Silu).then_inc(gated[b].h, 1)
                                    else:
                                        act.wait_ge(evacuated[b].h, evacuated[b].base + i + 1)
                                        high_part(hv(hid.high, i * 2 + b), gate[b]).then_inc(high_ready.h, 1)
                                ahead(act, 2 * n_hid, 4, prepare, finish)

                            @block.vector
                            def _(dve):
                                def prepare(i, q, s, n):
                                    ring.cut_low(dve, n, s)
                                    if cut and isinstance(i, int) and i == q == 0:
                                        cut_dve(dve)

                                def finish(i, q, s, n):
                                    if s == 0:
                                        return
                                    b = q // 2
                                    dve.wait_ge(gated[b].h, gated[b].base + i + 1)
                                    dve.wait_ge(tile_done[1].h, tile_done[1].base + n + 1)
                                    nc.vector.scalar_tensor_tensor(
                                        gate[b], gate[b], 0.5, PS[:, b * 2048 + 1024:b * 2048 + 2048].rearrange(
                                            "p (a t) -> p a t", a=4), ALU.mult, ALU.mult).then_inc(evacuated[b].h, 1)
                                    h0 = high_ready.base + (len(MAIN_CHUNKS) if cut else 0)
                                    dve.wait_ge(high_ready.h, i * 2 + (h0 + b + 1))
                                    low_part(hv(hid.low, i * 2 + b), gate[b], hv(hid.high, i * 2 + b))\
                                        .then_inc(stored[b].h, 1)
                                ahead(dve, 2 * n_hid, 4, prepare, finish)
                        for s in range(2):
                            w_loaded[s].base += 16 * n_hid
                            for q in (w_high, w_low, tile_done):
                                q[s].base += n_hid
                            for q in (evacuated, gated, stored):
                                q[s].base += n_hid // 2
                        high_ready.base += n_hid
                        if cut:
                            high_ready.base += len(MAIN_CHUNKS)
                            parts_ready.base += len(MAIN_CHUNKS)
                    product_stage(f"{name}_down{p}", lambda m: w_down[m][:, first:first + n_hid, :], KD, n_hid, None, hid,
                                  MAIN_CHUNKS,
                                  lambda m, s: deepnorm_update(m, s * 1536, ALPHA if p == 0 else 1.0))

        def gmlp_stage(mT):
            with ExitStack() as ctx:
                z = sb(ctx, "gz", [P, 8, SEQ])
                ws = sb(ctx, "gws", [P, 8, P])
                bs = sb(ctx, "gbs", [1, 8, P])
                tri = sb(ctx, "tri", [P, P])
                vt = sb(ctx, "vt", [P, 2, DB])
                with nc.Block("gmlp_gelu") as block:
                    @block.sync
                    def _(sp):
                        sp.dma_start(z[:, :, :], proj_2[8:16].rearrange("n p t -> p n t")).then_inc(loaded.h, 16)
                        sp.dma_start(ws[:, :, :], A["gmlp_ws"]).then_inc(loaded.h, 16)
                        sp.dma_start(bs[:, :, :], A["gmlp_bs"]).then_inc(loaded.h, 16)
                        sp.dma_start(tri[:, :], A["tri"]).then_inc(loaded.h, 16)

                    @block.scalar
                    def _(act):
                        act.wait_ge(loaded.h, loaded.base + 64)
                        nc.scalar.activation(z[:, :, :].rearrange("p n t -> p (n t)"),
                                             z[:, :, :].rearrange("p n t -> p (n t)"), ACT.Gelu_apprx_tanh)\
                            .then_inc(act_step.h, 1)

                    @block.vector
                    def _(dve):
                        dve.wait_ge(loaded.h, loaded.base + 64)
                        nc.vector.tensor_tensor(ws[:, :, :], ws[:, :, :], tri[:, :].unsqueeze(1).to_broadcast([P, 8, P]),
                                                ALU.mult).then_inc(dve_step.h, 1)
                act_step.base += 1
                dve_step.base += 1
                loaded.base += 64
                zv = z[:, 4:8, :]
                norm_stage("gmlp_ln", zv, zv, MAIN_CHUNKS, 4, 1e-5, True, lambda k, c: v("gmlp_ln_g_2", k),
                           lambda k, c: v("gmlp_ln_b_2", k))
                with nc.Block("gmlp_mix") as block:
                    @block.tensor
                    def _(pe):
                        for n in range(SEQ // P):
                            s = n % 2
                            if n >= 2:
                                pe.wait_ge(act_step.h, act_step.base + n - 1)
                            for k in range(4):
                                last = nc.tensor.transpose(bank(s, P, k * P), z[:, 4 + k, n * P:n * P + P], ident[:, :])
                            last.then_inc(tile_done[0].h, 1)
                            pe.wait_ge(act_step.h, act_step.base + n + 1)
                            if n >= 2:
                                pe.wait_ge(dve_step.h, dve_step.base + n - 1)
                            for g in range(8):
                                hp = slice((g % 2) * 64, (g % 2) * 64 + 64)
                                o = PS[hp, (2 + s) * 512 + (g // 2) * P:(2 + s) * 512 + (g // 2) * P + P]
                                nc.tensor.matmul(o, vt[:, s, g * 64:g * 64 + 64], ws[:, g, :], start=True, stop=False)
                                last = nc.tensor.matmul(o, ones[0:1, 0:64], bs[:, g, :], start=False, stop=True)
                            last.then_inc(tile_done[1].h, 1)

                    @block.scalar
                    def _(act):
                        for n in range(SEQ // P):
                            s = n % 2
                            act.wait_ge(tile_done[0].h, tile_done[0].base + n + 1)
                            if n >= 2:
                                act.wait_ge(tile_done[1].h, tile_done[1].base + n - 1)
                            nc.scalar.activation(vt[:, s, :], bank(s), ACT.Copy).then_inc(act_step.h, 1)

                    @block.vector
                    def _(dve):
                        for n in range(SEQ // P):
                            s = n % 2
                            dve.wait_ge(tile_done[1].h, tile_done[1].base + n + 1)
                            nc.vector.tensor_tensor(mT[:, 4:8, n * P:n * P + P], z[:, 0:4, n * P:n * P + P],
                                                    bank(2 + s).rearrange("p (k t) -> p k t", k=4), ALU.mult)\
                                .then_inc(dve_step.h, 1)
            for q in (act_step, dve_step, tile_done[0], tile_done[1]):
                q.base += SEQ // P

        def attention_stage(mT):
            NQ = SEQ // P
            NH = 8
            with ExitStack() as ctx:
                qT = sb(ctx, "qT", [P, 4, SEQ])
                cT = sb(ctx, "cT", [P, 1, SEQ])
                qi = sb(ctx, "qi", [P, 2, SEQ])
                ki = sb(ctx, "ki", [P, SEQ])
                wi = sb(ctx, "wi", [4, SEQ])
                uk = sb(ctx, "uk", [P, 4, P])
                uv = sb(ctx, "uv", [P, NH, 64])
                neg = sb(ctx, "neg", [P, P])
                one_row = sb(ctx, "one_row", [P, SEQ])
                with nc.Block("att_load") as block:
                    @block.sync
                    def _(sp):
                        sp.dma_start(qT[:, :, :], proj_2[0:4].rearrange("n p t -> p n t")).then_inc(loaded.h, 16)
                        sp.dma_start(cT[:, 0, :], proj_2[4]).then_inc(loaded.h, 16)
                        sp.dma_start(qi[:, :, :], proj_2[5:7].rearrange("n p t -> p n t")).then_inc(loaded.h, 16)
                        for h in range(2):
                            sp.dma_start(ki[h * 64:h * 64 + 64, :], proj_2[7][0:64, :]).then_inc(loaded.h, 16)
                        sp.dma_start(wi[:, :], proj_2[7][64:68, :]).then_inc(loaded.h, 16)
                        sp.dma_start(uk[:, :, :], A["w_uk"]).then_inc(loaded.h, 16)
                        sp.dma_start(uv[:, :, :], A["w_uv"]).then_inc(loaded.h, 16)
                        sp.dma_start(neg[:, :], A["neg"]).then_inc(loaded.h, 16)
                        sp.wait_ge(loaded.h, loaded.base + 16 * 9)

                    @block.vector
                    def _(dve):
                        nc.vector.memset(one_row[:, :], 1.0).then_inc(dve_step.h, 1)
                loaded.base += 16 * 9
                dve_step.base += 1
                norm_stage("kv_norm", cT, cT, MAIN_CHUNKS, 1, 1e-5, False, lambda k, c: v("kv_norm_g_2"), zero)
                qabs = sb(ctx, "qabs", [P, NH, SEQ])
                ctok = sb(ctx, "ctok", [P, NQ, P])
                wis = sb(ctx, "wis", [P, NQ, 4])
                with nc.Block("att_prepare") as block:
                    @block.tensor
                    def _(pe):
                        for h in range(NH):
                            s = h % 2
                            hp = slice(s * 64, s * 64 + 64)
                            if h >= 2:
                                pe.wait_ge(act_step.h, act_step.base + h - 1)
                            for c in range(2):
                                last = nc.tensor.matmul(bank(2 * s + c), uk[hp, h // 2, :],
                                                        qT[hp, h // 2, c * 512:c * 512 + 512], start=True, stop=True)
                            last.then_inc(tile_done[0].h, 1)
                        for n in range(NQ):
                            nc.tensor.transpose(bank(4 + n // 4, P, (n % 4) * P), cT[:, 0, n * P:n * P + P],
                                                ident[:, :])
                        for n in range(NQ):
                            last = nc.tensor.transpose(bank(6, 4, n * 4), wi[0:4, n * P:n * P + P], ident[0:4, 0:4])
                        last.then_inc(tile_done[1].h, 1)

                    @block.scalar
                    def _(act):
                        for h in range(NH):
                            act.wait_ge(tile_done[0].h, tile_done[0].base + h + 1)
                            s = h % 2
                            nc.scalar.activation(qabs[:, h, :], PS[:, s * 1024:s * 1024 + 1024], ACT.Copy, scale=0.125)\
                                .then_inc(act_step.h, 1)

                    @block.vector
                    def _(dve):
                        dve.wait_ge(tile_done[1].h, tile_done[1].base + 1)
                        nc.vector.tensor_copy(ctok[:, :, :].rearrange("p n c -> p (n c)"), PS[:, 2048:3072])
                        nc.vector.tensor_scalar(wis[:, :, :].rearrange("p n h -> p (n h)"), bank(6, 32), 0.5, None,
                                                ALU.mult).then_inc(dve_step.h, 1)
                act_step.base += NH
                dve_step.base += 1
                tile_done[0].base += NH
                tile_done[1].base += 1

                names = ("a_scored", "a_relu", "a_summed", "a_bias", "a_added", "a_exp", "a_prob", "a_transposed",
                         "a_turned", "a_inverse", "a_latent", "a_latcopy", "a_value", "a_stored")
                S = {n: sem(n).h for n in names}
                rl = qT[:, 0:2, :]
                sm = qT[:, 2:4, :]
                score = sb(ctx, "score", [P, SEQ])
                work = sb(ctx, "work", [P, SEQ])
                best = sb(ctx, "best", [P, 8])
                eq = sb(ctx, "eq", [P, SEQ])
                bias = sb(ctx, "bias", [P, 2, SEQ])
                count = sb(ctx, "count", [P, 2])
                pr = sb(ctx, "pr", [P, 2, SEQ])
                pT = sb(ctx, "pT", [P, 2, NQ, P])
                mx = sb(ctx, "mx", [P, 2])
                nmx = sb(ctx, "nmx", [P, 2])
                rs = sb(ctx, "rs", [P, 2])
                ri = sb(ctx, "ri", [P, 2])
                lat = sb(ctx, "lat", [P, 4, P])
                with nc.Block("attention") as block:
                    def pieces(width):
                        return [(c, min(512, width - c)) for c in range(0, width, 512)]

                    uses = [("index", 0, h) for h in range(4)]
                    for b in range(NQ):
                        if b + 1 < NQ:
                            uses += [("index", b + 1, h) for h in range(4)]
                        uses += [("head", b, h) for h in range(NH)]
                    place = {use: n for n, use in enumerate(uses)}

                    @block.tensor
                    def _(pe):
                        def score(use, lhsT, rhs_of, b):
                            n = place[use]
                            if n >= 2:
                                kind, b2, h2 = uses[n - 2]
                                if kind == "index":
                                    pe.wait_ge(S["a_relu"], 4 * b2 + h2 + 1)
                                else:
                                    pe.wait_ge(S["a_added"], NH * b2 + h2 + 1)
                            for c, w in pieces((b + 1) * P):
                                at = (n % 2) * 1024 + c
                                last = nc.tensor.matmul(PS[:, at:at + w], lhsT, rhs_of(c, w), start=True, stop=True)
                            last.then_inc(S["a_scored"], 1)

                        def index_scores(b):
                            for h in range(4):
                                hp = slice((h % 2) * 64, (h % 2) * 64 + 64)
                                score(("index", b, h), qi[hp, h // 2, b * P:b * P + P],
                                      lambda c, w: ki[hp, c:c + w], b)

                        def head_scores(b, h):
                            score(("head", b, h), qabs[:, h, b * P:b * P + P], lambda c, w: cT[:, 0, c:c + w], b)

                        index_scores(0)
                        for b in range(NQ):
                            if b + 1 < NQ:
                                index_scores(b + 1)
                            head_scores(b, 0)
                            for h in range(NH):
                                if h + 1 < NH:
                                    head_scores(b, h + 1)
                                n = NH * b + h
                                pe.wait_ge(S["a_prob"], n + 1)
                                if n:
                                    pe.wait_ge(S["a_turned"], n)
                                for k in range(b + 1):
                                    last = nc.tensor.transpose(PS[:, 2048 + k * P:2048 + k * P + P],
                                                               pr[:, h % 2, k * P:k * P + P], ident[:, :])
                                last.then_inc(S["a_transposed"], 1)
                                pe.wait_ge(S["a_turned"], n + 1)
                                if h % 4 == 0 and n:
                                    pe.wait_ge(S["a_latcopy"], n // 4)
                                for k in range(b + 1):
                                    last = nc.tensor.matmul(bank(6, P, (h % 4) * P), ctok[:, k, :], pT[:, h % 2, k, :],
                                                            start=k == 0, stop=k == b)
                                if h % 4 == 3:
                                    last.then_inc(S["a_latent"], 1)
                                    pe.wait_ge(S["a_latcopy"], 2 * b + h // 4 + 1)
                                    if h == 3 and b:
                                        pe.wait_ge(S["a_stored"], b)
                                    for g in range(h - 3, h + 1):
                                        hp = slice((g % 2) * 64, (g % 2) * 64 + 64)
                                        last = nc.tensor.matmul(PS[hp, 7 * 512 + (g // 2) * P:7 * 512 + (g // 2) * P + P],
                                                                uv[:, g, :], lat[:, g % 4, :], start=True, stop=True)
                                    last.then_inc(S["a_value"], 1)

                    @block.scalar
                    def _(act):
                        def relus(b):
                            width = (b + 1) * P
                            for h in range(4):
                                n = place["index", b, h]
                                act.wait_ge(S["a_scored"], n + 1)
                                if 4 * b + h >= 2:
                                    act.wait_ge(S["a_summed"], 4 * b + h - 1)
                                nc.scalar.activation(rl[:, h % 2, 0:width], PS[:, (n % 2) * 1024:(n % 2) * 1024 + width],
                                                     ACT.Relu, scale=0.125).then_inc(S["a_relu"], 1)

                        relus(0)
                        for b in range(NQ):
                            width = (b + 1) * P
                            if b + 1 < NQ:
                                relus(b + 1)

                            def normalise(h):
                                n = NH * b + h
                                act.wait_ge(S["a_inverse"], n + 1)
                                nc.scalar.activation(pr[:, h % 2, 0:width], pr[:, h % 2, 0:width], ACT.Copy,
                                                     scale=ri[:, h % 2:h % 2 + 1]).then_inc(S["a_prob"], 1)

                            def turn(h):
                                n = NH * b + h
                                act.wait_ge(S["a_transposed"], n + 1)
                                nc.scalar.activation(pT[:, h % 2, 0:b + 1, :].rearrange("p k t -> p (k t)"),
                                                     PS[:, 2048:2048 + width], ACT.Copy).then_inc(S["a_turned"], 1)
                                if h % 4 == 3:
                                    m = 2 * b + h // 4
                                    act.wait_ge(S["a_latent"], m + 1)
                                    if m:
                                        act.wait_ge(S["a_value"], m)
                                    nc.scalar.activation(lat[:, :, :].rearrange("p h t -> p (h t)"), bank(6), ACT.Copy)\
                                        .then_inc(S["a_latcopy"], 1)

                            for h in range(NH):
                                n = NH * b + h
                                act.wait_ge(S["a_added"], n + 1)
                                if n >= 2:
                                    act.wait_ge(S["a_transposed"], n - 1)
                                nc.scalar.activation(pr[:, h % 2, 0:width], sm[:, h % 2, 0:width], ACT.Exp,
                                                     bias=nmx[:, h % 2:h % 2 + 1], accum_out=rs[:, h % 2:h % 2 + 1])\
                                    .then_inc(S["a_exp"], 1)
                                if h:
                                    turn(h - 1)
                                normalise(h)
                            turn(NH - 1)
                            act.wait_ge(S["a_value"], 2 * b + 2)
                            nc.scalar.activation(mT[:, 0:4, b * P:b * P + P], bank(7).rearrange("p (k t) -> p k t", k=4),
                                                 ACT.Copy).then_inc(S["a_stored"], 1)

                    @block.vector
                    def _(dve):
                        link = Link(dve, dve_step)

                        def select(b):
                            full = slice(0, (b + 1) * P)
                            diag = slice(b * P, b * P + P)
                            out = bias[:, b % 2]
                            for h in range(4):
                                dve.wait_ge(S["a_relu"], 4 * b + h + 1)
                                if h == 0:
                                    ins = nc.vector.tensor_scalar(score[:, full], rl[:, 0, full], wis[:, b, 0:1], None,
                                                                  ALU.mult)
                                else:
                                    ins = nc.vector.scalar_tensor_tensor(score[:, full], rl[:, h % 2, full],
                                                                         wis[:, b, h:h + 1], score[:, full], ALU.mult,
                                                                         ALU.add)
                                ins.then_inc(S["a_summed"], 1)
                                dve.wait_ge(S["a_summed"], 4 * b + h + 1)
                            yield
                            if (b + 1) * P <= TOPK:
                                if b:
                                    link(nc.vector.memset(out[:, 0:b * P], 0.0))
                                link(nc.vector.tensor_copy(out[:, diag], neg[:, :]))
                                return
                            link(nc.vector.tensor_tensor(score[:, diag], score[:, diag], neg[:, :], ALU.add))
                            src = score
                            for r in range(TOPK // 8):
                                link(nc.vector.max(best[:, :], src[:, full]))
                                if r + 1 < TOPK // 8:
                                    link(nc.vector.match_replace(work[:, full], best[:, :], src[:, full], -3.0e38))
                                src = work
                                yield
                            thr = best[:, 7:8]
                            link(nc.vector.tensor_scalar(out[:, full], score[:, full], thr, 0.0, ALU.is_gt, ALU.add,
                                                         accum_out=count[:, 0:1]))
                            link(nc.vector.tensor_scalar(count[:, 1:2], count[:, 0:1], -1.0, float(TOPK), ALU.mult,
                                                         ALU.add))
                            link(nc.vector.tensor_scalar(eq[:, full], score[:, full], thr, None, ALU.is_equal))
                            link(nc.vector.tensor_tensor_scan(work[:, full], one_row[:, full], eq[:, full], 0.0,
                                                              ALU.mult, ALU.add))
                            yield
                            link(nc.vector.scalar_tensor_tensor(eq[:, full], work[:, full], count[:, 1:2],
                                                                eq[:, full], ALU.is_le, ALU.mult))
                            link(nc.vector.tensor_tensor(out[:, full], out[:, full], eq[:, full], ALU.add))
                            link(nc.vector.tensor_scalar(out[:, full], out[:, full], -NEG, NEG, ALU.mult, ALU.add))
                            link(nc.vector.tensor_tensor(out[:, diag], out[:, diag], neg[:, :], ALU.add))

                        for _ in select(0):
                            pass
                        for b in range(NQ):
                            width = (b + 1) * P
                            full = slice(0, width)
                            ahead_steps = select(b + 1) if b + 1 < NQ else iter(())

                            def fill(n):
                                for _ in range(n):
                                    next(ahead_steps, None)

                            def add(h):
                                s = h % 2
                                n = NH * b + h
                                use = place["head", b, h]
                                dve.wait_ge(S["a_scored"], use + 1)
                                if n >= 2:
                                    dve.wait_ge(S["a_exp"], n - 1)
                                link(nc.vector.tensor_tensor_reduce(
                                    out=sm[:, s, full], in0=PS[:, (use % 2) * 1024:(use % 2) * 1024 + width],
                                    in1=bias[:, b % 2, full], scale=1.0, scalar=-3.0e38, op0=ALU.add, op1=ALU.max,
                                    accum_out=mx[:, s:s + 1]))
                                nc.vector.tensor_scalar(nmx[:, s:s + 1], mx[:, s:s + 1], -1.0, None, ALU.mult)\
                                    .then_inc(S["a_added"], 1)

                            fill(1)
                            add(0)
                            for h in range(NH):
                                if h + 1 < NH:
                                    add(h + 1)
                                fill(2)
                                s = h % 2
                                dve.wait_ge(S["a_exp"], NH * b + h + 1)
                                nc.vector.reciprocal(ri[:, s:s + 1], rs[:, s:s + 1]).then_inc(S["a_inverse"], 1)
                                fill(3)
                            for _ in ahead_steps:
                                pass
                        link.end()

        def mod_cols(w):
            scale, shift, _ = mods[w]
            return (lambda k, c: scale[:, k, c // 2:c // 2 + 1]), (lambda k, c: shift[:, k, c // 2:c // 2 + 1])

        with ExitStack() as first:
            hT = sb(first, "hT", [P, KD, T])
            norm_stage("norm_e", xT, hT, ALL_CHUNKS, KD, 1e-6, False, *mod_cols("e"))
            project_stage("in_e", A["in_e"], 0, 24, hT, ALL_CHUNKS, proj_e)
            even_branch_stage(hT)
            combine_stage("out_e", A["out_e"], hT, ALL_CHUNKS, gated_update(mods["e"][2], True))
            norm_stage("norm_o", xT, hT, ALL_CHUNKS, KD, 1e-6, False, *mod_cols("o"))
            project_stage("in_o", A["in_o"], 0, 12, hT, ALL_CHUNKS, proj_o)
            project_stage("in_o2", A["in_o"], 12, 20, hT, MAIN_CHUNKS, proj_o)
        mix_stage()
        scan_stage()
        with ExitStack() as odd:
            yT = sb(odd, "yT", [P, KD, SEQ])
            rwkv_out_stage(yT)
            with ExitStack() as conf:
                cv = sb(conf, "cv", [P, JB, SEQ])
                conformer_conv_stage(cv)
                norm_stage("conf_ln", cv, cv, MAIN_CHUNKS, JB, 1e-5, True, lambda k, c: v("conf_ln_g", k),
                           lambda k, c: v("conf_ln_b", k))
                conformer_gate_stage(cv, yT)
            combine_stage("out_o", A["out_o"], yT, MAIN_CHUNKS, gated_update(mods["o"][2], False))
        norm_stage("final_norm", xT, xT, MAIN_CHUNKS, KD, 1e-6, False, lambda k, c: v("final_g", k), zero)
        ffn_stage("ffn1", A["ffn1_up"], A["ffn1_down"])
        norm_stage("ln1", xT, xT, MAIN_CHUNKS, KD, 1e-5, True, lambda k, c: v("ln1_g_2", k),
                   lambda k, c: v("ln1_b_2", k))
        project_stage("in_2", A["w_in"], 0, IN_TILES_2, xT, MAIN_CHUNKS, proj_2)
        with ExitStack() as mixer:
            mT = sb(mixer, "mT", [P, KD, SEQ])
            gmlp_stage(mT)
            with ExitStack():
                attention_stage(mT)
            combine_stage("out_2", A["w_out"], mT, MAIN_CHUNKS, deepnorm_update)
        norm_stage("ln2", xT, xT, MAIN_CHUNKS, KD, 1e-5, True, lambda k, c: v("ln2_g_2", k),
                   lambda k, c: v("ln2_b_2", k))
        ffn_stage("ffn2", A["ffn2_up"], A["ffn2_down"])
        norm_stage("ln3", xT, xT, MAIN_CHUNKS, KD, 1e-5, True, lambda k, c: v("ln3_g_2", k),
                   lambda k, c: v("ln3_b_2", k), out_dram=A["out"])


def constants():
    i = np.arange(P)
    same_head = (i[:, None] // 64 == i[None, :] // 64)
    before = (i[:, None] < i[None, :])
    eye = np.eye(P)
    ev = np.stack([np.stack([m, m + eye, m, m + eye]) for m in (before * 1.0, before.T * 1.0)])
    inv = []
    for lv in range(N_LEVELS):
        b = i >> lv
        lower = (b[:, None] % 2 == 1) & (b[None, :] == b[:, None] - 1)
        inv.append(np.stack([lower + eye, lower.T + eye]))
    inv.append(inv[0][::-1])
    reset = np.ones((P, JB, P))
    reset[:, :, 0] = 0
    counts = []
    for w in POOL_WINDOWS:
        for length in (LINE, CTX):
            t = np.arange(length)
            lo, hi = np.clip(t - w // 2, 0, length), np.clip(t - w // 2 + w, 0, length)
            counts.append(1.0 / (hi - lo))
    counts = np.concatenate(counts).reshape(1, JB, LINE + CTX)
    f = lambda a: np.ascontiguousarray(np.asarray(a, np.float32))
    return {"ident": f(eye), "ones": f(np.ones((P, P))), "head_ones": f(same_head), "tri": f(before + eye),
            "neg": f(np.where(before, NEG, 0.0)), "reset": f(reset), "evmask": f(ev.transpose(2, 0, 1, 3)),
            "invmask": f(np.stack(inv).transpose(2, 0, 1, 3)),
            "inv_count": f(np.broadcast_to(counts, (P, JB, LINE + CTX)))}


def kernel(**inputs):
    import concourse.bacc as bacc
    from concourse.bass_utils import run_bass_kernel_spmd

    g = {k: np.asarray(a) for k, a in inputs.items()}

    def tiles(w, order=None):
        k, n = w.shape
        t = w.reshape(k // P, P, n // P, P).transpose(2, 1, 0, 3)
        return t if order is None else t[order]

    def columns(a):
        return a.reshape(-1, P).T

    def features_first(a):
        return a.T.reshape(-1, P, a.shape[0]).transpose(1, 0, 2)

    a = {"vecs": np.concatenate([columns(g[n]) for n, _ in VECS], axis=1)}
    a["x"] = features_first(g["x"][0])
    a["ctx"] = features_first(g["ctx"][0])
    a["ada"] = np.concatenate([tiles(g["ada_w_e"][0]), tiles(g["ada_w_o"][0])])
    a["in_e"] = tiles(g["in_e"][0], [q * JB + i for i in range(JB) for q in range(6)])
    a["out_e"] = tiles(g["out_e"][0])
    a["pool_w"] = g["pool_w"][0].transpose(1, 0, 2)
    a["in_o"] = tiles(g["in_o"][0], [q * JB + i for q in (0, 2, 3, 1, 4, 5, 6, 7) for i in range(JB)])
    a["out_o"] = tiles(g["out_o"][0])
    by_k = lambda w: w.reshape(-1, P, w.shape[-1]).transpose(1, 0, 2)
    for n, (first, second) in enumerate((("w1", "w2"), ("a1", "a2"))):
        a[f"low1_{n}"] = by_k(np.concatenate([g[first][0, 0], g[first][0, 1]], axis=1))
        a[f"low2_{n}"] = np.concatenate([g[second][0, 0], g[second][0, 1]], axis=0)
    a["low1_2"], a["low2_2"] = by_k(g["g1"][0]), g["g2"][0]
    for n in (1, 2):
        up = [tiles(g[f"ffn{n}_w{m}_2"][0]) for m in (1, 3)]
        a[f"ffn{n}_up"] = np.stack(up, axis=1).reshape(2 * KF, P, KD, P)
        a[f"ffn{n}_down"] = tiles(g[f"ffn{n}_w2_2"][0])
    w_in = g["w_in_2"][0]
    pad = np.zeros((D, IN_TILES_2 * P - w_in.shape[1]), w_in.dtype)
    a["w_in"] = tiles(np.concatenate([w_in[:, :964], pad, w_in[:, 964:]], axis=1))
    a["w_out"] = tiles(g["w_out_2"][0])
    a["w_uk"] = g["w_uk_2"][0].transpose(0, 2, 1).reshape(4, P, P).transpose(1, 0, 2)
    a["w_uv"] = g["w_uv_2"][0].transpose(1, 0, 2)
    a["gmlp_ws"] = g["gmlp_ws_2"][0].transpose(2, 0, 1)
    a["gmlp_bs"] = g["gmlp_bs_2"][0][None]
    a = {n: np.ascontiguousarray(x) for n, x in a.items()}
    a.update(constants())

    nc = bacc.Bacc("TRN2", target_bir_lowering=False, num_devices=1)
    fp32 = mybir.dt.float32
    A = {n: nc.dram_tensor("in_" + n, x.shape, fp32, kind="ExternalInput").ap() for n, x in a.items()}
    A["low1"] = [A[f"low1_{n}"] for n in range(3)]
    A["low2"] = [A[f"low2_{n}"] for n in range(3)]
    A["out"] = nc.dram_tensor("out", (P, KD, SEQ), fp32, kind="ExternalOutput").ap()
    program(nc, A)
    r = run_bass_kernel_spmd(nc, [{"in_" + n: x for n, x in a.items()}], core_ids=[0])
    y = r.results[0]["out"]
    return np.ascontiguousarray(y.transpose(1, 0, 2).reshape(D, SEQ).T)[None]
```
